# Optimizing a Trainium2 kernel written in Bass

```python
import jax, jax.numpy as jnp
from jax import lax
import numpy as np

D_MODEL = 1024
BATCH = 1
SEQ = 1024
DEPTH = 1
DEC_BATCH = 8
DEC_SEQ = 4
PAST_LEN = 2048
PAGE_SIZE = 128

N_HEADS = 8
N_KV_HEADS = 2
HEAD_DIM = 64
Q_GROUP = N_HEADS // N_KV_HEADS
WINDOW = 128
ATTN_WIDTH = N_HEADS * HEAD_DIM
KV_WIDTH = N_KV_HEADS * HEAD_DIM
SGU_GROUPS = 4
SGU_WIDTH = D_MODEL // 2
SGU_GROUP_DIM = SGU_WIDTH // SGU_GROUPS
CHUNK = 128
N_GROUPS = 4
EXPERTS_PER_GROUP = 4
N_EXPERTS = N_GROUPS * EXPERTS_PER_GROUP
TOP_K = 2
D_EXPERT = 256
D_IN = ATTN_WIDTH + 2 * KV_WIDTH + 2 * SGU_WIDTH + 2 * D_MODEL
EPS = 1e-6
NEG_INF = -1e30

kernel_name = "hybrid_swa_sink_sgu_hmoe_step"

def rms_norm(x, g):
    xf = x.astype(jnp.float32)
    y = xf * lax.rsqrt(jnp.mean(xf * xf, axis=-1, keepdims=True) + EPS)
    return (y * g.astype(jnp.float32)).astype(x.dtype)

def layer_norm(x, g, b):
    xf = x.astype(jnp.float32)
    mu = jnp.mean(xf, axis=-1, keepdims=True)
    xc = xf - mu
    y = xc * lax.rsqrt(jnp.mean(xc * xc, axis=-1, keepdims=True) + EPS)
    return (y * g.astype(jnp.float32) + b.astype(jnp.float32)).astype(x.dtype)

def input_branches(x, norm1_g, w_in, q_norm_g, k_norm_g, ln_v_g, ln_v_b):
    b, s = x.shape[0], x.shape[1]
    h = rms_norm(x, norm1_g)
    z = jnp.einsum("bsd,de->bse", h, w_in)
    widths = [ATTN_WIDTH, KV_WIDTH, KV_WIDTH, SGU_WIDTH, SGU_WIDTH, D_MODEL]
    cuts = [int(c) for c in np.cumsum(widths)]
    q, k, v, u, vs, ga, gb = jnp.split(z, cuts, axis=-1)
    q = rms_norm(q.reshape(b, s, N_KV_HEADS, Q_GROUP, HEAD_DIM), q_norm_g)
    k = rms_norm(k.reshape(b, s, N_KV_HEADS, HEAD_DIM), k_norm_g)
    v = v.reshape(b, s, N_KV_HEADS, HEAD_DIM)
    u = jax.nn.gelu(u)
    vs = layer_norm(jax.nn.gelu(vs), ln_v_g, ln_v_b).reshape(b, s, SGU_GROUPS, SGU_GROUP_DIM)
    return q, k, v, u, vs, ga, gb

def window_mask(n_q, n_s):
    t = jnp.arange(n_q)[:, None]
    s = jnp.arange(n_s)[None, :]
    return (s > t) & (s <= t + WINDOW)

def sink_probs(scores, mask, sinks):
    sc = jnp.where(mask, scores, NEG_INF)
    sink = sinks.astype(jnp.float32).reshape(N_KV_HEADS, Q_GROUP, 1, 1)
    m = jnp.maximum(jnp.max(sc, axis=-1, keepdims=True), sink)
    p = jnp.exp(sc - m)
    denom = jnp.sum(p, axis=-1, keepdims=True) + jnp.exp(sink - m)
    return p / denom

def attn_prompt(q, k, v, sinks):
    b, s = q.shape[0], q.shape[1]
    nb = s // WINDOW
    qb = q.reshape(b, nb, WINDOW, N_KV_HEADS, Q_GROUP, HEAD_DIM)
    kb = k.reshape(b, nb, WINDOW, N_KV_HEADS, HEAD_DIM)
    vb = v.reshape(b, nb, WINDOW, N_KV_HEADS, HEAD_DIM)
    pad = ((0, 0), (1, 0), (0, 0), (0, 0), (0, 0))
    kk = jnp.concatenate([jnp.pad(kb, pad)[:, :-1], kb], axis=2)
    vv = jnp.concatenate([jnp.pad(vb, pad)[:, :-1], vb], axis=2)
    scores = jnp.einsum("bnqkgd,bnskd->bnkgqs", qb, kk,
                        preferred_element_type=jnp.float32) * (HEAD_DIM ** -0.5)
    blk_ok = (jnp.arange(nb)[:, None] > 0) | (jnp.arange(2 * WINDOW)[None, :] >= WINDOW)
    mask = window_mask(WINDOW, 2 * WINDOW)[None, None, :, :] & blk_ok.reshape(nb, 1, 1, 2 * WINDOW)[None]
    mask = mask.reshape(1, nb, 1, 1, WINDOW, 2 * WINDOW)
    p = sink_probs(scores, mask, sinks).astype(vv.dtype)
    o = jnp.einsum("bnkgqs,bnskd->bnqkgd", p, vv).reshape(b, s, ATTN_WIDTH)
    return o, k[:, s - WINDOW:], v[:, s - WINDOW:]

def attn_sample(q, k, v, k_buf, v_buf, sinks):
    b, t = q.shape[0], q.shape[1]
    kk = jnp.concatenate([k_buf, k], axis=1)
    vv = jnp.concatenate([v_buf, v], axis=1)
    scores = jnp.einsum("btkgd,bskd->bkgts", q, kk,
                        preferred_element_type=jnp.float32) * (HEAD_DIM ** -0.5)
    mask = window_mask(t, WINDOW + t)
    p = sink_probs(scores, mask, sinks).astype(vv.dtype)
    o = jnp.einsum("bkgts,bskd->btkgd", p, vv).reshape(b, t, ATTN_WIDTH)
    return o, kk[:, t:], vv[:, t:]

def causal_spatial(w_spatial):
    return w_spatial * jnp.tril(jnp.ones((CHUNK, CHUNK), w_spatial.dtype))[None]

def sgu_prompt(u, vs, w_spatial, b_spatial):
    b, s = u.shape[0], u.shape[1]
    nc = s // CHUNK
    vc = vs.reshape(b, nc, CHUNK, SGU_GROUPS, SGU_GROUP_DIM)
    mixed = jnp.einsum("hij,bnjhc->bnihc", causal_spatial(w_spatial), vc) + b_spatial.T[:, :, None]
    return u * mixed.reshape(b, s, SGU_WIDTH)

def sgu_sample(u, vs, w_spatial, b_spatial):
    b, t = u.shape[0], u.shape[1]
    w = causal_spatial(w_spatial)[:, :t, :t]
    mixed = jnp.einsum("hij,bjhc->bihc", w, vs) + b_spatial[:, :t].T[:, :, None]
    return u * mixed.reshape(b, t, SGU_WIDTH), vs

def merge_branches(oa, ob, ga, gb, w_branch_a, w_branch_b, w_out):
    ya = jnp.einsum("bse,ed->bsd", oa, w_branch_a)
    yb = jnp.einsum("bse,ed->bsd", ob, w_branch_b)
    h = jax.nn.sigmoid(ga) * ya + jax.nn.sigmoid(gb) * yb
    return jnp.einsum("bsd,de->bse", h, w_out)

def hier_moe(h, w_rg, b_rg, w_re, b_re, w_gate, w_up, w_down):
    n = h.shape[0]
    gl = (h @ w_rg + b_rg).astype(jnp.float32)
    gidx = jnp.argmax(gl, axis=-1)
    gw = jnp.take_along_axis(jax.nn.softmax(gl, axis=-1), gidx[:, None], axis=1)
    el = (h @ w_re + b_re).astype(jnp.float32).reshape(n, N_GROUPS, EXPERTS_PER_GROUP)
    el_sel = jnp.take_along_axis(el, gidx[:, None, None], axis=1)[:, 0]
    top_l, top_i = lax.top_k(el_sel, TOP_K)
    top_w = jax.nn.softmax(top_l, axis=-1) * gw
    eidx = gidx[:, None] * EXPERTS_PER_GROUP + top_i
    combine = jnp.sum(jax.nn.one_hot(eidx, N_EXPERTS, dtype=jnp.float32) * top_w[..., None], axis=1)
    a = jnp.einsum("nd,edf->nef", h, w_gate)
    bu = jnp.einsum("nd,edf->nef", h, w_up)
    hid = jax.nn.silu(a) * bu * combine[..., None].astype(h.dtype)
    return jnp.einsum("nef,efd->nd", hid, w_down)

def moe_ffn(x, norm2_g, w_rg, b_rg, w_re, b_re, w_gate, w_up, w_down):
    h = rms_norm(x, norm2_g).reshape(-1, D_MODEL)
    return hier_moe(h, w_rg, b_rg, w_re, b_re, w_gate, w_up, w_down).reshape(x.shape)

def setup_inputs(seed: int = 0) -> dict:
    key = jax.random.key(seed)
    ks = jax.random.split(key, 26)

    def nrm(k, shape, scale):
        return jax.random.normal(k, shape, jnp.float32) * scale

    cache_shape = (DEPTH, DEC_BATCH, WINDOW, N_KV_HEADS, HEAD_DIM)
    return {
        "x_prompt": nrm(ks[0], (BATCH, SEQ, D_MODEL), 1.0),
        "x_sample": nrm(ks[1], (DEC_BATCH, DEC_SEQ, D_MODEL), 1.0),
        "cache_k_win": nrm(ks[2], cache_shape, 1.0),
        "cache_v_win": nrm(ks[3], cache_shape, 1.0),
        "norm1_g": 1.0 + nrm(ks[4], (DEPTH, D_MODEL), 0.02),
        "w_in": nrm(ks[5], (DEPTH, D_MODEL, D_IN), D_MODEL ** -0.5),
        "q_norm_g": 1.0 + nrm(ks[6], (DEPTH, HEAD_DIM), 0.02),
        "k_norm_g": 1.0 + nrm(ks[7], (DEPTH, HEAD_DIM), 0.02),
        "attn_sinks": nrm(ks[8], (DEPTH, N_HEADS), 0.5),
        "ln_v_g": 1.0 + nrm(ks[9], (DEPTH, SGU_WIDTH), 0.02),
        "ln_v_b": nrm(ks[10], (DEPTH, SGU_WIDTH), 0.02),
        "w_spatial": nrm(ks[11], (DEPTH, SGU_GROUPS, CHUNK, CHUNK), 0.5 * CHUNK ** -0.5),
        "b_spatial": 1.0 + nrm(ks[12], (DEPTH, SGU_GROUPS, CHUNK), 0.1),
        "w_branch_a": nrm(ks[13], (DEPTH, ATTN_WIDTH, D_MODEL), ATTN_WIDTH ** -0.5),
        "w_branch_b": nrm(ks[14], (DEPTH, SGU_WIDTH, D_MODEL), SGU_WIDTH ** -0.5),
        "w_out": nrm(ks[15], (DEPTH, D_MODEL, D_MODEL), D_MODEL ** -0.5),
        "norm2_g": 1.0 + nrm(ks[16], (DEPTH, D_MODEL), 0.02),
        "w_router_group": nrm(ks[17], (DEPTH, D_MODEL, N_GROUPS), D_MODEL ** -0.5),
        "b_router_group": nrm(ks[18], (DEPTH, N_GROUPS), 0.01),
        "w_router_expert": nrm(ks[19], (DEPTH, D_MODEL, N_EXPERTS), D_MODEL ** -0.5),
        "b_router_expert": nrm(ks[20], (DEPTH, N_EXPERTS), 0.01),
        "w_exp_gate": nrm(ks[21], (DEPTH, N_EXPERTS, D_MODEL, D_EXPERT), D_MODEL ** -0.5),
        "w_exp_up": nrm(ks[22], (DEPTH, N_EXPERTS, D_MODEL, D_EXPERT), D_MODEL ** -0.5),
        "w_exp_down": nrm(ks[23], (DEPTH, N_EXPERTS, D_EXPERT, D_MODEL), D_EXPERT ** -0.5),
    }

def reference(x_prompt, x_sample, cache_k_win, cache_v_win, norm1_g, w_in, q_norm_g, k_norm_g,
              attn_sinks, ln_v_g, ln_v_b, w_spatial, b_spatial, w_branch_a, w_branch_b, w_out,
              norm2_g, w_router_group, b_router_group, w_router_expert, b_router_expert,
              w_exp_gate, w_exp_up, w_exp_down):
    yp, ys = x_prompt, x_sample
    kp_list, vp_list, ks_list, vs_list, sgu_list = [], [], [], [], []
    for l in range(DEPTH):
        q, k, v, u, vsg, ga, gb = input_branches(yp, norm1_g[l], w_in[l], q_norm_g[l], k_norm_g[l],
                                                 ln_v_g[l], ln_v_b[l])
        oa, k_new, v_new = attn_prompt(q, k, v, attn_sinks[l])
        ob = sgu_prompt(u, vsg, w_spatial[l], b_spatial[l])
        yp = yp + merge_branches(oa, ob, ga, gb, w_branch_a[l], w_branch_b[l], w_out[l])
        yp = yp + moe_ffn(yp, norm2_g[l], w_router_group[l], b_router_group[l], w_router_expert[l],
                          b_router_expert[l], w_exp_gate[l], w_exp_up[l], w_exp_down[l])
        kp_list.append(k_new)
        vp_list.append(v_new)
        q, k, v, u, vsg, ga, gb = input_branches(ys, norm1_g[l], w_in[l], q_norm_g[l], k_norm_g[l],
                                                 ln_v_g[l], ln_v_b[l])
        oa, k_buf, v_buf = attn_sample(q, k, v, cache_k_win[l], cache_v_win[l], attn_sinks[l])
        ob, v_open = sgu_sample(u, vsg, w_spatial[l], b_spatial[l])
        ys = ys + merge_branches(oa, ob, ga, gb, w_branch_a[l], w_branch_b[l], w_out[l])
        ys = ys + moe_ffn(ys, norm2_g[l], w_router_group[l], b_router_group[l], w_router_expert[l],
                          b_router_expert[l], w_exp_gate[l], w_exp_up[l], w_exp_down[l])
        ks_list.append(k_buf)
        vs_list.append(v_buf)
        sgu_list.append(v_open)
    new_k_prompt = jnp.stack(kp_list)
    new_v_prompt = jnp.stack(vp_list)
    new_k_sample = jnp.stack(ks_list)
    new_v_sample = jnp.stack(vs_list)
    new_vsgu_sample = jnp.stack(sgu_list)
    return (yp, ys, new_k_prompt, new_v_prompt, new_k_sample, new_v_sample, new_vsgu_sample)


_drawn_inputs = setup_inputs


def setup_inputs(seed=0):
    import zlib

    import numpy as np

    out = dict(_drawn_inputs(seed))
    spreads = {}
    factors = {'q_norm_g': 7.52,
     'k_norm_g': 2.701,
     'attn_sinks': 64.0,
     'ln_v_g': 24.016,
     'ln_v_b': 22.647,
     'b_router_group': 3.91,
     'b_router_expert': 12.592,
     'norm2_g': 3.42}
    for name, (base, spread) in spreads.items():
        noise = np.random.default_rng([zlib.crc32(name.encode()), seed]).standard_normal(out[name].shape)
        drawn = base * np.exp(spread * noise) if base else spread * noise
        out[name] = __import__('jax').numpy.asarray(drawn.astype(out[name].dtype))
    for name, factor in factors.items():
        out[name] = (out[name] * factor).astype(out[name].dtype)
    return out
```

```python
from contextlib import ExitStack

import concourse.bass as bass
from concourse import mybir

F32 = mybir.dt.float32
F32R = mybir.dt.float32r
I32 = mybir.dt.int32
ALU = mybir.AluOpType
ACT = mybir.ActivationFunctionType
AX_X = mybir.AxisListType.X

P = 128
D = 1024
KD = D // P
SEQ = 1024
DEC_B, DEC_T = 8, 4
NS = DEC_B * DEC_T
NTOK = SEQ + NS
PT = SEQ // P
NT = PT + 1
HEADS, KV, G, HD = 8, 2, 4, 64
AW = HEADS * HD
KVW = KV * HD
QKV = AW + 2 * KVW
WIN = 128
SG = 4
SW = 512
KE = AW // P
OFF_VS = QKV + SW
OFF_GA = QKV + 2 * SW
OFF_GB = OFF_GA + D
TC = NTOK // 3
NG, EPG = 4, 4
NE = NG * EPG
NR = NG + NE
DE = 256
EPS = 1e-6
NEG = -1e30
SLOT = 128
NSTEP = (2 * NTOK + NE * (SLOT - 1)) // SLOT
NSTEP += NSTEP % 2
FAR = 1 << 20
DMA = 16


def rows(t):
    return P if t < PT else NS


def toks(t):
    return slice(t * P, t * P + rows(t))


def product(eng, out, lhs, rhs, nk, first=True, last=True):
    for k in range(nk):
        lh, ll = lhs(k)
        rh, rl = rhs(k)
        eng.matmul(out, lh, rh, start=first and k == 0, stop=False)
        eng.matmul(out, lh, rl, start=False, stop=False)
        mm = eng.matmul(out, ll, rh, start=False, stop=last and k == nk - 1)
    return mm


def bank(psum, n):
    return psum[:, n, :]


class Step:

    def __init__(self, eng, sem):
        self.eng, self.sem, self.n = eng, sem, 0

    def did(self, ins):
        self.n += 1
        ins.then_inc(self.sem, 1)
        self.eng.wait_ge(self.sem, self.n)


class Flow:

    def __init__(self, sem, start=2):
        self.sem, self.start = sem, start

    def begin(self, eng):
        eng.sem_inc(self.sem, self.start)

    def after(self, n):
        return n + (self.start + 1)

    def wait(self, eng, n):
        eng.wait_ge(self.sem, self.after(n))

    def wait_alone(self, eng, n, passed):
        eng.wait_ge(self.sem, self.after(n))
        eng.sem_inc(passed, 1)


def attention_phase(nc, io, keep, psum):
    ident, hT, oaT = keep["ident"], (keep["hT_hi"], keep["hT_lo"]), (keep["oaT_hi"], keep["oaT_lo"])
    NP = QKV // P
    w_src = io["w_in"][0].rearrange("(k p) c -> p k c", p=P)

    used = []
    with ExitStack() as ctx:
        def sb(name, shape, dt=F32):
            return ctx.enter_context(nc.sbuf_tensor(name, shape, dt))

        def sem(name):
            used.append(ctx.enter_context(nc.semaphore(name)))
            return used[-1]

        w_raw = sb("qkv_w_raw", [P, 2, KD, P])
        w_hi = sb("qkv_w_hi", [P, KD, QKV], F32R)
        w_lo = sb("qkv_w_lo", [P, KD, QKV], F32R)
        x_in = sb("x_in", [P, 2, D])
        x_norm = sb("x_norm", [P, D])
        h_raw = sb("h_raw", [P, 2, 4, P])
        z = sb("z_qkv", [P, AW + KVW])
        z_sq = w_raw[:, 1].rearrange("p k c -> p (k c)")[:, 0:AW + KVW]
        v_ring = sb("v_ring", [P, 3, KVW])
        q_norm = sb("q_norm", [P, G, KV, HD])
        k_norm = sb("k_norm", [P, KV, HD])
        qT = sb("qT", [P, G, P])
        kT = sb("kT", [P, NT, P])
        sp_sb = sb("sp_sb", [P, 2, G, 2 * WIN])
        s_sb, p_sb = sp_sb[:, 0], sp_sb[:, 1]
        pT = sb("pT", [P, 2, G, P])
        o_sb = sb("o_sb", [P, KV, G, HD])
        mask = sb("mask", [P, 2 * WIN])
        g1 = sb("g1", [P, KD])
        qk_gain = sb("qk_gain", [P, 2])
        k_gain = sb("k_gain", [P, HD])
        sinks = sb("sinks", [P, HEADS])
        minus_half = sb("minus_half", [P, 1])
        xss = sb("xss", [P, NT])
        xrs = sb("xrs", [P, NT])
        qks = sb("qks", [P, HEADS + KV])
        qkr = sb("qkr", [P, HEADS + KV])
        top = sb("top", [P, G])
        ntop = sb("ntop", [P, 2, G])
        sink_d = sb("sink_d", [P, 2, G])
        den = sb("den", [P, 2, G])
        sink_e = sb("sink_e", [P, 2, G])
        rden = sb("rden", [P, G])
        k_out = sb("k_out", [P, KV, HD])
        s_mask = sb("s_mask", [P, DEC_B * WIN + NS])
        s_sinks = sb("s_sinks", [P, KV])
        s_scores = sp_sb[:, :, :, :].rearrange("p a g s -> p (a g s)")[:, 0:DEC_B * WIN + NS]
        v_cache = w_raw[:, 0]
        k_cache = x_in[:, 0, :].rearrange("p (b c) -> p b c", b=DEC_B)
        kT_cache = x_norm
        pT_s = x_in[:, 1, :].rearrange("p (b c) -> p b c", b=DEC_B)
        pT_n = pT[:, 0, 0, :]

        const_in = sem("const_in")
        w_in = [sem("w_in_even"), sem("w_in_odd")]
        x_came = [sem("x_came_even"), sem("x_came_odd")]
        act_step, dve_step, pool_step = sem("act_step"), sem("dve_step"), sem("pool_step")
        masks_made = sem("masks_made")
        ident_made = sem("ident_made")
        gains_made = sem("gains_made")
        w_hi_made, w_lo_made = sem("w_hi_made"), sem("w_lo_made")
        x_squared, x_meaned, x_rstd, x_normed = sem("x_squared"), sem("x_meaned"), sem("x_rstd"), sem("x_normed")
        xT_made = sem("xT_made")
        h_scaled, h_hi_made, h_lo_made = sem("h_scaled"), sem("h_hi_made"), sem("h_lo_made")
        q_made, kv_made = sem("q_made"), sem("kv_made")
        z_copied, z_squared, z_summed, z_rstd, qk_normed = (sem("z_copied"), sem("z_squared"), sem("z_summed"),
                                                             sem("z_rstd"), sem("qk_normed"))
        qkT_made, qkT_copied = sem("qkT_made"), sem("qkT_copied")
        s_made, s_ready, p_made = sem("s_made"), sem("s_ready"), sem("p_made")
        pT_made, pT_copied = sem("pT_made"), sem("pT_copied")
        o_made, o_copied = sem("o_made"), sem("o_copied")
        oT_made, oa_hi_made, oa_lo_made = sem("oT_made"), sem("oa_hi_made"), sem("oa_lo_made")
        k_out_made = sem("k_out_made")
        kv_stored = sem("kv_stored")
        k_out_stored = sem("k_out_stored")
        cache_in = sem("cache_in")
        cT_made, cT_copied = sem("cT_made"), sem("cT_copied")
        ss_made, ss_ready, sp_made = sem("ss_made"), sem("ss_ready"), sem("sp_made")
        spT_made, spT_copied, so_made, so_copied = sem("spT_made"), sem("spT_copied"), sem("so_made"), sem("so_copied")
        N_CONST = 7 + G * KV

        def scores_bank():
            return psum[:, 2:4, :].rearrange("p a (b c) -> p (a b) c", c=2 * WIN)

        def block_keys(t):
            return WIN if t == 0 else 0

        block_ctx = ctx.enter_context(ExitStack())
        block = block_ctx.enter_context(nc.Block())

        @block.sync
        def _(sp):
            def load_x(t):
                if t >= 2:
                    sp.wait_ge(x_normed, t - 1)
                sp.dma_start(x_in[0:rows(t), t % 2, :], io["x"][toks(t), :]).then_inc(x_came[t % 2], DMA)

            load_x(0)
            for c in range(NP):
                if c >= 2:
                    sp.wait_ge(w_hi_made, c - 1)
                    sp.wait_ge(w_lo_made, c - 1)
                sp.dma_start(w_raw[:, c % 2], w_src[:, :, c * P:(c + 1) * P]).then_inc(w_in[c % 2], DMA)
                if c == 1:
                    load_x(1)
            sp.wait_ge(w_hi_made, NP)
            sp.wait_ge(w_lo_made, NP)
            sp.dma_start(v_cache, io["cache_v"][0].rearrange("b s k d -> s b (k d)")).then_inc(cache_in, DMA)
            for t in range(2, NT):
                load_x(t)
            for cached, new in (("cache_k", "new_k_s"), ("cache_v", "new_v_s")):
                sp.dma_start(io[new][0, :, 0:WIN - DEC_T], io[cached][0, :, DEC_T:WIN]).then_inc(kv_stored, DMA)
            sp.wait_ge(x_normed, NT)
            sp.wait_ge(cache_in, DMA)
            sp.dma_start(k_cache, io["cache_k"][0].rearrange("b s k d -> s b (k d)")).then_inc(cache_in, DMA)
            sp.wait_ge(k_out_made, 1)
            sp.dma_start(io["new_k_p"][0, 0].rearrange("s k d -> s (k d)"),
                         k_out[:, :, :].rearrange("p k d -> p (k d)")).then_inc(k_out_stored, DMA)
            sp.wait_ge(z_copied, 2 * PT)
            sp.dma_start(io["new_v_p"][0, 0].rearrange("s k d -> s (k d)"), v_ring[:, (PT - 1) % 3, :]).then_inc(kv_stored, DMA)
            sp.wait_ge(z_copied, 2 * NT)
            for b in range(DEC_B):
                sp.dma_start(io["new_v_s"][0, b, WIN - DEC_T:WIN].rearrange("s k d -> s (k d)"),
                             v_ring[b * DEC_T:(b + 1) * DEC_T, PT % 3, :]).then_inc(kv_stored, DMA)
            sp.wait_ge(k_out_made, 2)
            for b in range(DEC_B):
                sp.dma_start(io["new_k_s"][0, b, WIN - DEC_T:WIN].rearrange("s k d -> s (k d)"),
                             k_out[b * DEC_T:(b + 1) * DEC_T, :, :].rearrange("p k d -> p (k d)")).then_inc(kv_stored, DMA)
            sp.wait_ge(kv_stored, DMA * (3 + 2 * DEC_B))

        @block.gpsimd
        def _(pool):
            step = Step(pool, pool_step)
            step.did(pool.memset(ident[:, :], 0.0))
            pool.affine_select(out=ident[:, :], in_=ident[:, :], compare_op=ALU.not_equal, fill=1.0, base=0,
                               pattern=[[-1, P]], channel_multiplier=1).then_inc(ident_made, 1)
            step.did(pool.memset(minus_half[:, :], -0.5))
            step.did(pool.memset(mask[:, :], 0.0))
            step.did(pool.affine_select(out=mask[:, :], in_=mask[:, :], compare_op=ALU.is_ge, fill=NEG, base=-1,
                                        pattern=[[1, 2 * WIN]], channel_multiplier=-1))
            pool.affine_select(out=mask[:, :], in_=mask[:, :], compare_op=ALU.is_ge, fill=NEG, base=WIN,
                               pattern=[[-1, 2 * WIN]], channel_multiplier=1).then_inc(masks_made, 1)

            def rstd(t):
                pool.wait_ge(x_meaned, t + 1)
                pool.tensor_tensor(xrs[0:rows(t), t:t + 1], xss[0:rows(t), t:t + 1], minus_half[0:rows(t), :],
                                   ALU.pow).then_inc(x_rstd, 1)

            def h_low(t):
                for half in range(2):
                    pool.wait_ge(h_hi_made, 2 * t + half + 1)
                    ks = slice(4 * half, 4 * half + 4)
                    pool.tensor_tensor(hT[1][:, ks, toks(t)], h_raw[:, half, :, 0:rows(t)],
                                       hT[0][:, ks, toks(t)].bitcast(F32), ALU.subtract).then_inc(h_lo_made, 1)

            def z_root(t):
                pool.wait_ge(z_summed, t + 1)
                pool.tensor_tensor(qkr[0:rows(t), :], qks[0:rows(t), :],
                                   minus_half[0:rows(t), 0:1].broadcast_to([rows(t), HEADS + KV]),
                                   ALU.pow).then_inc(z_rstd, 1)

            rstd(0)
            h_low(0)
            rstd(1)
            step.did(pool.memset(s_mask[:, :], 0.0))
            for g in range(G):
                q = slice(32 * g, 32 * g + 32)
                old = s_mask[q, 0:DEC_B * WIN].rearrange("p (b s) -> p b s", b=DEC_B)
                new = s_mask[q, DEC_B * WIN:].rearrange("p (b j) -> p b j", b=DEC_B)
                for part, n in ((old, WIN), (new, DEC_T)):
                    step.did(pool.affine_select(out=part, in_=part, compare_op=ALU.is_ge, fill=NEG, base=0,
                                                pattern=[[-DEC_T, DEC_B], [0, n]], channel_multiplier=1))
                    step.did(pool.affine_select(out=part, in_=part, compare_op=ALU.is_ge, fill=NEG, base=DEC_T - 1,
                                                pattern=[[DEC_T, DEC_B], [0, n]], channel_multiplier=-1))
                step.did(pool.affine_select(out=old, in_=old, compare_op=ALU.is_ge, fill=NEG, base=-1,
                                            pattern=[[DEC_T, DEC_B], [1, WIN]], channel_multiplier=-1))
                last = pool.affine_select(out=new, in_=new, compare_op=ALU.is_ge, fill=NEG, base=0,
                                          pattern=[[-DEC_T, DEC_B], [-1, DEC_T]], channel_multiplier=1)
                if g < G - 1:
                    step.did(last)
                else:
                    last.then_inc(masks_made, 1)
            pool.wait_ge(masks_made, 2)
            z_root(0)
            for s in range(1, NT):
                h_low(s)
                if s + 1 < NT:
                    rstd(s + 1)
                z_root(s)

        @block.scalar
        def _(act):
            act.dma_start(g1[:, :], io["norm1_g"][0].rearrange("(k p) -> p k", p=P)).then_inc(const_in, DMA)
            for half in range(2):
                part = slice(HD * half, HD * half + HD)
                act.dma_start(qk_gain[part, 0:1], io["q_norm_g"].rearrange("a d -> d a")).then_inc(const_in, DMA)
                act.dma_start(qk_gain[part, 1:2], io["k_norm_g"].rearrange("a d -> d a")).then_inc(const_in, DMA)
            act.dma_start(k_gain[:, :], io["k_norm_g"][0].partition_broadcast(P)).then_inc(const_in, DMA)
            act.dma_start(sinks[:, :], io["attn_sinks"][0].partition_broadcast(P)).then_inc(const_in, DMA)
            for g in range(G):
                for kv in range(KV):
                    h = kv * G + g
                    act.dma_start(s_sinks[32 * g:32 * g + 32, kv:kv + 1],
                                  io["attn_sinks"][0, h:h + 1].partition_broadcast(32)).then_inc(const_in, DMA)

            def normalise(t):
                n = rows(t)
                act.wait_ge(x_came[t % 2], DMA * (t // 2 + 1))
                if t >= 1:
                    act.wait_ge(xT_made, t)
                act.activation(x_norm[0:n, :], x_in[0:n, t % 2, :], ACT.Square,
                               accum_out=xss[0:n, t:t + 1]).then_inc(x_squared, 1)
                act.wait_ge(x_rstd, t + 1)
                act.activation(x_norm[0:n, :], x_in[0:n, t % 2, :], ACT.Copy,
                               scale=xrs[0:n, t:t + 1]).then_inc(x_normed, 1)

            def h_high(t):
                for half in range(2):
                    act.wait_ge(h_scaled, 2 * t + half + 1)
                    act.activation(hT[0][:, 4 * half:4 * half + 4, toks(t)], h_raw[:, half, :, 0:rows(t)],
                                   ACT.Copy).then_inc(h_hi_made, 1)

            def copy_q(t):
                n = rows(t)
                act.wait_ge(q_made, t + 1)
                if t >= 1:
                    act.wait_ge(qk_normed, 2 * t)
                act.activation(z[0:n, 0:AW], bank(psum, 0)[0:n, 0:AW], ACT.Copy).then_inc(z_copied, 1)

            def copy_kv(t):
                n = rows(t)
                act.wait_ge(kv_made, t + 1)
                act.activation(z[0:n, AW:], bank(psum, 1)[0:n, 0:KVW], ACT.Copy).then_inc(act_step, 1)
                if t >= 3:
                    act.wait_ge(o_made, 2 * (t - 1))
                act.activation(v_ring[0:n, t % 3, :], bank(psum, 1)[0:n, KVW:2 * KVW], ACT.Copy).then_inc(z_copied, 1)
                act.wait_ge(act_step, t + 1)
                act.wait_ge(z_copied, 2 * t + 1)
                act.activation(z_sq[0:n, :], z[0:n, :], ACT.Square).then_inc(z_squared, 1)

            def probs(t, kv):
                u = 2 * t + kv
                k0 = block_keys(t)
                act.wait_ge(s_ready, u + 1)
                if u >= 1:
                    act.wait_ge(pT_made, u)
                for g in range(G):
                    act.activation(p_sb[:, g, k0:], s_sb[:, g, k0:], ACT.Exp, bias=ntop[:, kv, g:g + 1],
                                   accum_out=den[:, kv, g:g + 1])
                act.activation(sink_e[:, kv, :], sink_d[:, kv, :], ACT.Exp).then_inc(p_made, 1)

            def oa_high(t):
                act.wait_ge(oT_made, t + 1)
                act.activation(oaT[0][:, :, toks(t)], bank(psum, 4).rearrange("p (k c) -> p k c", k=KE)[:, :, 0:rows(t)],
                               ACT.Copy).then_inc(oa_hi_made, 1)

            normalise(0)
            for c in range(NP):
                act.wait_ge(w_in[c % 2], DMA * (c // 2 + 1))
                act.activation(w_hi[:, :, c * P:(c + 1) * P], w_raw[:, c % 2], ACT.Copy).then_inc(w_hi_made, 1)
                if c == 1:
                    h_high(0)
            normalise(1)
            copy_q(0)
            copy_kv(0)
            h_high(1)
            for s in range(1, NT):
                t = s - 1
                if s + 1 < NT:
                    normalise(s + 1)
                copy_q(s)
                probs(t, 0)
                copy_kv(s)
                probs(t, 1)
                if s + 1 < NT:
                    h_high(s + 1)
                oa_high(t)
            for kv in range(KV):
                act.wait_ge(ss_ready, kv + 1)
                act.activation(s_scores, s_scores, ACT.Exp, bias=ntop[:, kv, 0:1], accum_out=den[:, kv, 0:1])
                act.activation(sink_e[:, kv, 0:1], s_sinks[:, kv:kv + 1], ACT.Exp, bias=ntop[:, kv, 0:1]).then_inc(sp_made, 1)
            oa_high(PT)

        @block.tensor
        def _(pe):
            pe.wait_ge(ident_made, 1)

            def x_turn(t):
                n = rows(t)
                pe.wait_ge(x_normed, t + 1)
                if t >= 2:
                    pe.wait_ge(pT_copied, 2 * (t - 1))
                for half in range(2):
                    for k in range(4):
                        mm = pe.transpose(bank(psum, 6 + half)[:, k * P:k * P + n],
                                          x_norm[0:n, (4 * half + k) * P:(4 * half + k + 1) * P], ident[0:n, 0:n])
                mm.then_inc(xT_made, 1)

            def project(t, c0, c1, out, done):
                n = rows(t)
                pe.wait_ge(h_hi_made, 2 * t + 2)
                pe.wait_ge(h_lo_made, 2 * t + 2)
                pe.wait_ge(w_hi_made, -(-c1 // P))
                pe.wait_ge(w_lo_made, -(-c1 // P))
                if t >= 1:
                    pe.wait_ge(z_copied, 2 * t)
                product(pe, out[0:n, 0:c1 - c0], lambda k: (hT[0][:, k, toks(t)], hT[1][:, k, toks(t)]),
                        lambda k: (w_hi[:, k, c0:c1], w_lo[:, k, c0:c1]), KD).then_inc(done, 1)

            def qk_turn(t):
                n = rows(t)
                pe.wait_ge(qk_normed, 2 * t + 2)
                if t >= 1:
                    pe.wait_ge(oa_lo_made, t)
                    pe.wait_ge(o_copied, 2 * t)
                for g in range(G):
                    pe.transpose(bank(psum, 4)[:, g * P:g * P + n], q_norm[0:n, g, :, :].rearrange("p k d -> p (k d)"),
                                 ident[0:n, 0:n])
                pe.transpose(bank(psum, 5)[:, 0:n], k_norm[0:n, :, :].rearrange("p k d -> p (k d)"),
                             ident[0:n, 0:n]).then_inc(qkT_made, 1)

            def scores(t, kv):
                u = 2 * t + kv
                k0 = block_keys(t)
                head = slice(HD * kv, HD * kv + HD)
                pe.wait_ge(qkT_copied, 2 * t + 2)
                if u >= 1:
                    pe.wait_ge(s_ready, u)
                keys = kT[:, :, :].rearrange("p a b -> p (a b)")[head, (t - 1) * P + k0:(t + 1) * P]
                for g in range(G):
                    mm = pe.matmul(scores_bank()[:, g, k0:], qT[head, g, :], keys, start=True, stop=True)
                mm.then_inc(s_made, 1)

            def probs_turn(t, kv):
                u = 2 * t + kv
                pe.wait_ge(p_made, u + 1)
                if u >= 1:
                    pe.wait_ge(pT_copied, u)
                if kv == 0:
                    pe.wait_ge(h_scaled, 2 * t + 4)
                for half in range(block_keys(t) // WIN, 2):
                    for g in range(G):
                        mm = pe.transpose(bank(psum, 6 + half)[:, g * P:(g + 1) * P],
                                          p_sb[:, g, half * WIN:(half + 1) * WIN], ident[:, :])
                mm.then_inc(pT_made, 1)

            def values(t, kv):
                u = 2 * t + kv
                pe.wait_ge(pT_copied, u + 1)
                pe.wait_ge(z_copied, 2 * t + 2)
                if u >= 1:
                    pe.wait_ge(o_copied, u)
                first = block_keys(t) // WIN
                for g in range(G):
                    for half in range(first, 2):
                        mm = pe.matmul(bank(psum, 5)[:, g * HD:(g + 1) * HD], pT[:, half, g, :],
                                       v_ring[:, (t - 1 + half) % 3, kv * HD:(kv + 1) * HD],
                                       start=half == first, stop=half == 1)
                mm.then_inc(o_made, 1)

            def o_turn(t):
                n = rows(t)
                pe.wait_ge(o_copied, 2 * t + 2)
                flat = o_sb[:, :, :, :].rearrange("p k g d -> p (k g d)")
                for c in range(KE):
                    mm = pe.transpose(bank(psum, 4)[:, c * P:c * P + n], flat[0:n, c * P:(c + 1) * P], ident[0:n, 0:n])
                mm.then_inc(oT_made, 1)

            x_turn(0)
            project(0, 0, AW, bank(psum, 0), q_made)
            project(0, AW, QKV, bank(psum, 1), kv_made)
            pe.wait_ge(h_scaled, 2)
            x_turn(1)
            for s in range(1, NT):
                t = s - 1
                qk_turn(t)
                project(s, 0, AW, bank(psum, 0), q_made)
                scores(t, 0)
                project(s, AW, QKV, bank(psum, 1), kv_made)
                scores(t, 1)
                probs_turn(t, 0)
                values(t, 0)
                probs_turn(t, 1)
                values(t, 1)
                if s + 1 < NT:
                    x_turn(s + 1)
                o_turn(t)
            qk_turn(PT)
            pe.wait_ge(cache_in, 2 * DMA)
            pe.wait_ge(pT_copied, 2 * PT)
            for b in range(DEC_B):
                mm = pe.transpose(bank(psum, 6 + b // 4)[:, (b % 4) * P:(b % 4 + 1) * P], k_cache[:, b, :], ident[:, :])
            mm.then_inc(cT_made, 1)
            pe.wait_ge(qkT_copied, 2 * NT)
            pe.wait_ge(cT_copied, 2)
            for kv in range(KV):
                head = slice(HD * kv, HD * kv + HD)
                q_all = qT[head, 0, :]
                if kv == 1:
                    pe.wait_ge(ss_ready, 1)
                for c in range(2):
                    pe.matmul(bank(psum, 2 + c), q_all, kT_cache[head, c * 512:(c + 1) * 512], start=True, stop=True)
                pe.matmul(bank(psum, 1)[:, 0:NS], q_all, kT[head, PT, 0:NS], start=True, stop=True).then_inc(ss_made, 1)
                pe.wait_ge(sp_made, kv + 1)
                if kv == 1:
                    pe.wait_ge(spT_copied, 1)
                for b in range(DEC_B):
                    pe.transpose(bank(psum, 6 + b // 4)[:, (b % 4) * P:(b % 4 + 1) * P],
                                 s_scores[:, b * WIN:(b + 1) * WIN], ident[:, :])
                pe.transpose(bank(psum, 0)[0:NS, 0:P], s_scores[:, DEC_B * WIN:], ident[:, :]).then_inc(spT_made, 1)
                pe.wait_ge(spT_copied, kv + 1)
                if kv == 1:
                    pe.wait_ge(so_copied, 1)
                for b in range(DEC_B):
                    pe.matmul(bank(psum, 5)[:, 0:HD], pT_s[:, b, :], v_cache[:, b, kv * HD:(kv + 1) * HD],
                              start=b == 0, stop=False)
                pe.matmul(bank(psum, 5)[:, 0:HD], pT_n[0:NS, :], v_ring[0:NS, PT % 3, kv * HD:(kv + 1) * HD],
                          start=False, stop=True).then_inc(so_made, 1)
            pe.wait_ge(so_copied, 2)
            flat = o_sb[:, :, :, :].rearrange("p k g d -> p (k g d)")
            for c in range(KE):
                mm = pe.transpose(bank(psum, 4)[:, c * P:c * P + NS], flat[0:NS, c * P:(c + 1) * P], ident[0:NS, 0:NS])
            mm.then_inc(oT_made, 1)

        @block.vector
        def _(dve):
            step = Step(dve, dve_step)

            def mean_square(t):
                n = rows(t)
                dve.wait_ge(x_squared, t + 1)
                dve.tensor_scalar(xss[0:n, t:t + 1], xss[0:n, t:t + 1], 1.0 / D, EPS, ALU.mult,
                                  ALU.add).then_inc(x_meaned, 1)

            def h_scale(t):
                n = rows(t)
                dve.wait_ge(xT_made, t + 1)
                if t >= 1:
                    dve.wait_ge(h_lo_made, 2 * t)
                for half in range(2):
                    ks = slice(4 * half, 4 * half + 4)
                    dve.tensor_tensor(h_raw[:, half, :, 0:n],
                                      bank(psum, 6 + half).rearrange("p (k c) -> p k c", k=4)[:, :, 0:n],
                                      g1[:, ks].unsqueeze(2).broadcast_to([P, 4, n]), ALU.mult).then_inc(h_scaled, 1)

            def qk_scale(t):
                n = rows(t)
                zz = z[0:n, :].rearrange("p (h d) -> p h d", d=HD)
                dve.wait_ge(z_squared, t + 1)
                step.did(dve.tensor_reduce(qks[0:n, :], z_sq[0:n, :].rearrange("p (h d) -> p h d", d=HD), AX_X, ALU.add))
                dve.tensor_scalar(qks[0:n, :], qks[0:n, :], 1.0 / HD, EPS, ALU.mult, ALU.add).then_inc(z_summed, 1)
                dve.wait_ge(z_rstd, t + 1)
                if t >= 1:
                    dve.wait_ge(qkT_made, t)
                dve.tensor_tensor(q_norm[0:n, :, :, :].rearrange("p g k d -> p k g d"),
                                  zz[:, 0:HEADS, :].rearrange("p (k g) d -> p k g d", k=KV),
                                  qkr[0:n, 0:HEADS].rearrange("p (k g) -> p k g", k=KV).unsqueeze(3)
                                  .broadcast_to([n, KV, G, HD]), ALU.mult).then_inc(qk_normed, 1)
                dve.tensor_tensor(k_norm[0:n, :, :], zz[:, HEADS:, :],
                                  qkr[0:n, HEADS:].unsqueeze(2).broadcast_to([n, KV, HD]), ALU.mult).then_inc(qk_normed, 1)
                if t == PT:
                    dve.wait_ge(k_out_stored, DMA)
                if t >= PT - 1:
                    dve.wait_ge(qk_normed, 2 * t + 2)
                    dve.tensor_tensor(k_out[0:n, :, :], k_norm[0:n, :, :],
                                      k_gain[0:n, :].unsqueeze(1).broadcast_to([n, KV, HD]), ALU.mult).then_inc(k_out_made, 1)

            def qk_copy(t):
                n = rows(t)
                dve.wait_ge(qkT_made, t + 1)
                if t >= 1:
                    dve.wait_ge(s_made, 2 * t)
                if t < PT:
                    out = qT[:, :, 0:n]
                else:
                    out = qT[:, 0, :].rearrange("p (g n) -> p g n", g=G)
                dve.tensor_scalar(out, bank(psum, 4).rearrange("p (g n) -> p g n", g=G)[:, :, 0:n], qk_gain[:, 0:1],
                                  HD ** -0.5, ALU.mult, ALU.mult).then_inc(qkT_copied, 1)
                dve.tensor_scalar(kT[:, t, 0:n], bank(psum, 5)[:, 0:n], qk_gain[:, 1:2], None,
                                  ALU.mult).then_inc(qkT_copied, 1)

            def mask_scores(t, kv):
                u = 2 * t + kv
                k0 = block_keys(t)
                dve.wait_ge(s_made, u + 1)
                if u >= 1:
                    dve.wait_ge(p_made, u)
                for g in range(G):
                    ins = dve.tensor_tensor_reduce(s_sb[:, g, k0:], scores_bank()[:, g, k0:], mask[:, k0:], 1.0, NEG,
                                                   ALU.add, ALU.max, top[:, g:g + 1])
                step.did(ins)
                sink = sinks[:, kv * G:(kv + 1) * G]
                step.did(dve.tensor_tensor(top[:, :], top[:, :], sink, ALU.max))
                step.did(dve.tensor_scalar(ntop[:, kv, :], top[:, :], -1.0, None, ALU.mult))
                dve.tensor_tensor(sink_d[:, kv, :], sink, ntop[:, kv, :], ALU.add).then_inc(s_ready, 1)

            def pT_copy(t, kv):
                u = 2 * t + kv
                dve.wait_ge(pT_made, u + 1)
                if u >= 1:
                    dve.wait_ge(o_made, u)
                first = block_keys(t) // WIN
                for half in range(first, 2):
                    ins = dve.tensor_copy(pT[:, half, :, :].rearrange("p g c -> p (g c)"), bank(psum, 6 + half))
                ins.then_inc(pT_copied, 1)

            def o_scale(t, kv):
                u = 2 * t + kv
                if u >= 1:
                    dve.wait_ge(o_copied, u)
                step.did(dve.tensor_tensor(rden[:, :], den[:, kv, :], sink_e[:, kv, :], ALU.add))
                step.did(dve.reciprocal(rden[:, :], rden[:, :]))
                dve.wait_ge(o_made, u + 1)
                if t >= 1:
                    dve.wait_ge(oT_made, t)
                dve.tensor_tensor(o_sb[:, kv, :, :], bank(psum, 5)[:, 0:G * HD].rearrange("p (g d) -> p g d", g=G),
                                  rden[:, :].unsqueeze(2).broadcast_to([P, G, HD]), ALU.mult).then_inc(o_copied, 1)

            def oa_low(t):
                dve.wait_ge(oa_hi_made, t + 1)
                dve.tensor_tensor(oaT[1][:, :, toks(t)],
                                  bank(psum, 4).rearrange("p (k c) -> p k c", k=KE)[:, :, 0:rows(t)],
                                  oaT[0][:, :, toks(t)].bitcast(F32), ALU.subtract).then_inc(oa_lo_made, 1)

            mean_square(0)
            dve.wait_ge(const_in, DMA * N_CONST)
            h_scale(0)
            for c in range(NP):
                dve.wait_ge(w_hi_made, c + 1)
                dve.tensor_tensor(w_lo[:, :, c * P:(c + 1) * P], w_raw[:, c % 2],
                                  w_hi[:, :, c * P:(c + 1) * P].bitcast(F32), ALU.subtract).then_inc(w_lo_made, 1)
            mean_square(1)
            dve.wait_ge(masks_made, 1)
            h_scale(1)
            qk_scale(0)
            for s in range(1, NT):
                t = s - 1
                qk_copy(t)
                if s + 1 < NT:
                    mean_square(s + 1)
                mask_scores(t, 0)
                mask_scores(t, 1)
                pT_copy(t, 0)
                o_scale(t, 0)
                pT_copy(t, 1)
                o_scale(t, 1)
                if s + 1 < NT:
                    h_scale(s + 1)
                qk_scale(s)
                oa_low(t)
            qk_copy(PT)
            dve.wait_ge(cT_made, 1)
            for half in range(2):
                dve.tensor_copy(kT_cache[:, half * 512:(half + 1) * 512], bank(psum, 6 + half)).then_inc(cT_copied, 1)
            dve.wait_ge(masks_made, 2)
            for kv in range(KV):
                dve.wait_ge(ss_made, kv + 1)
                if kv == 1:
                    dve.wait_ge(spT_made, 1)
                for c in range(2):
                    part = slice(c * 512, (c + 1) * 512)
                    dve.tensor_tensor(s_scores[:, part], bank(psum, 2 + c), s_mask[:, part], ALU.add)
                step.did(dve.tensor_tensor(s_scores[:, DEC_B * WIN:], bank(psum, 1)[:, 0:NS], s_mask[:, DEC_B * WIN:],
                                           ALU.add))
                step.did(dve.tensor_reduce(top[:, 0:1], s_scores, AX_X, ALU.max))
                step.did(dve.tensor_tensor(top[:, 0:1], top[:, 0:1], s_sinks[:, kv:kv + 1], ALU.max))
                dve.tensor_scalar(ntop[:, kv, 0:1], top[:, 0:1], -1.0, None, ALU.mult).then_inc(ss_ready, 1)
                dve.wait_ge(sp_made, kv + 1)
                if kv == 0:
                    dve.wait_ge(o_copied, 2 * PT)
                else:
                    dve.wait_ge(so_copied, 1)
                step.did(dve.tensor_tensor(rden[:, 0:1], den[:, kv, 0:1], sink_e[:, kv, 0:1], ALU.add))
                step.did(dve.reciprocal(rden[:, 0:1], rden[:, 0:1]))
                dve.wait_ge(spT_made, kv + 1)
                if kv == 1:
                    dve.wait_ge(so_made, 1)
                for half in range(2):
                    dve.tensor_copy(pT_s[:, 4 * half:4 * half + 4, :].rearrange("p b c -> p (b c)"), bank(psum, 6 + half))
                dve.tensor_copy(pT_n[0:NS, :], bank(psum, 0)[0:NS, 0:P]).then_inc(spT_copied, 1)
                dve.wait_ge(so_made, kv + 1)
                for g in range(G):
                    q = slice(32 * g, 32 * g + 32)
                    ins = dve.tensor_scalar(o_sb[0:NS, kv, g, :], bank(psum, 5)[q, 0:HD], rden[q, 0:1], None, ALU.mult)
                ins.then_inc(so_copied, 1)
            oa_low(PT)

        block_ctx.close()
        with nc.Block() as clearing:
            @clearing.gpsimd
            def _(pool):
                for s in used:
                    pool.sem_clear(s)


def sgu_values_phase(nc, io, keep, psum):
    ident, hT, mixT = keep["ident"], (keep["hT_hi"], keep["hT_lo"]), keep["mixT"]
    NP = SW // P
    w_src = io["w_in"][0].rearrange("(k p) c -> p k c", p=P)

    with ExitStack() as ctx:
        def sb(name, shape, dt=F32):
            return ctx.enter_context(nc.sbuf_tensor(name, shape, dt))

        def sem(name):
            return keep["semaphores"].enter_context(nc.semaphore("v_" + name))

        w_raw = sb("vs_w_raw", [P, 2, KD, P])
        w_hi = sb("vs_w_hi", [P, KD, SW], F32R)
        w_lo = sb("vs_w_lo", [P, KD, SW], F32R)
        act_v = sb("act_v", [P, 2, SW])
        vs = sb("vs", [P, 2, SW])
        stats = sb("stats", [P, 6])
        mean_var = sb("mean_var", [P, 2])
        rstd = sb("rstd", [P, 1])
        minus_half = sb("v_minus_half", [P, 1])
        ln_g = sb("ln_g", [P, SW])
        ln_b = sb("ln_b", [P, SW])
        w_mix = sb("w_mix", [P, SG, P])
        w_mixT = sb("w_mixT", [P, SG, P])
        w_mixT_s = sb("w_mixT_s", [NS, SG, NS])
        b_mix = sb("b_mix", [P, SG, P])
        b_mix_s = sb("b_mix_s", [P, SG, NS])

        const_in, zeroed, blocks_in = sem("const_in"), sem("zeroed"), sem("blocks_in")
        w_in = [sem("w_in_even"), sem("w_in_odd")]
        w_hi_made, w_lo_made = sem("w_hi_made"), sem("w_lo_made")
        v_made, v_gelu, v_stats, v_rstd, v_norm, v_gain, vs_made = (
            sem("made"), sem("gelu"), sem("stats"), sem("rstd"), sem("norm"), sem("gain"), sem("vs_made"))
        dve_step, mixed, mix_added = sem("dve_step"), sem("mixed"), sem("mix_added")
        mixT_turned, mixT_copied, mix_ready = sem("mixT_turned"), sem("mixT_copied"), sem("mix_ready")
        vs_stored = sem("vs_stored")
        N_CONST = 4 + DEC_B
        block = ctx.enter_context(nc.Block())

        @block.sync
        def _(sp):
            for c in range(NP):
                if c >= 2:
                    sp.wait_ge(w_hi_made, c - 1)
                    sp.wait_ge(w_lo_made, c - 1)
                c0 = OFF_VS + c * P
                sp.dma_start(w_raw[:, c % 2], w_src[:, :, c0:c0 + P]).then_inc(w_in[c % 2], DMA)
            sp.wait_ge(zeroed, 1)
            for b in range(DEC_B):
                r = slice(b * DEC_T, (b + 1) * DEC_T)
                for h in range(SG):
                    sp.dma_start(w_mixT_s[r, h, r],
                                 io["w_spatial"][0, h, 0:DEC_T, 0:DEC_T].rearrange("i j -> j i")).then_inc(blocks_in, DMA)
            sp.wait_ge(vs_made, NT)
            sp.dma_start(io["new_vs"].rearrange("a b t g c -> (a b t) (g c)"), vs[0:NS, PT % 2, :]).then_inc(vs_stored, DMA)
            sp.wait_ge(vs_stored, DMA)

        @block.gpsimd
        def _(pool):
            pool.memset(w_mixT_s[:, :, :], 0.0).then_inc(zeroed, 1)
            pool.memset(minus_half[:, :], -0.5).then_inc(zeroed, 1)
            pool.wait_ge(mixT_copied, 1)
            pool.affine_select(out=w_mixT[:, :, :], in_=w_mixT[:, :, :], compare_op=ALU.is_ge, fill=0.0, base=0,
                               pattern=[[0, SG], [1, P]], channel_multiplier=-1).then_inc(mix_ready, 1)
            pool.wait_ge(blocks_in, DMA * DEC_B * SG)
            pool.affine_select(out=w_mixT_s[:, :, :], in_=w_mixT_s[:, :, :], compare_op=ALU.is_ge, fill=0.0, base=0,
                               pattern=[[0, SG], [1, NS]], channel_multiplier=-1).then_inc(mix_ready, 1)
            pool.wait_ge(zeroed, 2)
            pool.wait_ge(const_in, DMA * N_CONST)
            for t in range(NT):
                n = rows(t)
                pool.wait_ge(v_stats, t + 1)
                pool.tensor_tensor(rstd[0:n, :], mean_var[0:n, 1:2], minus_half[0:n, :], ALU.pow).then_inc(v_rstd, 1)
                pool.wait_ge(v_norm, t + 1)
                pool.tensor_tensor(vs[0:n, t % 2, :], act_v[0:n, t % 2, :], ln_g[0:n, :], ALU.mult).then_inc(v_gain, 1)
                pool.wait_ge(v_gain, t + 1)
                pool.tensor_tensor(vs[0:n, t % 2, :], vs[0:n, t % 2, :], ln_b[0:n, :], ALU.add).then_inc(vs_made, 1)

        @block.scalar
        def _(act):
            act.dma_start(w_mix[:, :, :], io["w_spatial"][0].rearrange("h i j -> i h j")).then_inc(const_in, DMA)
            act.dma_start(ln_g[:, :], io["ln_v_g"][0].partition_broadcast(P)).then_inc(const_in, DMA)
            act.dma_start(ln_b[:, :], io["ln_v_b"][0].partition_broadcast(P)).then_inc(const_in, DMA)
            act.dma_start(b_mix[:, :, :], io["b_spatial"][0].partition_broadcast(P)).then_inc(const_in, DMA)
            for b in range(DEC_B):
                act.dma_start(b_mix_s[:, :, b * DEC_T:(b + 1) * DEC_T],
                              io["b_spatial"][0, :, 0:DEC_T].partition_broadcast(P)).then_inc(const_in, DMA)
            for c in range(NP):
                act.wait_ge(w_in[c % 2], DMA * (c // 2 + 1))
                act.activation(w_hi[:, :, c * P:(c + 1) * P], w_raw[:, c % 2], ACT.Copy).then_inc(w_hi_made, 1)
            for t in range(NT):
                n = rows(t)
                act.wait_ge(v_made, t + 1)
                if t >= 2:
                    act.wait_ge(v_gain, t - 1)
                act.activation(act_v[0:n, t % 2, :], bank(psum, t % 2)[0:n, :], ACT.Gelu_apprx_tanh).then_inc(v_gelu, 1)

        @block.tensor
        def _(pe):
            pe.wait_ge(const_in, DMA * N_CONST)
            for h in range(SG):
                mm = pe.transpose(bank(psum, 4)[:, h * P:(h + 1) * P], w_mix[:, h, :], ident[:, :])
            mm.then_inc(mixT_turned, 1)
            pe.wait_ge(w_hi_made, NP)
            pe.wait_ge(w_lo_made, NP)

            def mix(t):
                n = rows(t)
                pe.wait_ge(vs_made, t + 1)
                pe.wait_ge(mix_ready, 1 if t < PT else 2)
                if t >= 2:
                    pe.wait_ge(mix_added, t - 1)
                w = w_mixT if t < PT else w_mixT_s
                for h in range(SG):
                    mm = pe.matmul(bank(psum, 2 + t % 2)[:, h * P:h * P + n], vs[0:n, t % 2, h * P:(h + 1) * P],
                                   w[0:n, h, 0:n], start=True, stop=True)
                mm.then_inc(mixed, 1)

            for t in range(NT):
                if t >= 2:
                    pe.wait_ge(v_gelu, t - 1)
                product(pe, bank(psum, t % 2)[0:rows(t), :], lambda k: (hT[0][:, k, toks(t)], hT[1][:, k, toks(t)]),
                        lambda k: (w_hi[:, k, :], w_lo[:, k, :]), KD).then_inc(v_made, 1)
                if t >= 1:
                    mix(t - 1)
            mix(PT)

        @block.vector
        def _(dve):
            step = Step(dve, dve_step)
            for c in range(NP):
                dve.wait_ge(w_hi_made, c + 1)
                dve.tensor_tensor(w_lo[:, :, c * P:(c + 1) * P], w_raw[:, c % 2],
                                  w_hi[:, :, c * P:(c + 1) * P].bitcast(F32), ALU.subtract).then_inc(w_lo_made, 1)
            dve.wait_ge(mixT_turned, 1)
            dve.tensor_copy(w_mixT[:, :, :].rearrange("p h i -> p (h i)"), bank(psum, 4)).then_inc(mixT_copied, 1)
            dve.wait_ge(const_in, DMA * N_CONST)

            def add_bias(t):
                n = rows(t)
                dve.wait_ge(mixed, t + 1)
                dve.tensor_tensor(mixT[:, :, toks(t)], bank(psum, 2 + t % 2).rearrange("p (h i) -> p h i", h=SG)[:, :, 0:n],
                                  (b_mix if t < PT else b_mix_s)[:, :, 0:n], ALU.add).then_inc(mix_added, 1)

            for t in range(NT):
                n = rows(t)
                a = act_v[0:n, t % 2, :]
                dve.wait_ge(v_gelu, t + 1)
                step.did(dve.bn_stats(stats[0:n, :], a))
                if t >= 1:
                    dve.wait_ge(v_norm, t)
                step.did(dve.bn_aggr(mean_var[0:n, :], stats[0:n, :]))
                dve.tensor_scalar(mean_var[0:n, 1:2], mean_var[0:n, 1:2], EPS, None, ALU.add).then_inc(v_stats, 1)
                dve.wait_ge(v_rstd, t + 1)
                if t >= 2:
                    dve.wait_ge(mixed, t - 1)
                dve.tensor_scalar(a, a, mean_var[0:n, 0:1], rstd[0:n, 0:1], ALU.subtract, ALU.mult).then_inc(v_norm, 1)
                if t >= 1:
                    add_bias(t - 1)
            add_bias(PT)


def sgu_gate_phase(nc, io, keep, psum):
    hT, mixT, obT = (keep["hT_hi"], keep["hT_lo"]), keep["mixT"], (keep["obT_hi"], keep["obT_lo"])
    w_src = io["w_in"][0].rearrange("(k p) c -> p k c", p=P)

    with ExitStack() as ctx:
        def sb(name, shape, dt=F32):
            return ctx.enter_context(nc.sbuf_tensor(name, shape, dt))

        def sem(name):
            return keep["semaphores"].enter_context(nc.semaphore("u_" + name))

        w_raw = sb("u_w_raw", [P, 2, KD, P])
        w_hi = sb("u_w_hi", [P, 2, KD, P], F32R)
        w_lo = sb("u_w_lo", [P, 2, KD, P], F32R)
        u_act = sb("u_act", [P, 2, TC])
        ob = sb("ob", [P, 2, TC])
        w_in = [sem("w_in_even"), sem("w_in_odd")]
        w_hi_made, w_lo_made = Flow(sem("w_hi_made")), Flow(sem("w_lo_made"))
        u_made, u_gelu, ob_made = Flow(sem("made"), 6), Flow(sem("gelu")), Flow(sem("ob_made"))
        hi_made, lo_made = Flow(sem("hi_made")), Flow(sem("lo_made"))
        block = ctx.enter_context(nc.Block())

        @block.sync
        def _(sp):
            with sp.Fori(0, KE // 2) as i:
                for j in range(2):
                    w_hi_made.wait(sp, 2 * i + (j - 2))
                    w_lo_made.wait(sp, 2 * i + (j - 2))
                    sp.dma_start(w_raw[:, j], w_src[:, :, bass.ds(i * 2 * P + (QKV + j * P), P)]).then_inc(w_in[j], DMA)

        @block.gpsimd
        def _(pool):
            lo_made.begin(pool)
            with pool.Fori(0, KE // 2) as i:
                for j in range(2):
                    for c in range(3):
                        m = 3 * j + c
                        hi_made.wait(pool, 6 * i + m)
                        part = slice(c * TC, (c + 1) * TC)
                        pool.tensor_tensor(obT[1][:, bass.ds(2 * i + j, 1), part], ob[:, m % 2, :].unsqueeze(1),
                                           obT[0][:, bass.ds(2 * i + j, 1), part].bitcast(F32),
                                           ALU.subtract).then_inc(lo_made.sem, 1)

        @block.scalar
        def _(act):
            w_hi_made.begin(act)
            u_gelu.begin(act)
            hi_made.begin(act)

            with act.Fori(0, KE // 2) as i:
                for j in range(2):
                    act.wait_ge(w_in[j], DMA * i + DMA)
                    u_made.wait(act, 6 * i + (3 * j - 4))
                    act.activation(w_hi[:, j], w_raw[:, j], ACT.Copy).then_inc(w_hi_made.sem, 1)
                for m in range(6):
                    j, c = m // 3, m % 3
                    u_made.wait(act, 6 * i + m)
                    ob_made.wait(act, 6 * i + (m - 2))
                    act.activation(u_act[:, m % 2, :], bank(psum, m % 2)[:, 0:TC], ACT.Gelu_apprx_tanh).then_inc(u_gelu.sem, 1)
                    ob_made.wait(act, 6 * i + m)
                    act.activation(obT[0][:, bass.ds(2 * i + j, 1), c * TC:(c + 1) * TC], ob[:, m % 2, :].unsqueeze(1),
                                   ACT.Copy).then_inc(hi_made.sem, 1)

        @block.tensor
        def _(pe):
            u_made.begin(pe)
            with pe.Fori(0, KE // 2) as i:
                for j in range(2):
                    w_hi_made.wait(pe, 2 * i + j)
                    w_lo_made.wait(pe, 2 * i + j)
                    for c in range(3):
                        m = 3 * j + c
                        u_gelu.wait(pe, 6 * i + (m - 2))
                        part = slice(c * TC, (c + 1) * TC)
                        product(pe, bank(psum, m % 2)[:, 0:TC], lambda k: (w_hi[:, j, k, :], w_lo[:, j, k, :]),
                                lambda k: (hT[0][:, k, part], hT[1][:, k, part]), KD).then_inc(u_made.sem, 1)

        @block.vector
        def _(dve):
            w_lo_made.begin(dve)
            ob_made.begin(dve)
            with dve.Fori(0, KE // 2) as i:
                for j in range(2):
                    w_hi_made.wait(dve, 2 * i + j)
                    u_made.wait(dve, 6 * i + (3 * j - 4))
                    dve.tensor_tensor(w_lo[:, j], w_raw[:, j], w_hi[:, j].bitcast(F32), ALU.subtract).then_inc(w_lo_made.sem, 1)
                for m in range(6):
                    j, c = m // 3, m % 3
                    u_gelu.wait(dve, 6 * i + m)
                    lo_made.wait(dve, 6 * i + (m - 2))
                    dve.tensor_tensor(ob[:, m % 2, :].unsqueeze(1), u_act[:, m % 2, :].unsqueeze(1),
                                      mixT[:, bass.ds(2 * i + j, 1), c * TC:(c + 1) * TC], ALU.mult).then_inc(ob_made.sem, 1)


def gates_phase(nc, io, keep, psum):
    hT = (keep["hT_hi"], keep["hT_lo"])
    branch = ((keep["oaT_hi"], keep["oaT_lo"]), (keep["obT_hi"], keep["obT_lo"]))
    KB = KD + KE
    w_gate = io["w_in"][0].rearrange("(k p) c -> p k c", p=P)
    w_branch = [io[n][0].rearrange("(k p) c -> p k c", p=P) for n in ("w_branch_a", "w_branch_b")]

    with ExitStack() as ctx:
        def sb(name, shape, dt=F32):
            return ctx.enter_context(nc.sbuf_tensor(name, shape, dt))

        def sem(name):
            return keep["semaphores"].enter_context(nc.semaphore("g_" + name))

        w_raw = sb("g_w_raw", [P, 2, KB, P])
        w_hi = sb("g_w_hi", [P, 2, KB, P], F32R)
        w_lo = sb("g_w_lo", [P, 2, KB, P], F32R)
        gate = sb("gate", [P, 2, TC])
        part_a = sb("part_a", [P, 3, TC])
        part_b = sb("part_b", [P, 3, TC])
        h2 = sb("h2", [P, 3, TC])
        w_in = [sem("w_in_a"), sem("w_in_b")]
        h2_stored = [sem(f"h2_stored_{c}") for c in range(3)]
        w_hi_made, w_lo_made = Flow(sem("w_hi_made")), Flow(sem("w_lo_made"))
        made, gated, multiplied, h2_made = (Flow(sem("made"), 6), Flow(sem("gated"), 4), Flow(sem("multiplied"), 4),
                                            Flow(sem("h2_made"), 3))
        block = ctx.enter_context(nc.Block())

        def pair(ab, c):
            return 2 * ((3 * ab + c) % 4)

        def over_pieces(eng, step):
            step(0, 0, 0)
            with eng.Fori(0, KD - 1) as i:
                step(2 * i + 1, i, 1)
                step(2 * i + 2, i + 1, 0)
            step(2 * KD - 1, KD - 1, 1)

        def is_last(q):
            return isinstance(q, int) and q == 2 * KD - 1

        @block.sync
        def _(sp):
            for c in range(3):
                sp.sem_inc(h2_stored[c], DMA)

            def store(d):
                for c in range(3):
                    h2_made.wait(sp, 3 * d + c)
                    sp.dma_start(io["h2T"][:, bass.ds(d, 1), c * TC:(c + 1) * TC],
                                 h2[:, c, :].unsqueeze(1)).then_inc(h2_stored[c], DMA)

            def load(q, d, ab):
                w_hi_made.wait(sp, q - 2)
                w_lo_made.wait(sp, q - 2)
                sp.dma_start(w_raw[:, ab, 0:KD], w_gate[:, :, bass.ds(d * P + (OFF_GA, OFF_GB)[ab], P)]).then_inc(w_in[ab], DMA)
                sp.dma_start(w_raw[:, ab, KD:], w_branch[ab][:, :, bass.ds(d * P, P)]).then_inc(w_in[ab], DMA)
                if ab == 0 and not (isinstance(q, int) and q == 0):
                    store(d - 1)

            over_pieces(sp, load)
            store(KD - 1)
            for c in range(3):
                sp.wait_ge(h2_stored[c], DMA * (KD + 1))

        @block.scalar
        def _(act):
            w_hi_made.begin(act)
            gated.begin(act)

            def weights(q, d, ab):
                act.wait_ge(w_in[ab], 2 * DMA * d + 2 * DMA)
                made.wait(act, 3 * q - 4)
                act.activation(w_hi[:, ab], w_raw[:, ab], ACT.Copy).then_inc(w_hi_made.sem, 1)

            def step(q, d, ab):
                if not is_last(q):
                    weights(q + 1, d + ab, 1 - ab)
                for c in range(3):
                    u = 3 * q + c
                    made.wait(act, u)
                    multiplied.wait(act, u - 2)
                    act.activation(gate[:, (ab + c) % 2, :], bank(psum, pair(ab, c))[:, 0:TC], ACT.Sigmoid).then_inc(gated.sem, 1)

            weights(0, 0, 0)
            over_pieces(act, step)

        @block.tensor
        def _(pe):
            made.begin(pe)

            def step(q, d, ab):
                w_hi_made.wait(pe, q)
                w_lo_made.wait(pe, q)
                src = branch[ab]
                for c in range(3):
                    u = 3 * q + c
                    gated.wait(pe, u - 2)
                    multiplied.wait(pe, u - 2)
                    part = slice(c * TC, (c + 1) * TC)
                    product(pe, bank(psum, pair(ab, c))[:, 0:TC], lambda k: (w_hi[:, ab, k, :], w_lo[:, ab, k, :]),
                            lambda k: (hT[0][:, k, part], hT[1][:, k, part]), KD)
                    product(pe, bank(psum, pair(ab, c) + 1)[:, 0:TC],
                            lambda k: (w_hi[:, ab, KD + k, :], w_lo[:, ab, KD + k, :]),
                            lambda k: (src[0][:, k, part], src[1][:, k, part]), KE).then_inc(made.sem, 1)

            over_pieces(pe, step)

        @block.vector
        def _(dve):
            w_lo_made.begin(dve)
            multiplied.begin(dve)
            h2_made.begin(dve)

            def weights(q, ab):
                w_hi_made.wait(dve, q)
                made.wait(dve, 3 * q - 4)
                dve.tensor_tensor(w_lo[:, ab], w_raw[:, ab], w_hi[:, ab].bitcast(F32), ALU.subtract).then_inc(w_lo_made.sem, 1)

            def step(q, d, ab):
                if not is_last(q):
                    weights(q + 1, 1 - ab)
                for c in range(3):
                    u = 3 * q + c
                    gated.wait(dve, u)
                    h2_made.wait(dve, 3 * d + c - 3)
                    out = part_b[:, c, :] if ab else part_a[:, c, :]
                    dve.tensor_tensor(out, bank(psum, pair(ab, c) + 1)[:, 0:TC], gate[:, (ab + c) % 2, :],
                                      ALU.mult).then_inc(multiplied.sem, 1)
                    if ab:
                        multiplied.wait(dve, u)
                        dve.wait_ge(h2_stored[c], DMA * d + DMA)
                        dve.tensor_tensor(h2[:, c, :], part_a[:, c, :], part_b[:, c, :], ALU.add).then_inc(h2_made.sem, 1)

            weights(0, 0)
            over_pieces(dve, step)


def merge_phase(nc, io, keep, psum):
    hT, ident, y, lg = (keep["hT_hi"], keep["hT_lo"]), keep["ident"], keep["y"], keep["lg"]
    w_src = io["w_out"][0].rearrange("(k p) c -> p k c", p=P)
    x_p = io["x"][0:SEQ, :].rearrange("(t p) d -> p t d", p=P)

    with ExitStack() as ctx:
        def sb(name, shape, dt=F32):
            return ctx.enter_context(nc.sbuf_tensor(name, shape, dt))

        def sem(name):
            return keep["semaphores"].enter_context(nc.semaphore("m_" + name))

        h2 = sb("h2_back", [P, 2, NTOK])
        w_raw = sb("o_w_raw", [P, 2, KD, P])
        w_hi = sb("o_w_hi", [P, 2, KD, P], F32R)
        w_lo = sb("o_w_lo", [P, 2, KD, P], F32R)
        x_in = sb("x_chunk", [P, 2, NT, P])
        wT = sb("woutT", [P, 2, NTOK])
        yT = sb("yT", [P, 2, NTOK])
        g2 = sb("g2_rows", [P, KD])
        w_r = sb("w_router", [P, KD, NR])
        const_in, h2_in, w_in, x_in_done = (sem("const_in"), [sem("h2_in_even"), sem("h2_in_odd")],
                                            [sem("w_in_even"), sem("w_in_odd")], [sem("x_in_even"), sem("x_in_odd")])
        passed = sem("passed")
        h2_hi, h2_lo, w_r_made, zeroed = sem("h2_hi"), sem("h2_lo"), sem("w_r_made"), sem("zeroed")
        w_hi_made, w_lo_made = Flow(sem("w_hi_made")), Flow(sem("w_lo_made"))
        made, evicted = Flow(sem("made"), 6), Flow(sem("evicted"), 6)
        xT_made, yT_made = Flow(sem("xT_made")), Flow(sem("yT_made"))
        back_made, y_copied, y_rest = Flow(sem("back_made")), Flow(sem("y_copied")), Flow(sem("y_rest"))
        block = ctx.enter_context(nc.Block())
        BANKS = ((0, 0, 4), (1, 4, 8), (2, 8, NT))

        def over_chunks(eng, step):
            step(0, 0)
            with eng.Fori(0, KD // 2 - 1) as i:
                step(2 * i + 1, 1)
                step(2 * i + 2, 0)
            step(KD - 1, 1)

        def times(d, j, per=DMA):
            return (d - j) * (per // 2) + per

        @block.sync
        def _(sp):
            for k in range(KD):
                if k >= 2:
                    sp.wait_ge(h2_lo, k - 1)
                sp.dma_start(h2[:, k % 2, :], io["h2T"][:, k, :]).then_inc(h2_in[k % 2], DMA)

        @block.gpsimd
        def _(pool):
            def load(d, j):
                w_hi_made.wait(pool, d - 2)
                w_lo_made.wait_alone(pool, d - 2, passed)
                pool.dma_start(w_raw[:, j], w_src[:, :, bass.ds(d * P, P)]).then_inc(w_in[j], DMA)
                xT_made.wait_alone(pool, d - 2, passed)
                pool.dma_start(x_in[:, j, 0:PT], x_p[:, :, bass.ds(d * P, P)]).then_inc(x_in_done[j], DMA)
                pool.dma_start(x_in[0:NS, j, PT], io["x"][SEQ:NTOK, bass.ds(d * P, P)]).then_inc(x_in_done[j], DMA)

            over_chunks(pool, load)

        @block.scalar
        def _(act):
            act.dma_start(g2[:, :], io["norm2_g"][0].rearrange("(k p) -> p k", p=P)).then_inc(const_in, DMA)
            act.dma_start(w_r[:, :, 0:NG], io["w_router_group"][0].rearrange("(k p) e -> p k e", p=P)).then_inc(const_in, DMA)
            act.dma_start(w_r[:, :, NG:], io["w_router_expert"][0].rearrange("(k p) e -> p k e", p=P)).then_inc(const_in, DMA)
            w_hi_made.begin(act)
            evicted.begin(act)
            y_copied.begin(act)

            def weights(d, j):
                act.wait_ge(w_in[j], times(d, j))
                made.wait(act, 3 * d - 4)
                act.activation(w_hi[:, j], w_raw[:, j], ACT.Copy).then_inc(w_hi_made.sem, 1)

            weights(0, 0)
            for k in range(KD):
                act.wait_ge(h2_in[k % 2], DMA * (k // 2 + 1))
                act.activation(hT[0][:, k, :], h2[:, k % 2, :], ACT.Copy).then_inc(h2_hi, 1)

            def step(d, j):
                if not (isinstance(d, int) and d == KD - 1):
                    weights(d + 1, 1 - j)
                for c in range(3):
                    made.wait(act, 3 * d + c)
                    if c == 0:
                        yT_made.wait(act, d - 2)
                    act.activation(wT[:, j, c * TC:(c + 1) * TC], bank(psum, c % 2)[:, 0:TC], ACT.Copy).then_inc(evicted.sem, 1)
                back_made.wait(act, d)
                for b, t0, t1 in BANKS[0:2]:
                    ins = act.activation(y[:, t0:t1, bass.ds(d * P, P)],
                                         bank(psum, 5 + b).rearrange("p (t c) -> p t c", c=P)[:, 0:t1 - t0], ACT.Copy)
                ins.then_inc(y_copied.sem, 1)

            over_chunks(act, step)

        @block.tensor
        def _(pe):
            made.begin(pe)
            xT_made.begin(pe)
            back_made.begin(pe)

            def step(d, j):
                pe.wait_ge(x_in_done[j], times(d, j, 2 * DMA))
                yT_made.wait(pe, d - 1)
                for b, t0, t1 in BANKS:
                    for t in range(t0, t1):
                        n = rows(t)
                        mm = pe.transpose(bank(psum, 2 + b)[:, (t - t0) * P:(t - t0) * P + n], x_in[0:n, j, t, :],
                                          ident[0:n, 0:n])
                mm.then_inc(xT_made.sem, 1)
                w_hi_made.wait(pe, d)
                w_lo_made.wait(pe, d)
                for c in range(3):
                    evicted.wait(pe, 3 * d + c - (1 if c == 0 else 2))
                    part = slice(c * TC, (c + 1) * TC)
                    if isinstance(d, int) and d == 0 and c == 0:
                        for k in range(KD):
                            pe.wait_ge(h2_lo, k + 1)
                            mm = product(pe, bank(psum, 0)[:, 0:TC], lambda _: (w_hi[:, j, k, :], w_lo[:, j, k, :]),
                                         lambda _: (hT[0][:, k, part], hT[1][:, k, part]), 1, k == 0, k == KD - 1)
                    else:
                        mm = product(pe, bank(psum, c % 2)[:, 0:TC], lambda k: (w_hi[:, j, k, :], w_lo[:, j, k, :]),
                                     lambda k: (hT[0][:, k, part], hT[1][:, k, part]), KD)
                    mm.then_inc(made.sem, 1)
                yT_made.wait(pe, d)
                y_copied.wait(pe, d - 1)
                y_rest.wait(pe, d - 1)
                if isinstance(d, int) and d == 0:
                    pe.wait_ge(w_r_made, 1)
                for b, t0, t1 in BANKS:
                    for t in range(t0, t1):
                        n = rows(t)
                        pe.transpose(bank(psum, 5 + b)[0:n, (t - t0) * P:(t - t0 + 1) * P], yT[:, j, toks(t)], ident[:, :])
                for t in range(NT):
                    mm = pe.matmul(bank(psum, 7)[0:rows(t), P + t * NR:P + (t + 1) * NR], yT[:, j, toks(t)],
                                   w_r[:, bass.ds(d, 1), :].rearrange("p a r -> p (a r)"), start=True, stop=True)
                mm.then_inc(back_made.sem, 1)

            over_chunks(pe, step)

        @block.vector
        def _(dve):
            w_lo_made.begin(dve)
            yT_made.begin(dve)
            y_rest.begin(dve)
            dve.memset(lg[:, :, :], 0.0).then_inc(zeroed, 1)
            dve.memset(y[:, PT, :], 0.0).then_inc(zeroed, 1)
            dve.wait_ge(const_in, DMA * 3)
            dve.tensor_tensor(w_r[:, :, :], w_r[:, :, :], g2[:, :].unsqueeze(2).broadcast_to([P, KD, NR]), ALU.mult).then_inc(w_r_made, 1)

            def weights(d, j):
                w_hi_made.wait(dve, d)
                made.wait(dve, 3 * d - 4)
                dve.tensor_tensor(w_lo[:, j], w_raw[:, j], w_hi[:, j].bitcast(F32), ALU.subtract).then_inc(w_lo_made.sem, 1)

            weights(0, 0)
            for k in range(KD):
                dve.wait_ge(h2_hi, k + 1)
                dve.tensor_tensor(hT[1][:, k, :], h2[:, k % 2, :], hT[0][:, k, :].bitcast(F32), ALU.subtract).then_inc(h2_lo, 1)
            dve.wait_ge(zeroed, 2)

            def step(d, j):
                if not (isinstance(d, int) and d == KD - 1):
                    weights(d + 1, 1 - j)
                xT_made.wait(dve, d)
                evicted.wait(dve, 3 * d + 2)
                back_made.wait(dve, d - 2)
                for b, t0, t1 in BANKS:
                    part = slice(t0 * P, min(t1 * P, NTOK))
                    ins = dve.tensor_tensor(yT[:, j, part], bank(psum, 2 + b)[:, 0:part.stop - part.start], wT[:, j, part], ALU.add)
                ins.then_inc(yT_made.sem, 1)
                back_made.wait(dve, d)
                dve.tensor_copy(y[0:NS, PT:NT, bass.ds(d * P, P)], bank(psum, 7)[0:NS, 0:P].unsqueeze(1))
                y_rest.wait(dve, d - 1)
                sums = bank(psum, 7)[:, P:P + NT * NR].rearrange("p (t r) -> p t r", r=NR)
                dve.tensor_tensor(lg[:, 0:PT, :], lg[:, 0:PT, :], sums[:, 0:PT], ALU.add)
                dve.tensor_tensor(lg[0:NS, PT, :], lg[0:NS, PT, :], sums[0:NS, PT], ALU.add).then_inc(y_rest.sem, 1)

            over_chunks(dve, step)


def routing_phase(nc, io, keep, psum):
    ident, y, lg = keep["ident"], keep["y"], keep["lg"]
    slot_w, gather_at, scatter_at, step_expert = keep["slot_w"], keep["gather_at"], keep["scatter_at"], keep["step_expert"]

    with ExitStack() as ctx:
        def sb(name, shape, dt=F32):
            return ctx.enter_context(nc.sbuf_tensor("r_" + name, shape, dt))

        def sem(name):
            return keep["semaphores"].enter_context(nc.semaphore("r_" + name))

        hn = sb("hn", [P, 3, D])
        g2 = sb("g2", [P, D])
        bias = sb("bias", [P, NR])
        zeros = sb("zeros", [P, D])

        yss = sb("yss", [P, NT])
        r2 = sb("r2", [P, NT])
        minus_half = sb("minus_half", [P, NT])
        logits = sb("logits", [P, NT, NR])
        g_top = sb("g_top", [P, NT])
        g_exp = sb("g_exp", [P, NT, NG])
        g_sum = sb("g_sum", [P, NT])
        g_pick = sb("g_pick", [P, NT, NG])
        eq = sb("eq", [P, NT, EPG])
        pr_top = sb("pr_top", [P, NT])
        prio = sb("prio", [P, EPG])
        sel4 = sb("sel4", [P, NT, NG, EPG])
        e_sel = sb("e_sel", [P, NT, EPG])
        e_top = sb("e_top", [P, 2, NT])
        e_pick = sb("e_pick", [P, 2, NT, EPG])
        wts = sb("wts", [P, 2, NT])
        ratio = sb("ratio", [P, NT])
        chosen = sb("chosen", [P, 2, NT, NE])
        both = sb("both", [P, NT + 1, NE])
        before = sb("before", [P, NT + 1, NE])
        lower = sb("lower", [P, P])
        ones = sb("ones", [P, P])
        place = sb("place", [P, NT, NE])
        limits = sb("limits", [P, NT])
        over = sb("over", [P, NE, NT])
        steps_of = sb("steps_of", [P, NE])
        step_end = sb("step_end", [P, NE])
        picked = sb("picked", [P, NT, NE])
        slot = sb("slot", [P, 2, NT])
        slot_i = sb("slot_i", [P, 2, NT], I32)
        slot_hi_i = sb("slot_hi_i", [P, 2, NT], I32)
        slot_lo_i = sb("slot_lo_i", [P, 2, NT], I32)
        slot_hi = sb("slot_hi", [P, 2, NT])
        slot_lo = sb("slot_lo", [P, 2, NT])
        slots = sb("slots", [P, P])
        steps = sb("steps", [P, NSTEP])
        number = sb("number", [P, NT])
        in_slot = sb("in_slot", [P, 4, P])
        in_step = sb("in_step", [P, 4, 2, NSTEP])
        found = sb("found", [P, 2, NSTEP])
        empty = sb("empty", [P, NSTEP])
        spare = sb("spare", [P, 1])
        where = sb("where", [P, NSTEP])
        ended = sb("ended", [P, NSTEP, NE])
        expert_f = sb("expert_f", [P, NSTEP])
        slots_i = sb("slots_i", [P, P], I32)

        const_in, consts, stored = sem("const_in"), sem("consts"), sem("stored")
        hn_stored = [sem(f"hn_stored_{b}") for b in range(3)]
        dve_step, squared, meaned, rooted, hn_made = (sem("dve_step"), sem("squared"), sem("meaned"), sem("rooted"),
                                                      sem("hn_made"))
        g_shifted, g_exped, e_shifted, e_exped = sem("g_shifted"), sem("g_exped"), sem("e_shifted"), sem("e_exped")
        sums_ready, sums_made, pair_made, pair_used, found_made = (sem("sums_ready"), sem("sums_made"), sem("pair_made"),
                                                                   sem("pair_used"), sem("found_made"))
        sq_done = sem("sq_done")
        block = ctx.enter_context(nc.Block())

        @block.sync
        def _(sp):
            for t in range(NT):
                sp.dma_start(io["y"][toks(t), :], y[0:rows(t), t, :]).then_inc(stored, DMA)
            sp.wait_ge(consts, 1)
            sp.dma_start(io["y"][NTOK:NTOK + SLOT, :], zeros[:, :]).then_inc(stored, DMA)
            for t in range(NT):
                sp.wait_ge(hn_made, t + 1)
                sp.dma_start(io["hn"][toks(t), :], hn[0:rows(t), t % 3, :]).then_inc(hn_stored[t % 3], DMA)
            sp.wait_ge(stored, DMA * (NT + 1))
            for b in range(3):
                sp.wait_ge(hn_stored[b], DMA * 3)

        @block.gpsimd
        def _(pool):
            pool.memset(zeros[:, :], 0.0).then_inc(consts, 1)
            pool.memset(minus_half[:, :], -0.5).then_inc(consts, 1)
            pool.memset(ones[:, :], 1.0).then_inc(consts, 1)
            pool.memset(lower[:, :], 1.0).then_inc(consts, 1)
            pool.wait_ge(consts, 4)
            pool.affine_select(out=lower[:, :], in_=lower[:, :], compare_op=ALU.is_ge, fill=0.0, base=-1,
                               pattern=[[1, P]], channel_multiplier=-1).then_inc(consts, 1)
            kw = dict(allow_small_or_imprecise_dtypes=True)
            pool.iota(prio[:, :], [[-1, EPG]], base=EPG, channel_multiplier=0, **kw).then_inc(consts, 1)
            pool.iota(limits[:, :], [[SLOT, NT]], base=0, channel_multiplier=0, **kw).then_inc(consts, 1)
            pool.iota(slots[:, :], [[1, P]], base=0, channel_multiplier=0, **kw).then_inc(consts, 1)
            pool.iota(steps[:, :], [[1, NSTEP]], base=0, channel_multiplier=0, **kw).then_inc(consts, 1)
            pool.iota(number[:, :], [[P, NT]], base=1, channel_multiplier=1, **kw).then_inc(consts, 1)
            pool.iota(spare[:, :], [[1, 1]], base=NTOK + 1, channel_multiplier=1, **kw).then_inc(consts, 1)
            pool.wait_ge(meaned, 1)
            pool.tensor_tensor(r2[:, :], yss[:, :], minus_half[:, :], ALU.pow).then_inc(rooted, 1)

        @block.scalar
        def _(act):
            act.dma_start(g2[:, :], io["norm2_g"][0].partition_broadcast(P)).then_inc(const_in, DMA)
            act.dma_start(bias[:, 0:NG], io["b_router_group"][0].partition_broadcast(P)).then_inc(const_in, DMA)
            act.dma_start(bias[:, NG:], io["b_router_expert"][0].partition_broadcast(P)).then_inc(const_in, DMA)
            for t in range(NT):
                if t >= 3:
                    act.wait_ge(squared, t - 2)
                act.activation(hn[:, t % 3, :], y[:, t, :], ACT.Square, accum_out=yss[:, t:t + 1]).then_inc(squared, 1)
            act.wait_ge(g_shifted, 1)
            act.activation(g_exp[:, :, :], g_exp[:, :, :], ACT.Exp).then_inc(g_exped, 1)
            act.wait_ge(e_shifted, 1)
            act.activation(ratio[:, :], ratio[:, :], ACT.Exp).then_inc(e_exped, 1)

        @block.tensor
        def _(pe):
            pe.wait_ge(sums_ready, 1)
            width = (NT + 1) * NE
            flat = [a[:, :, :].rearrange("p t e -> p (t e)") for a in (both, before)]
            pe.matmul(bank(psum, 0)[:, 0:width], lower[:, :], flat[0], start=True, stop=False)
            pe.matmul(bank(psum, 0)[:, 0:width], ones[:, :], flat[1], start=False, stop=True).then_inc(sums_made, 1)
            for n in range(2 * NT):
                pe.wait_ge(pair_made, n + 1)
                pe.matmul(bank(psum, 1)[:, 0:2 * NSTEP], in_slot[:, n % 4, :],
                          in_step[:, n % 4, :, :].rearrange("p a s -> p (a s)"), start=n == 0,
                          stop=n == 2 * NT - 1).then_inc(pair_used, 1)

        @block.vector
        def _(dve):
            step = Step(dve, dve_step)
            did = step.did

            def tt(out, a, b, op):
                did(dve.tensor_tensor(out, a, b, op))

            def over_last(a, n):
                return a.unsqueeze(2).broadcast_to([P, NT, n])

            def first_top(out, values, top):
                tt(out, values, over_last(top, EPG), ALU.is_equal)
                tt(eq[:, :, :], out, prio[:, :].unsqueeze(1).broadcast_to([P, NT, EPG]), ALU.mult)
                did(dve.tensor_reduce(pr_top[:, :], eq[:, :, :], AX_X, ALU.max))
                tt(out, eq[:, :, :], over_last(pr_top[:, :], EPG), ALU.is_equal)

            dve.wait_ge(squared, NT)
            dve.tensor_scalar(yss[:, :], yss[:, :], 1.0 / D, EPS, ALU.mult, ALU.add).then_inc(meaned, 1)
            dve.wait_ge(const_in, DMA * 3)
            dve.wait_ge(consts, 11)
            dve.wait_ge(rooted, 1)
            tt(logits[:, :, :], lg[:, :, :], over_last(r2[:, :], NR), ALU.mult)
            tt(logits[:, :, :], logits[:, :, :], bias[:, :].unsqueeze(1).broadcast_to([P, NT, NR]), ALU.add)
            gl = logits[:, :, 0:NG]
            el = logits[:, :, NG:].rearrange("p t (g e) -> p t g e", g=NG)
            did(dve.tensor_reduce(g_top[:, :], gl, AX_X, ALU.max))
            dve.tensor_tensor(g_exp[:, :, :], gl, over_last(g_top[:, :], NG), ALU.subtract).then_inc(g_shifted, 1)
            first_top(g_pick[:, :, :], gl, g_top[:, :])
            tt(sel4[:, :, :, :], el, g_pick[:, :, :].unsqueeze(3).broadcast_to([P, NT, NG, EPG]), ALU.mult)
            did(dve.tensor_reduce(e_sel[:, :, :], sel4[:, :, :, :].rearrange("p t g e -> p t e g"), AX_X, ALU.add))
            for n in range(2):
                did(dve.tensor_reduce(e_top[:, n, :], e_sel[:, :, :], AX_X, ALU.max))
                first_top(e_pick[:, n, :, :], e_sel[:, :, :], e_top[:, n, :])
                if n == 0:
                    did(dve.scalar_tensor_tensor(e_sel[:, :, :], e_pick[:, 0, :, :], NEG, e_sel[:, :, :], ALU.mult, ALU.add))
            dve.tensor_tensor(ratio[:, :], e_top[:, 1, :], e_top[:, 0, :], ALU.subtract).then_inc(e_shifted, 1)
            for n in range(2):
                tt(chosen[:, n, :, :].rearrange("p t (g e) -> p t g e", g=NG),
                   g_pick[:, :, :].unsqueeze(3).broadcast_to([P, NT, NG, EPG]),
                   e_pick[:, n, :, :].unsqueeze(2).broadcast_to([P, NT, NG, EPG]), ALU.mult)
            for q in range(NS, P, 32):
                did(dve.memset(chosen[q:q + 32, :, PT, :], 0.0))
                did(dve.memset(number[q:q + 32, PT:NT], 0.0))
            did(dve.memset(both[:, NT, :], 0.0))
            tt(both[:, 0:NT, :], chosen[:, 0, :, :], chosen[:, 1, :, :], ALU.add)
            did(dve.memset(before[:, 0, :], 0.0))
            for t in range(NT - 1):
                tt(before[:, t + 1, :], before[:, t, :], both[:, t, :], ALU.add)
            dve.tensor_tensor(before[:, NT, :], before[:, NT - 1, :], both[:, NT - 1, :], ALU.add).then_inc(sums_ready, 1)
            dve.wait_ge(g_exped, 1)
            did(dve.tensor_reduce(g_sum[:, :], g_exp[:, :, :], AX_X, ALU.add))
            dve.wait_ge(e_exped, 1)
            did(dve.tensor_scalar(wts[:, 0, :], ratio[:, :], 1.0, None, ALU.add))
            tt(wts[:, 0, :], wts[:, 0, :], g_sum[:, :], ALU.mult)
            did(dve.reciprocal(wts[:, 0, :], wts[:, 0, :]))
            tt(wts[:, 1, :], wts[:, 0, :], ratio[:, :], ALU.mult)
            for q in range(NS, P, 32):
                did(dve.memset(wts[q:q + 32, :, PT:NT], 0.0))
            dve.wait_ge(sums_made, 1)
            sums = bank(psum, 0)[:, 0:(NT + 1) * NE].rearrange("p (t e) -> p t e", e=NE)
            did(dve.tensor_copy(place[:, :, :], sums[:, 0:NT, :]))
            did(dve.tensor_copy(step_end[:, :], sums[:, NT, :]))
            tt(over[:, :, :], step_end[:, :].unsqueeze(2).broadcast_to([P, NE, NT]),
               limits[:, :].unsqueeze(1).broadcast_to([P, NE, NT]), ALU.is_gt)
            did(dve.tensor_reduce(steps_of[:, :], over[:, :, :], AX_X, ALU.add))
            did(dve.tensor_tensor_scan(step_end[:, :], ones[:, 0:NE], steps_of[:, :], 0.0, ALU.mult, ALU.add))
            tt(steps_of[:, :], step_end[:, :], steps_of[:, :], ALU.subtract)
            did(dve.tensor_scalar(steps_of[:, :], steps_of[:, :], float(SLOT), None, ALU.mult))
            tt(place[:, :, :], place[:, :, :], steps_of[:, :].unsqueeze(1).broadcast_to([P, NT, NE]), ALU.add)
            for n in range(2):
                tt(picked[:, :, :], place[:, :, :], chosen[:, n, :, :], ALU.mult)
                did(dve.tensor_reduce(slot[:, n, :], picked[:, :, :], AX_X, ALU.add))
            did(dve.tensor_copy(slot_i[:, :, :], slot[:, :, :]))
            did(dve.tensor_scalar(slot_hi_i[:, :, :], slot_i[:, :, :], SLOT.bit_length() - 1, None, ALU.logical_shift_right))
            did(dve.tensor_scalar(slot_lo_i[:, :, :], slot_i[:, :, :], SLOT - 1, None, ALU.bitwise_and))
            did(dve.tensor_copy(slot_hi[:, :, :], slot_hi_i[:, :, :]))
            did(dve.tensor_copy(slot_lo[:, :, :], slot_lo_i[:, :, :]))
            for n in range(2 * NT):
                t, c = n // 2, n % 2
                if n >= 4:
                    dve.wait_ge(pair_used, n - 3)
                dve.tensor_scalar(in_slot[:, n % 4, :], slots[:, :], slot_lo[:, c, t:t + 1], None, ALU.is_equal)
                for v, value in enumerate((number[:, t:t + 1], wts[:, c, t:t + 1])):
                    ins = dve.tensor_scalar(in_step[:, n % 4, v, :], steps[:, :], slot_hi[:, c, t:t + 1], value,
                                            ALU.is_equal, ALU.mult)
                ins.then_inc(pair_made, 1)
            tt(ended[:, :, :], step_end[:, :].unsqueeze(1).broadcast_to([P, NSTEP, NE]),
               steps[:, :].unsqueeze(2).broadcast_to([P, NSTEP, NE]), ALU.is_le)
            did(dve.tensor_reduce(expert_f[:, :], ended[:, :, :], AX_X, ALU.add))
            did(dve.tensor_scalar(expert_f[:, :], expert_f[:, :], float(NE - 1), None, ALU.min))
            did(dve.tensor_copy(step_expert[:, :], expert_f[:, :]))
            dve.wait_ge(pair_used, 2 * NT)
            did(dve.tensor_copy(found[:, :, :].rearrange("p a s -> p (a s)"), bank(psum, 1)[:, 0:2 * NSTEP]))
            did(dve.tensor_copy(slot_w[:, :], found[:, 1, :]))
            did(dve.tensor_scalar(where[:, :], found[:, 0, :], -1.0, 0.0, ALU.add, ALU.max))
            did(dve.tensor_copy(gather_at[:, :], where[:, :]))
            did(dve.tensor_scalar(empty[:, :], found[:, 0, :], 0.0, spare[:, 0:1], ALU.is_equal, ALU.mult))
            tt(empty[:, :], empty[:, :], found[:, 0, :], ALU.add)
            did(dve.tensor_scalar(empty[:, :], empty[:, :], -1.0, None, ALU.add))
            did(dve.tensor_copy(scatter_at[:, :], empty[:, :]))
            for t in range(NT):
                n = rows(t)
                if t >= 3:
                    dve.wait_ge(hn_stored[t % 3], DMA * (t // 3))
                dve.scalar_tensor_tensor(hn[0:n, t % 3, :], y[0:n, t, :], r2[0:n, t:t + 1], g2[0:n, :], ALU.mult,
                                         ALU.mult).then_inc(hn_made, 1)


def experts_phase(nc, io, keep, psum):
    ident = keep["ident"]
    slot_w, gather_at, scatter_at, step_expert = keep["slot_w"], keep["gather_at"], keep["scatter_at"], keep["step_expert"]
    w_gate = io["w_exp_gate"][0].rearrange("e (k p) f -> p e k f", p=P)
    w_up = io["w_exp_up"][0].rearrange("e (k p) f -> p e k f", p=P)
    w_down = io["w_exp_down"][0].rearrange("e (k p) d -> p e k d", p=P)
    KF = DE // P
    HD2 = D // 2

    with ExitStack() as ctx:
        def sb(name, shape, dt=F32):
            return ctx.enter_context(nc.sbuf_tensor("x_" + name, shape, dt))

        def sem(name):
            return keep["semaphores"].enter_context(nc.semaphore("x_" + name))

        gu_raw = sb("gu_raw", [P, 2, KD, 2, DE])
        gu_hi = sb("gu_hi", [P, 2, KD, 2, DE], F32R)
        gu_lo = sb("gu_lo", [P, 2, KD, 2, DE], F32R)
        dn_raw = sb("dn_raw", [P, 2, KF, D])
        dn_hi = sb("dn_hi", [P, 2, KF, D], F32R)
        dn_lo = sb("dn_lo", [P, 2, KF, D], F32R)
        at = sb("at", [P, 2, 2], I32)
        xg = sb("xg", [P, 2, D])
        xT_hi = sb("xT_hi", [P, 2, KD, P], F32R)
        xT_lo = sb("xT_lo", [P, 2, KD, P], F32R)
        silu = sb("silu", [P, DE])
        hid = sb("hid", [P, DE])
        hidT_hi = sb("hidT_hi", [P, KF, P], F32R)
        hidT_lo = sb("hidT_lo", [P, KF, P], F32R)
        out = sb("out", [P, 2, D])

        gu_in, dn_in = [sem("gu_in_0"), sem("gu_in_1")], [sem("dn_in_0"), sem("dn_in_1")]
        gathered, added = [sem("gathered_0"), sem("gathered_1")], sem("added")
        passed = sem("passed")
        gu_hi_made, gu_lo_made = Flow(sem("gu_hi_made")), Flow(sem("gu_lo_made"))
        dn_hi_made, dn_lo_made = Flow(sem("dn_hi_made")), Flow(sem("dn_lo_made"))
        at_made, xT_made, xT_hi_made, xT_lo_made = Flow(sem("at_made")), Flow(sem("xT_made")), Flow(sem("xT_hi_made")), Flow(sem("xT_lo_made"))
        up_made, silu_made, hid_made = Flow(sem("up_made")), Flow(sem("silu_made")), Flow(sem("hid_made"))
        hidT_made, hidT_hi_made, hidT_lo_made = Flow(sem("hidT_made")), Flow(sem("hidT_hi_made")), Flow(sem("hidT_lo_made"))
        down_made, out_made, at_copied = Flow(sem("down_made")), Flow(sem("out_made")), Flow(sem("at_copied"))
        add_turn = Flow(sem("add_turn"))
        block = ctx.enter_context(nc.Block())

        def over_steps(eng, step):
            step(0, 0)
            with eng.Fori(0, NSTEP // 2 - 1) as i:
                step(2 * i + 1, 1)
                step(2 * i + 2, 0)
            step(NSTEP - 1, 1)

        def first(s):
            return isinstance(s, int) and s == 0

        def last(s):
            return isinstance(s, int) and s == NSTEP - 1

        def times(s, j, per=DMA):
            return (s - j) * (per // 2) + per

        @block.sync
        def _(sp):
            def load(s, j):
                e = sp.value_load(step_expert[0:1, bass.ds(s, 1)], min_val=0, max_val=NE - 1)
                gu_hi_made.wait(sp, s - 2)
                gu_lo_made.wait(sp, s - 2)
                sp.dma_start(gu_raw[:, j, :, 0, :].unsqueeze(1), w_gate[:, bass.ds(e, 1)]).then_inc(gu_in[j], DMA)
                sp.dma_start(gu_raw[:, j, :, 1, :].unsqueeze(1), w_up[:, bass.ds(e, 1)]).then_inc(gu_in[j], DMA)
                dn_hi_made.wait(sp, s - 2)
                dn_lo_made.wait(sp, s - 2)
                sp.dma_start(dn_raw[:, j].unsqueeze(1), w_down[:, bass.ds(e, 1)]).then_inc(dn_in[j], DMA)

            over_steps(sp, load)

        @block.gpsimd
        def _(pool):
            at_made.begin(pool)
            dn_lo_made.begin(pool)

            def gather(s, j):
                xT_made.wait(pool, s - 2)
                pool.tensor_copy(at[:, j, 0:1], gather_at[:, bass.ds(s, 1)]).then_inc(at_made.sem, 1)
                at_made.wait_alone(pool, s, passed)
                pool.indirect_dma_start(xg[:, j, :], None, io["hn"], bass.IndirectOffsetOnAxis(at[:, j, 0:1], 0)).then_inc(gathered[j], DMA)

            def scatter(s, j):
                out_made.wait(pool, s)
                pool.tensor_copy(at[:, j, 1:2], scatter_at[:, bass.ds(s, 1)]).then_inc(at_copied.sem, 1)
                at_copied.wait(pool, s)
                if not first(s):
                    pool.wait_ge(added, s * DMA)
                pool.sem_inc(add_turn.sem, 1)
                pool.indirect_dma_start(io["y"], bass.IndirectOffsetOnAxis(at[:, j, 1:2], 0), out[:, j, :], None,
                                        compute_op=ALU.add).then_inc(added, DMA)

            at_copied.begin(pool)
            add_turn.begin(pool)

            def step(s, j):
                gather(s, j)
                dn_hi_made.wait(pool, s)
                down_made.wait(pool, s - 2)
                pool.tensor_tensor(dn_lo[:, j], dn_raw[:, j], dn_hi[:, j].bitcast(F32), ALU.subtract).then_inc(dn_lo_made.sem, 1)
                if not first(s):
                    scatter(s - 1, 1 - j)

            over_steps(pool, step)
            scatter(NSTEP - 1, 1)
            pool.wait_ge(added, DMA * NSTEP)

        @block.scalar
        def _(act):
            for f in (gu_hi_made, dn_hi_made, xT_hi_made, silu_made, hidT_hi_made):
                f.begin(act)

            def weights(s, j):
                act.wait_ge(gu_in[j], times(s, j, 2 * DMA))
                up_made.wait(act, s - 2)
                act.activation(gu_hi[:, j].rearrange("p k a f -> p (k a f)"), gu_raw[:, j].rearrange("p k a f -> p (k a f)"),
                               ACT.Copy).then_inc(gu_hi_made.sem, 1)
                act.wait_ge(dn_in[j], times(s, j))
                down_made.wait(act, s - 2)
                act.activation(dn_hi[:, j].rearrange("p k d -> p (k d)"), dn_raw[:, j].rearrange("p k d -> p (k d)"),
                               ACT.Copy).then_inc(dn_hi_made.sem, 1)

            def token_parts(s, j):
                xT_made.wait(act, s)
                up_made.wait(act, s - 2)
                for half in range(2):
                    ins = act.activation(xT_hi[:, j, 4 * half:4 * half + 4, :].rearrange("p k c -> p (k c)"),
                                         bank(psum, half), ACT.Copy)
                ins.then_inc(xT_hi_made.sem, 1)

            def hidden_parts(s):
                hidT_made.wait(act, s)
                down_made.wait(act, s - 1)
                act.activation(hidT_hi[:, :, :].rearrange("p k c -> p (k c)"), bank(psum, 4)[:, 0:DE], ACT.Copy).then_inc(hidT_hi_made.sem, 1)

            def step(s, j):
                token_parts(s, j)
                if not first(s):
                    hidden_parts(s - 1)
                if not last(s):
                    weights(s + 1, 1 - j)
                up_made.wait(act, s)
                hid_made.wait(act, s - 1)
                act.activation(silu[:, :], bank(psum, 2 + j)[:, 0:DE], ACT.Silu).then_inc(silu_made.sem, 1)

            weights(0, 0)
            over_steps(act, step)
            hidden_parts(NSTEP - 1)

        @block.tensor
        def _(pe):
            for f in (xT_made, up_made, hidT_made, down_made):
                f.begin(pe)

            def hidden_turn(s):
                hid_made.wait(pe, s)
                hidT_lo_made.wait(pe, s - 1)
                for f in range(KF):
                    mm = pe.transpose(bank(psum, 4)[:, f * P:(f + 1) * P], hid[:, f * P:(f + 1) * P], ident[:, :])
                mm.then_inc(hidT_made.sem, 1)

            def down(s, j):
                hidT_hi_made.wait(pe, s)
                hidT_lo_made.wait(pe, s)
                dn_hi_made.wait(pe, s)
                dn_lo_made.wait(pe, s)
                out_made.wait(pe, s - 1)
                for n in range(2):
                    part = slice(n * HD2, (n + 1) * HD2)
                    mm = product(pe, bank(psum, 5 + n), lambda k: (hidT_hi[:, k, :], hidT_lo[:, k, :]),
                                 lambda k: (dn_hi[:, j, k, part], dn_lo[:, j, k, part]), KF)
                mm.then_inc(down_made.sem, 1)

            def step(s, j):
                pe.wait_ge(gathered[j], times(s, j))
                xT_lo_made.wait(pe, s - 1)
                for k in range(KD):
                    mm = pe.transpose(bank(psum, k // 4)[:, (k % 4) * P:(k % 4 + 1) * P], xg[:, j, k * P:(k + 1) * P], ident[:, :])
                mm.then_inc(xT_made.sem, 1)
                if not first(s):
                    hidden_turn(s - 1)
                xT_hi_made.wait(pe, s)
                xT_lo_made.wait(pe, s)
                gu_hi_made.wait(pe, s)
                gu_lo_made.wait(pe, s)
                hid_made.wait(pe, s - 2)
                product(pe, bank(psum, 2 + j), lambda k: (xT_hi[:, j, k, :], xT_lo[:, j, k, :]),
                        lambda k: (gu_hi[:, j, k].rearrange("p a f -> p (a f)"), gu_lo[:, j, k].rearrange("p a f -> p (a f)")),
                        KD).then_inc(up_made.sem, 1)
                if not first(s):
                    down(s - 1, 1 - j)

            over_steps(pe, step)
            hidden_turn(NSTEP - 1)
            down(NSTEP - 1, 1)

        @block.vector
        def _(dve):
            for f in (gu_lo_made, xT_lo_made, hid_made, hidT_lo_made, out_made):
                f.begin(dve)

            def weights(s, j):
                gu_hi_made.wait(dve, s)
                up_made.wait(dve, s - 2)
                dve.tensor_tensor(gu_lo[:, j].rearrange("p k a f -> p (k a f)"), gu_raw[:, j].rearrange("p k a f -> p (k a f)"),
                                  gu_hi[:, j].rearrange("p k a f -> p (k a f)").bitcast(F32), ALU.subtract).then_inc(gu_lo_made.sem, 1)

            def token_parts(s, j):
                xT_hi_made.wait(dve, s)
                for half in range(2):
                    ks = slice(4 * half, 4 * half + 4)
                    ins = dve.tensor_tensor(xT_lo[:, j, ks, :].rearrange("p k c -> p (k c)"), bank(psum, half),
                                            xT_hi[:, j, ks, :].rearrange("p k c -> p (k c)").bitcast(F32), ALU.subtract)
                ins.then_inc(xT_lo_made.sem, 1)

            def hidden_parts(s):
                hidT_hi_made.wait(dve, s)
                dve.tensor_tensor(hidT_lo[:, :, :].rearrange("p k c -> p (k c)"), bank(psum, 4)[:, 0:DE],
                                  hidT_hi[:, :, :].rearrange("p k c -> p (k c)").bitcast(F32), ALU.subtract).then_inc(hidT_lo_made.sem, 1)

            def evict(s, j):
                down_made.wait(dve, s)
                add_turn.wait(dve, s - 1)
                dve.tensor_copy(out[:, j, :], psum[:, 5:7, :].rearrange("p a c -> p (a c)")).then_inc(out_made.sem, 1)

            def step(s, j):
                token_parts(s, j)
                if not first(s):
                    hidden_parts(s - 1)
                if not last(s):
                    weights(s + 1, 1 - j)
                silu_made.wait(dve, s)
                hidT_made.wait(dve, s - 1)
                dve.scalar_tensor_tensor(hid[:, :], silu[:, :], slot_w_at(s), bank(psum, 2 + j)[:, DE:], ALU.mult,
                                         ALU.mult).then_inc(hid_made.sem, 1)
                if not first(s):
                    evict(s - 1, 1 - j)

            def slot_w_at(s):
                return slot_w[:, bass.ds(s, 1)]

            weights(0, 0)
            over_steps(dve, step)
            hidden_parts(NSTEP - 1)
            evict(NSTEP - 1, 1)


def hybrid_layer(nc, io):
    with ExitStack() as ctx:
        def sb(stack, name, shape, dt=F32):
            return stack.enter_context(nc.sbuf_tensor(name, shape, dt))

        ctx.enter_context(nc.allow_non_contiguous_dma(reason="small per-row constants"))
        psum = ctx.enter_context(nc.psum_tensor("psum", [P, 8, 512], F32))
        keep = {"ident": sb(ctx, "ident", [P, P]), "semaphores": ctx}
        for name in ("gather_at", "scatter_at", "step_expert"):
            keep[name] = sb(ctx, name, [P, NSTEP], I32)
        keep["slot_w"] = sb(ctx, "slot_w", [P, NSTEP])
        keep["lg"] = sb(ctx, "lg", [P, NT, NR])
        with ExitStack() as dense:
            for name in ("hT_hi", "hT_lo"):
                keep[name] = sb(dense, name, [P, KD, NTOK], F32R)
            with ExitStack() as branches:
                for name in ("oaT_hi", "oaT_lo"):
                    keep[name] = sb(branches, name, [P, KE, NTOK], F32R)
                attention_phase(nc, io, keep, psum)
                keep["mixT"] = sb(branches, "mixT", [P, SG, NTOK])
                sgu_values_phase(nc, io, keep, psum)
                for name in ("obT_hi", "obT_lo"):
                    keep[name] = sb(branches, name, [P, KE, NTOK], F32R)
                sgu_gate_phase(nc, io, keep, psum)
                gates_phase(nc, io, keep, psum)
            keep["y"] = sb(dense, "y", [P, NT, D])
            merge_phase(nc, io, keep, psum)
            routing_phase(nc, io, keep, psum)
        experts_phase(nc, io, keep, psum)


_INS = ["cache_k_win", "cache_v_win", "norm1_g", "w_in", "q_norm_g", "k_norm_g", "attn_sinks", "ln_v_g", "ln_v_b",
        "w_spatial", "b_spatial", "w_branch_a", "w_branch_b", "w_out", "norm2_g", "w_router_group", "b_router_group",
        "w_router_expert", "b_router_expert", "w_exp_gate", "w_exp_up", "w_exp_down"]
_OUTS = {"y": (NTOK + SLOT, D), "new_k_p": (1, 1, WIN, KV, HD), "new_v_p": (1, 1, WIN, KV, HD),
         "new_k_s": (1, DEC_B, WIN, KV, HD), "new_v_s": (1, DEC_B, WIN, KV, HD),
         "new_vs": (1, DEC_B, DEC_T, SG, SW // SG)}


def kernel(**inputs):
    import numpy as np
    import concourse.bacc as bacc
    from concourse.bass_utils import run_bass_kernel_spmd

    nc = bacc.Bacc("TRN2", target_bir_lowering=False, num_devices=1)
    arrays = {"in_x": np.concatenate([np.asarray(inputs["x_prompt"]).reshape(SEQ, D),
                                      np.asarray(inputs["x_sample"]).reshape(NS, D)])}
    for name in _INS:
        arrays["in_" + name] = np.ascontiguousarray(inputs[name])
    short = {"cache_k_win": "cache_k", "cache_v_win": "cache_v"}
    io = {}
    for name, a in arrays.items():
        t = nc.dram_tensor(name, a.shape, mybir.dt.from_np(a.dtype), kind="ExternalInput").ap()
        io[short.get(name[3:], name[3:])] = t
    for name, shape in _OUTS.items():
        io[name] = nc.dram_tensor("out_" + name, shape, F32, kind="ExternalOutput").ap()
    io["h2T"] = nc.dram_tensor("h2T_rows", (P, KD, NTOK), F32, kind="Internal").ap()
    io["hn"] = nc.dram_tensor("hn_rows", (NTOK, D), F32, kind="Internal").ap()
    hybrid_layer(nc, io)
    got = run_bass_kernel_spmd(nc, [arrays], core_ids=[0]).results[0]
    y = got["out_y"]
    return (y[0:SEQ].reshape(1, SEQ, D), y[SEQ:NTOK].reshape(DEC_B, DEC_T, D), got["out_new_k_p"], got["out_new_v_p"],
            got["out_new_k_s"], got["out_new_v_s"], got["out_new_vs"])
```

```python
from contextlib import ExitStack

import concourse.bass as bass
from concourse import mybir

F32 = mybir.dt.float32
F32R = mybir.dt.float32r
I32 = mybir.dt.int32
ALU = mybir.AluOpType
ACT = mybir.ActivationFunctionType
AX_X = mybir.AxisListType.X

P = 128
D = 1024
KD = D // P
SEQ = 1024
DEC_B, DEC_T = 8, 4
NS = DEC_B * DEC_T
NTOK = SEQ + NS
PT = SEQ // P
NT = PT + 1
HEADS, KV, G, HD = 8, 2, 4, 64
AW = HEADS * HD
KVW = KV * HD
QKV = AW + 2 * KVW
WIN = 128
SG = 4
SW = 512
KE = AW // P
OFF_VS = QKV + SW
OFF_GA = QKV + 2 * SW
OFF_GB = OFF_GA + D
TC = NTOK // 3
NG, EPG = 4, 4
NE = NG * EPG
NR = NG + NE
DE = 256
EPS = 1e-6
NEG = -1e30
SLOT = 128
MOST_STEPS = (2 * NTOK + NE * (SLOT - 1)) // SLOT
MOST_STEPS += MOST_STEPS % 2
PLANNED = MOST_STEPS + 3
FAR = 1 << 20
DMA = 16


def rows(t):
    return P if t < PT else NS


def toks(t):
    return slice(t * P, t * P + rows(t))


def product(eng, out, lhs, rhs, nk, first=True, last=True):
    for k in range(nk):
        lh, ll = lhs(k)
        rh, rl = rhs(k)
        eng.matmul(out, lh, rh, start=first and k == 0, stop=False)
        eng.matmul(out, lh, rl, start=False, stop=False)
        mm = eng.matmul(out, ll, rh, start=False, stop=last and k == nk - 1)
    return mm


def bank(psum, n):
    return psum[:, n, :]


class Step:

    def __init__(self, eng, sem):
        self.eng, self.sem, self.n = eng, sem, 0

    def did(self, ins):
        self.n += 1
        ins.then_inc(self.sem, 1)
        self.eng.wait_ge(self.sem, self.n)


class Flow:

    def __init__(self, sem, start=2):
        self.sem, self.start = sem, start

    def begin(self, eng):
        eng.sem_inc(self.sem, self.start)

    def after(self, n):
        return n + (self.start + 1)

    def wait(self, eng, n):
        eng.wait_ge(self.sem, self.after(n))

    def wait_alone(self, eng, n, passed):
        eng.wait_ge(self.sem, self.after(n))
        eng.sem_inc(passed, 1)


def attention_phase(nc, io, keep, psum):
    ident, hT, oaT = keep["ident"], (keep["hT_hi"], keep["hT_lo"]), (keep["oaT_hi"], keep["oaT_lo"])
    NP = QKV // P
    w_src = io["w_in"][0].rearrange("(k p) c -> p k c", p=P)

    used = []
    with ExitStack() as ctx:
        def sb(name, shape, dt=F32):
            return ctx.enter_context(nc.sbuf_tensor(name, shape, dt))

        def sem(name):
            used.append(ctx.enter_context(nc.semaphore(name)))
            return used[-1]

        w_raw = sb("qkv_w_raw", [P, 2, KD, P])
        w_hi = sb("qkv_w_hi", [P, KD, QKV], F32R)
        w_lo = sb("qkv_w_lo", [P, KD, QKV], F32R)
        x_in = sb("x_in", [P, 2, D])
        x_norm = sb("x_norm", [P, D])
        h_raw = sb("h_raw", [P, 2, 4, P])
        z = sb("z_qkv", [P, AW + KVW])
        z_sq = w_raw[:, 1].rearrange("p k c -> p (k c)")[:, 0:AW + KVW]
        v_ring = sb("v_ring", [P, 4, KVW])
        q_norm = sb("q_norm", [P, G, KV, HD])
        k_norm = sb("k_norm", [P, KV, HD])
        qT = sb("qT", [P, G, P])
        kT = sb("kT", [P, NT, P])
        sp_sb = sb("sp_sb", [P, 1 + KV, G, 2 * WIN])
        s_sb, p_sb = sp_sb[:, 0], sp_sb[:, 1:]
        pT = sb("pT", [P, 2, G, P])
        o_sb = sb("o_sb", [P, KV, G, HD])
        mask = sb("mask", [P, 2 * WIN])
        g1 = sb("g1", [P, KD])
        qk_gain = sb("qk_gain", [P, 2])
        k_gain = sb("k_gain", [P, HD])
        sinks = sb("sinks", [P, HEADS])
        minus_half = sb("minus_half", [P, 1])
        xss = sb("xss", [P, NT])
        xrs = sb("xrs", [P, NT])
        qks = sb("qks", [P, HEADS + KV])
        qkr = sb("qkr", [P, HEADS + KV])
        top = sb("top", [P, G])
        ntop = sb("ntop", [P, 2, G])
        sink_d = sb("sink_d", [P, 2, G])
        den = sb("den", [P, 2, G])
        sink_e = sb("sink_e", [P, 2, G])
        rden = sb("rden", [P, G])
        k_out = sb("k_out", [P, KV, HD])
        s_mask_old = h_raw[:, :, :, :].rearrange("p a k c -> p (a k c)")
        s_mask_new = sb("s_mask_new", [P, NS])
        s_sinks = sb("s_sinks", [P, KV])
        s_scores = sp_sb[:, :, :, :].rearrange("p a g s -> p (a g s)")[:, 0:DEC_B * WIN + NS]
        v_cache = w_raw[:, 0]
        k_cache = x_in[:, 0, :].rearrange("p (b c) -> p b c", b=DEC_B)
        kT_cache = x_norm
        pT_s = x_in[:, 1, :].rearrange("p (b c) -> p b c", b=DEC_B)
        pT_n = pT[:, 0, 0, :]

        const_in = sem("const_in")
        w_in = [sem("w_in_even"), sem("w_in_odd")]
        x_came = [sem("x_came_even"), sem("x_came_odd")]
        act_step, dve_step, pool_step = sem("act_step"), sem("dve_step"), sem("pool_step")
        masks_made = sem("masks_made")
        ident_made = sem("ident_made")
        gains_made = sem("gains_made")
        w_hi_made, w_lo_made = sem("w_hi_made"), sem("w_lo_made")
        x_squared, x_meaned, x_rstd, x_normed = sem("x_squared"), sem("x_meaned"), sem("x_rstd"), sem("x_normed")
        xT_made = sem("xT_made")
        h_scaled, h_hi_made, h_lo_made = sem("h_scaled"), sem("h_hi_made"), sem("h_lo_made")
        q_made, kv_made = sem("q_made"), sem("kv_made")
        z_copied, z_squared, z_summed, z_rstd, qk_normed = (sem("z_copied"), sem("z_squared"), sem("z_summed"),
                                                             sem("z_rstd"), sem("qk_normed"))
        qkT_made, qkT_copied = sem("qkT_made"), sem("qkT_copied")
        s_made, s_ready, p_made = sem("s_made"), sem("s_ready"), sem("p_made")
        pT_made, pT_copied = sem("pT_made"), sem("pT_copied")
        o_made, o_copied = sem("o_made"), sem("o_copied")
        oT_made, oa_hi_made, oa_lo_made = sem("oT_made"), sem("oa_hi_made"), sem("oa_lo_made")
        k_out_made = sem("k_out_made")
        kv_stored = sem("kv_stored")
        k_out_stored = sem("k_out_stored")
        cache_in = sem("cache_in")
        cT_made, cT_copied = sem("cT_made"), sem("cT_copied")
        ss_made, ss_ready, sp_made = sem("ss_made"), sem("ss_ready"), sem("sp_made")
        spT_made, spT_copied, so_made, so_copied = sem("spT_made"), sem("spT_copied"), sem("so_made"), sem("so_copied")
        N_CONST = 7 + G * KV
        KT_AT = QKV - AW

        def scores_bank():
            return psum[:, 2:4, :].rearrange("p a (b c) -> p (a b) c", c=2 * WIN)

        def block_keys(t):
            return WIN if t == 0 else 0

        block_ctx = ctx.enter_context(ExitStack())
        block = block_ctx.enter_context(nc.Block())

        @block.sync
        def _(sp):
            def load_x(t):
                if t >= 2:
                    sp.wait_ge(x_normed, t - 1)
                sp.dma_start(x_in[0:rows(t), t % 2, :], io["x"][toks(t), :]).then_inc(x_came[t % 2], DMA)

            load_x(0)
            for c in range(NP):
                if c >= 2:
                    sp.wait_ge(w_hi_made, c - 1)
                    sp.wait_ge(w_lo_made, c - 1)
                sp.dma_start(w_raw[:, c % 2], w_src[:, :, c * P:(c + 1) * P]).then_inc(w_in[c % 2], DMA)
                if c == 1:
                    load_x(1)
            sp.wait_ge(w_hi_made, NP)
            sp.wait_ge(w_lo_made, NP)
            sp.dma_start(v_cache, io["cache_v"][0].rearrange("b s k d -> s b (k d)")).then_inc(cache_in, DMA)
            for t in range(2, NT):
                load_x(t)
            for cached, new in (("cache_k", "new_k_s"), ("cache_v", "new_v_s")):
                sp.dma_start(io[new][0, :, 0:WIN - DEC_T], io[cached][0, :, DEC_T:WIN]).then_inc(kv_stored, DMA)
            sp.wait_ge(x_normed, NT)
            sp.wait_ge(cache_in, DMA)
            sp.dma_start(k_cache, io["cache_k"][0].rearrange("b s k d -> s b (k d)")).then_inc(cache_in, DMA)
            sp.wait_ge(k_out_made, 1)
            sp.dma_start(io["new_k_p"][0, 0].rearrange("s k d -> s (k d)"),
                         k_out[:, :, :].rearrange("p k d -> p (k d)")).then_inc(k_out_stored, DMA)
            sp.wait_ge(z_copied, 2 * PT)
            sp.dma_start(io["new_v_p"][0, 0].rearrange("s k d -> s (k d)"), v_ring[:, (PT - 1) % 4, :]).then_inc(kv_stored, DMA)
            sp.wait_ge(z_copied, 2 * NT)
            for b in range(DEC_B):
                sp.dma_start(io["new_v_s"][0, b, WIN - DEC_T:WIN].rearrange("s k d -> s (k d)"),
                             v_ring[b * DEC_T:(b + 1) * DEC_T, PT % 4, :]).then_inc(kv_stored, DMA)
            sp.wait_ge(k_out_made, 2)
            for b in range(DEC_B):
                sp.dma_start(io["new_k_s"][0, b, WIN - DEC_T:WIN].rearrange("s k d -> s (k d)"),
                             k_out[b * DEC_T:(b + 1) * DEC_T, :, :].rearrange("p k d -> p (k d)")).then_inc(kv_stored, DMA)
            sp.wait_ge(kv_stored, DMA * (3 + 2 * DEC_B))

        @block.gpsimd
        def _(pool):
            step = Step(pool, pool_step)
            step.did(pool.memset(ident[:, :], 0.0))
            pool.affine_select(out=ident[:, :], in_=ident[:, :], compare_op=ALU.not_equal, fill=1.0, base=0,
                               pattern=[[-1, P]], channel_multiplier=1).then_inc(ident_made, 1)
            step.did(pool.memset(minus_half[:, :], -0.5))
            step.did(pool.memset(mask[:, :], 0.0))
            step.did(pool.affine_select(out=mask[:, :], in_=mask[:, :], compare_op=ALU.is_ge, fill=NEG, base=-1,
                                        pattern=[[1, 2 * WIN]], channel_multiplier=-1))
            pool.affine_select(out=mask[:, :], in_=mask[:, :], compare_op=ALU.is_ge, fill=NEG, base=WIN,
                               pattern=[[-1, 2 * WIN]], channel_multiplier=1).then_inc(masks_made, 1)

            def rstd(t):
                pool.wait_ge(x_meaned, t + 1)
                pool.tensor_tensor(xrs[0:rows(t), t:t + 1], xss[0:rows(t), t:t + 1], minus_half[0:rows(t), :],
                                   ALU.pow).then_inc(x_rstd, 1)

            def h_low(t):
                for half in range(2):
                    pool.wait_ge(h_hi_made, 2 * t + half + 1)
                    ks = slice(4 * half, 4 * half + 4)
                    pool.tensor_tensor(hT[1][:, ks, toks(t)], h_raw[:, half, :, 0:rows(t)],
                                       hT[0][:, ks, toks(t)].bitcast(F32), ALU.subtract).then_inc(h_lo_made, 1)

            def z_root(t):
                pool.wait_ge(z_summed, t + 1)
                pool.tensor_tensor(qkr[0:rows(t), :], qks[0:rows(t), :],
                                   minus_half[0:rows(t), 0:1].broadcast_to([rows(t), HEADS + KV]),
                                   ALU.pow).then_inc(z_rstd, 1)

            def sample_mask(g):
                q = slice(32 * g, 32 * g + 32)
                step.did(pool.memset(s_mask_old[q, :], 0.0))
                step.did(pool.memset(s_mask_new[q, :], 0.0))
                old = s_mask_old[q, :].rearrange("p (b s) -> p b s", b=DEC_B)
                new = s_mask_new[q, :].rearrange("p (b j) -> p b j", b=DEC_B)
                for part, n in ((old, WIN), (new, DEC_T)):
                    step.did(pool.affine_select(out=part, in_=part, compare_op=ALU.is_ge, fill=NEG, base=0,
                                                pattern=[[-DEC_T, DEC_B], [0, n]], channel_multiplier=1))
                    step.did(pool.affine_select(out=part, in_=part, compare_op=ALU.is_ge, fill=NEG, base=DEC_T - 1,
                                                pattern=[[DEC_T, DEC_B], [0, n]], channel_multiplier=-1))
                step.did(pool.affine_select(out=old, in_=old, compare_op=ALU.is_ge, fill=NEG, base=-1,
                                            pattern=[[DEC_T, DEC_B], [1, WIN]], channel_multiplier=-1))
                pool.affine_select(out=new, in_=new, compare_op=ALU.is_ge, fill=NEG, base=0,
                                   pattern=[[-DEC_T, DEC_B], [-1, DEC_T]], channel_multiplier=1).then_inc(masks_made, 1)
                pool.wait_ge(masks_made, 2 + g)

            rstd(0)
            h_low(0)
            rstd(1)
            h_low(1)
            z_root(0)
            rstd(2)
            for s in range(1, NT):
                if s + 1 < NT:
                    h_low(s + 1)
                z_root(s)
                if s + 2 < NT:
                    rstd(s + 2)
            pool.wait_ge(h_lo_made, 2 * NT)
            for g in range(G):
                sample_mask(g)

        @block.scalar
        def _(act):
            act.dma_start(g1[:, :], io["norm1_g"][0].rearrange("(k p) -> p k", p=P)).then_inc(const_in, DMA)
            for half in range(2):
                part = slice(HD * half, HD * half + HD)
                act.dma_start(qk_gain[part, 0:1], io["q_norm_g"].rearrange("a d -> d a")).then_inc(const_in, DMA)
                act.dma_start(qk_gain[part, 1:2], io["k_norm_g"].rearrange("a d -> d a")).then_inc(const_in, DMA)
            act.dma_start(k_gain[:, :], io["k_norm_g"][0].partition_broadcast(P)).then_inc(const_in, DMA)
            act.dma_start(sinks[:, :], io["attn_sinks"][0].partition_broadcast(P)).then_inc(const_in, DMA)
            for g in range(G):
                for kv in range(KV):
                    h = kv * G + g
                    act.dma_start(s_sinks[32 * g:32 * g + 32, kv:kv + 1],
                                  io["attn_sinks"][0, h:h + 1].partition_broadcast(32)).then_inc(const_in, DMA)

            def square(t):
                n = rows(t)
                act.wait_ge(x_came[t % 2], DMA * (t // 2 + 1))
                if t >= 1:
                    act.wait_ge(xT_made, t)
                act.activation(x_norm[0:n, :], x_in[0:n, t % 2, :], ACT.Square,
                               accum_out=xss[0:n, t:t + 1]).then_inc(x_squared, 1)

            def normalise(t):
                n = rows(t)
                act.wait_ge(x_rstd, t + 1)
                act.activation(x_norm[0:n, :], x_in[0:n, t % 2, :], ACT.Copy,
                               scale=xrs[0:n, t:t + 1]).then_inc(x_normed, 1)

            def h_high(t):
                for half in range(2):
                    act.wait_ge(h_scaled, 2 * t + half + 1)
                    act.activation(hT[0][:, 4 * half:4 * half + 4, toks(t)], h_raw[:, half, :, 0:rows(t)],
                                   ACT.Copy).then_inc(h_hi_made, 1)

            def copy_q(t):
                n = rows(t)
                act.wait_ge(q_made, t + 1)
                if t >= 1:
                    act.wait_ge(qk_normed, 2 * t)
                act.activation(z[0:n, 0:AW], bank(psum, 0)[0:n, 0:AW], ACT.Copy).then_inc(z_copied, 1)

            def copy_kv(t):
                n = rows(t)
                act.wait_ge(kv_made, t + 1)
                act.activation(z[0:n, AW:], bank(psum, 1)[0:n, 0:KVW], ACT.Copy).then_inc(act_step, 1)
                if t >= 4:
                    act.wait_ge(o_made, 2 * (t - 2))
                act.activation(v_ring[0:n, t % 4, :], bank(psum, 1)[0:n, KVW:2 * KVW], ACT.Copy).then_inc(z_copied, 1)
                act.wait_ge(act_step, t + 1)
                act.wait_ge(z_copied, 2 * t + 1)
                act.activation(z_sq[0:n, :], z[0:n, :], ACT.Square).then_inc(z_squared, 1)

            def probs(t, kv):
                u = 2 * t + kv
                k0 = block_keys(t)
                act.wait_ge(s_ready, u + 1)
                if t >= 1:
                    act.wait_ge(pT_made, u - 1)
                    act.wait_ge(o_copied, u - 1)
                for g in range(G):
                    act.activation(p_sb[:, kv, g, k0:], s_sb[:, g, k0:], ACT.Exp, bias=ntop[:, kv, g:g + 1],
                                   accum_out=den[:, kv, g:g + 1])
                act.activation(sink_e[:, kv, :], sink_d[:, kv, :], ACT.Exp).then_inc(p_made, 1)

            def oa_high(t):
                act.wait_ge(oT_made, t + 1)
                act.activation(oaT[0][:, :, toks(t)], bank(psum, 4).rearrange("p (k c) -> p k c", k=KE)[:, :, 0:rows(t)],
                               ACT.Copy).then_inc(oa_hi_made, 1)

            square(0)
            normalise(0)
            for c in range(NP):
                act.wait_ge(w_in[c % 2], DMA * (c // 2 + 1))
                act.activation(w_hi[:, :, c * P:(c + 1) * P], w_raw[:, c % 2], ACT.Copy).then_inc(w_hi_made, 1)
                if c == 1:
                    h_high(0)
            square(1)
            normalise(1)
            copy_q(0)
            h_high(1)
            copy_kv(0)
            square(2)
            for s in range(1, NT + 1):
                t, done = s - 1, s - 2
                if done >= 0:
                    probs(done, 1)
                if s + 1 < NT:
                    normalise(s + 1)
                if s < NT:
                    copy_q(s)
                if done >= 0:
                    oa_high(done)
                if t < PT:
                    probs(t, 0)
                if s + 1 < NT:
                    h_high(s + 1)
                if s < NT:
                    copy_kv(s)
                if s + 2 < NT:
                    square(s + 2)
            for kv in range(KV):
                act.wait_ge(ss_ready, kv + 1)
                act.activation(s_scores, s_scores, ACT.Exp, bias=ntop[:, kv, 0:1], accum_out=den[:, kv, 0:1])
                act.activation(sink_e[:, kv, 0:1], s_sinks[:, kv:kv + 1], ACT.Exp, bias=ntop[:, kv, 0:1]).then_inc(sp_made, 1)
            oa_high(PT)

        @block.tensor
        def _(pe):
            pe.wait_ge(ident_made, 1)

            def x_turn(t):
                n = rows(t)
                pe.wait_ge(x_normed, t + 1)
                if t >= 1:
                    pe.wait_ge(h_scaled, 2 * t)
                if t >= 3:
                    pe.wait_ge(pT_copied, 2 * (t - 2))
                for half in range(2):
                    for k in range(4):
                        mm = pe.transpose(bank(psum, 6 + half)[:, k * P:k * P + n],
                                          x_norm[0:n, (4 * half + k) * P:(4 * half + k + 1) * P], ident[0:n, 0:n])
                mm.then_inc(xT_made, 1)

            def project_q(t, half):
                n = rows(t)
                pe.wait_ge(h_hi_made, 2 * t + half + 1)
                pe.wait_ge(h_lo_made, 2 * t + half + 1)
                pe.wait_ge(w_hi_made, AW // P)
                pe.wait_ge(w_lo_made, AW // P)
                if t >= 1:
                    pe.wait_ge(z_copied, 2 * t - 1)
                h = half * (KD // 2)
                mm = product(pe, bank(psum, 0)[0:n, 0:AW], lambda k: (hT[0][:, h + k, toks(t)], hT[1][:, h + k, toks(t)]),
                             lambda k: (w_hi[:, h + k, 0:AW], w_lo[:, h + k, 0:AW]), KD // 2, first=half == 0, last=half == 1)
                if half == 1:
                    mm.then_inc(q_made, 1)

            def project_kv(t):
                n = rows(t)
                pe.wait_ge(w_hi_made, NP)
                pe.wait_ge(w_lo_made, NP)
                if t >= 1:
                    pe.wait_ge(z_copied, 2 * t)
                    pe.wait_ge(qkT_copied, 2 * t)
                product(pe, bank(psum, 1)[0:n, 0:QKV - AW], lambda k: (hT[0][:, k, toks(t)], hT[1][:, k, toks(t)]),
                        lambda k: (w_hi[:, k, AW:], w_lo[:, k, AW:]), KD).then_inc(kv_made, 1)

            def qk_turn(t):
                n = rows(t)
                pe.wait_ge(qk_normed, 2 * t + 2)
                if t >= 2:
                    pe.wait_ge(oa_lo_made, t - 1)
                for g in range(G):
                    pe.transpose(bank(psum, 4)[:, g * P:g * P + n], q_norm[0:n, g, :, :].rearrange("p k d -> p (k d)"),
                                 ident[0:n, 0:n])
                pe.transpose(bank(psum, 1)[:, KT_AT:KT_AT + n], k_norm[0:n, :, :].rearrange("p k d -> p (k d)"),
                             ident[0:n, 0:n]).then_inc(qkT_made, 1)

            def scores(t, kv):
                u = 2 * t + kv
                k0 = block_keys(t)
                head = slice(HD * kv, HD * kv + HD)
                pe.wait_ge(qkT_copied, 2 * t + 2)
                if u >= 1:
                    pe.wait_ge(s_ready, u)
                keys = kT[:, :, :].rearrange("p a b -> p (a b)")[head, (t - 1) * P + k0:(t + 1) * P]
                for g in range(G):
                    mm = pe.matmul(scores_bank()[:, g, k0:], qT[head, g, :], keys, start=True, stop=True)
                mm.then_inc(s_made, 1)

            def probs_turn(t, kv):
                u = 2 * t + kv
                pe.wait_ge(p_made, u + 1)
                if u >= 1:
                    pe.wait_ge(pT_copied, u)
                if kv == 0:
                    pe.wait_ge(h_scaled, 2 * min(t + 3, NT))
                for half in range(block_keys(t) // WIN, 2):
                    for g in range(G):
                        mm = pe.transpose(bank(psum, 6 + half)[:, g * P:(g + 1) * P],
                                          p_sb[:, kv, g, half * WIN:(half + 1) * WIN], ident[:, :])
                mm.then_inc(pT_made, 1)

            def values(t, kv):
                u = 2 * t + kv
                pe.wait_ge(pT_copied, u + 1)
                pe.wait_ge(z_copied, 2 * t + 2)
                if u >= 1:
                    pe.wait_ge(o_copied, u)
                first = block_keys(t) // WIN
                for g in range(G):
                    for half in range(first, 2):
                        mm = pe.matmul(bank(psum, 5)[:, g * HD:(g + 1) * HD], pT[:, half, g, :],
                                       v_ring[:, (t - 1 + half) % 4, kv * HD:(kv + 1) * HD],
                                       start=half == first, stop=half == 1)
                mm.then_inc(o_made, 1)

            def o_turn(t):
                n = rows(t)
                pe.wait_ge(o_copied, 2 * t + 2)
                pe.wait_ge(qkT_copied, 2 * t + 4)
                flat = o_sb[:, :, :, :].rearrange("p k g d -> p (k g d)")
                for c in range(KE):
                    mm = pe.transpose(bank(psum, 4)[:, c * P:c * P + n], flat[0:n, c * P:(c + 1) * P], ident[0:n, 0:n])
                mm.then_inc(oT_made, 1)

            x_turn(0)
            for half in range(2):
                project_q(0, half)
            x_turn(1)
            project_kv(0)
            for s in range(1, NT + 1):
                t, done = s - 1, s - 2
                if done >= 0:
                    probs_turn(done, 0)
                if s < NT:
                    project_q(s, 0)
                if done >= 0:
                    values(done, 0)
                    probs_turn(done, 1)
                if s < NT:
                    project_q(s, 1)
                qk_turn(t)
                if done >= 0:
                    values(done, 1)
                if t < PT:
                    scores(t, 0)
                if done >= 0:
                    o_turn(done)
                if s + 1 < NT:
                    x_turn(s + 1)
                if s < NT:
                    project_kv(s)
                if t < PT:
                    scores(t, 1)
            pe.wait_ge(cache_in, 2 * DMA)
            pe.wait_ge(pT_copied, 2 * PT)
            for b in range(DEC_B):
                mm = pe.transpose(bank(psum, 6 + b // 4)[:, (b % 4) * P:(b % 4 + 1) * P], k_cache[:, b, :], ident[:, :])
            mm.then_inc(cT_made, 1)
            pe.wait_ge(qkT_copied, 2 * NT)
            pe.wait_ge(cT_copied, 2)
            for kv in range(KV):
                head = slice(HD * kv, HD * kv + HD)
                q_all = qT[head, 0, :]
                if kv == 1:
                    pe.wait_ge(ss_ready, 1)
                for c in range(2):
                    pe.matmul(bank(psum, 2 + c), q_all, kT_cache[head, c * 512:(c + 1) * 512], start=True, stop=True)
                pe.matmul(bank(psum, 1)[:, 0:NS], q_all, kT[head, PT, 0:NS], start=True, stop=True).then_inc(ss_made, 1)
                pe.wait_ge(sp_made, kv + 1)
                if kv == 1:
                    pe.wait_ge(spT_copied, 1)
                for b in range(DEC_B):
                    pe.transpose(bank(psum, 6 + b // 4)[:, (b % 4) * P:(b % 4 + 1) * P],
                                 s_scores[:, b * WIN:(b + 1) * WIN], ident[:, :])
                pe.transpose(bank(psum, 0)[0:NS, 0:P], s_scores[:, DEC_B * WIN:], ident[:, :]).then_inc(spT_made, 1)
                pe.wait_ge(spT_copied, kv + 1)
                if kv == 1:
                    pe.wait_ge(so_copied, 1)
                for b in range(DEC_B):
                    pe.matmul(bank(psum, 5)[:, 0:HD], pT_s[:, b, :], v_cache[:, b, kv * HD:(kv + 1) * HD],
                              start=b == 0, stop=False)
                pe.matmul(bank(psum, 5)[:, 0:HD], pT_n[0:NS, :], v_ring[0:NS, PT % 4, kv * HD:(kv + 1) * HD],
                          start=False, stop=True).then_inc(so_made, 1)
            pe.wait_ge(so_copied, 2)
            flat = o_sb[:, :, :, :].rearrange("p k g d -> p (k g d)")
            for c in range(KE):
                mm = pe.transpose(bank(psum, 4)[:, c * P:c * P + NS], flat[0:NS, c * P:(c + 1) * P], ident[0:NS, 0:NS])
            mm.then_inc(oT_made, 1)

        @block.vector
        def _(dve):
            step = Step(dve, dve_step)

            def mean_square(t):
                n = rows(t)
                dve.wait_ge(x_squared, t + 1)
                dve.tensor_scalar(xss[0:n, t:t + 1], xss[0:n, t:t + 1], 1.0 / D, EPS, ALU.mult,
                                  ALU.add).then_inc(x_meaned, 1)

            def h_scale(t):
                n = rows(t)
                dve.wait_ge(xT_made, t + 1)
                if t >= 1:
                    dve.wait_ge(h_lo_made, 2 * t)
                for half in range(2):
                    ks = slice(4 * half, 4 * half + 4)
                    dve.tensor_tensor(h_raw[:, half, :, 0:n],
                                      bank(psum, 6 + half).rearrange("p (k c) -> p k c", k=4)[:, :, 0:n],
                                      g1[:, ks].unsqueeze(2).broadcast_to([P, 4, n]), ALU.mult).then_inc(h_scaled, 1)

            def qk_squares(t):
                n = rows(t)
                dve.wait_ge(z_squared, t + 1)
                step.did(dve.tensor_reduce(qks[0:n, :], z_sq[0:n, :].rearrange("p (h d) -> p h d", d=HD), AX_X, ALU.add))
                dve.tensor_scalar(qks[0:n, :], qks[0:n, :], 1.0 / HD, EPS, ALU.mult, ALU.add).then_inc(z_summed, 1)

            def qk_scale(t):
                n = rows(t)
                zz = z[0:n, :].rearrange("p (h d) -> p h d", d=HD)
                dve.wait_ge(z_rstd, t + 1)
                if t >= 1:
                    dve.wait_ge(qkT_made, t)
                dve.tensor_tensor(q_norm[0:n, :, :, :].rearrange("p g k d -> p k g d"),
                                  zz[:, 0:HEADS, :].rearrange("p (k g) d -> p k g d", k=KV),
                                  qkr[0:n, 0:HEADS].rearrange("p (k g) -> p k g", k=KV).unsqueeze(3)
                                  .broadcast_to([n, KV, G, HD]), ALU.mult).then_inc(qk_normed, 1)
                dve.tensor_tensor(k_norm[0:n, :, :], zz[:, HEADS:, :],
                                  qkr[0:n, HEADS:].unsqueeze(2).broadcast_to([n, KV, HD]), ALU.mult).then_inc(qk_normed, 1)
                if t == PT:
                    dve.wait_ge(k_out_stored, DMA)
                if t >= PT - 1:
                    dve.wait_ge(qk_normed, 2 * t + 2)
                    dve.tensor_tensor(k_out[0:n, :, :], k_norm[0:n, :, :],
                                      k_gain[0:n, :].unsqueeze(1).broadcast_to([n, KV, HD]), ALU.mult).then_inc(k_out_made, 1)

            def qk_copy(t):
                n = rows(t)
                dve.wait_ge(qkT_made, t + 1)
                if t >= 1:
                    dve.wait_ge(s_made, 2 * t)
                if t < PT:
                    out = qT[:, :, 0:n]
                else:
                    out = qT[:, 0, :].rearrange("p (g n) -> p g n", g=G)
                dve.tensor_scalar(out, bank(psum, 4).rearrange("p (g n) -> p g n", g=G)[:, :, 0:n], qk_gain[:, 0:1],
                                  HD ** -0.5, ALU.mult, ALU.mult).then_inc(qkT_copied, 1)
                dve.tensor_scalar(kT[:, t, 0:n], bank(psum, 1)[:, KT_AT:KT_AT + n], qk_gain[:, 1:2], None,
                                  ALU.mult).then_inc(qkT_copied, 1)

            def mask_scores(t, kv):
                u = 2 * t + kv
                k0 = block_keys(t)
                dve.wait_ge(s_made, u + 1)
                if u >= 1:
                    dve.wait_ge(p_made, u)
                for g in range(G):
                    ins = dve.tensor_tensor_reduce(s_sb[:, g, k0:], scores_bank()[:, g, k0:], mask[:, k0:], 1.0, NEG,
                                                   ALU.add, ALU.max, top[:, g:g + 1])
                step.did(ins)
                sink = sinks[:, kv * G:(kv + 1) * G]
                step.did(dve.tensor_tensor(top[:, :], top[:, :], sink, ALU.max))
                step.did(dve.tensor_scalar(ntop[:, kv, :], top[:, :], -1.0, None, ALU.mult))
                dve.tensor_tensor(sink_d[:, kv, :], sink, ntop[:, kv, :], ALU.add).then_inc(s_ready, 1)

            def pT_copy(t, kv):
                u = 2 * t + kv
                dve.wait_ge(pT_made, u + 1)
                if u >= 1:
                    dve.wait_ge(o_made, u)
                first = block_keys(t) // WIN
                for half in range(first, 2):
                    ins = dve.tensor_copy(pT[:, half, :, :].rearrange("p g c -> p (g c)"), bank(psum, 6 + half))
                ins.then_inc(pT_copied, 1)

            def o_scale(t, kv):
                u = 2 * t + kv
                if u >= 1:
                    dve.wait_ge(o_copied, u)
                step.did(dve.tensor_tensor(rden[:, :], den[:, kv, :], sink_e[:, kv, :], ALU.add))
                step.did(dve.reciprocal(rden[:, :], rden[:, :]))
                dve.wait_ge(o_made, u + 1)
                if t >= 1:
                    dve.wait_ge(oT_made, t)
                dve.tensor_tensor(o_sb[:, kv, :, :], bank(psum, 5)[:, 0:G * HD].rearrange("p (g d) -> p g d", g=G),
                                  rden[:, :].unsqueeze(2).broadcast_to([P, G, HD]), ALU.mult).then_inc(o_copied, 1)

            def oa_low(t):
                dve.wait_ge(oa_hi_made, t + 1)
                dve.tensor_tensor(oaT[1][:, :, toks(t)],
                                  bank(psum, 4).rearrange("p (k c) -> p k c", k=KE)[:, :, 0:rows(t)],
                                  oaT[0][:, :, toks(t)].bitcast(F32), ALU.subtract).then_inc(oa_lo_made, 1)

            mean_square(0)
            dve.wait_ge(const_in, DMA * N_CONST)
            h_scale(0)
            for c in range(NP):
                dve.wait_ge(w_hi_made, c + 1)
                dve.tensor_tensor(w_lo[:, :, c * P:(c + 1) * P], w_raw[:, c % 2],
                                  w_hi[:, :, c * P:(c + 1) * P].bitcast(F32), ALU.subtract).then_inc(w_lo_made, 1)
            mean_square(1)
            dve.wait_ge(masks_made, 1)
            h_scale(1)
            qk_squares(0)
            mean_square(2)
            for s in range(1, NT + 1):
                t, done = s - 1, s - 2
                if done >= 0:
                    pT_copy(done, 0)
                    o_scale(done, 0)
                    pT_copy(done, 1)
                qk_scale(t)
                qk_copy(t)
                if done >= 0:
                    o_scale(done, 1)
                if t < PT:
                    mask_scores(t, 0)
                if done >= 0:
                    oa_low(done)
                if s + 1 < NT:
                    h_scale(s + 1)
                if t < PT:
                    mask_scores(t, 1)
                if s < NT:
                    qk_squares(s)
                if s + 2 < NT:
                    mean_square(s + 2)
            dve.wait_ge(cT_made, 1)
            for half in range(2):
                dve.tensor_copy(kT_cache[:, half * 512:(half + 1) * 512], bank(psum, 6 + half)).then_inc(cT_copied, 1)
            dve.wait_ge(masks_made, 1 + G)
            for kv in range(KV):
                dve.wait_ge(ss_made, kv + 1)
                if kv == 1:
                    dve.wait_ge(spT_made, 1)
                for c in range(2):
                    part = slice(c * 512, (c + 1) * 512)
                    dve.tensor_tensor(s_scores[:, part], bank(psum, 2 + c), s_mask_old[:, part], ALU.add)
                step.did(dve.tensor_tensor(s_scores[:, DEC_B * WIN:], bank(psum, 1)[:, 0:NS], s_mask_new[:, :],
                                           ALU.add))
                step.did(dve.tensor_reduce(top[:, 0:1], s_scores, AX_X, ALU.max))
                step.did(dve.tensor_tensor(top[:, 0:1], top[:, 0:1], s_sinks[:, kv:kv + 1], ALU.max))
                dve.tensor_scalar(ntop[:, kv, 0:1], top[:, 0:1], -1.0, None, ALU.mult).then_inc(ss_ready, 1)
                dve.wait_ge(sp_made, kv + 1)
                if kv == 0:
                    dve.wait_ge(o_copied, 2 * PT)
                else:
                    dve.wait_ge(so_copied, 1)
                step.did(dve.tensor_tensor(rden[:, 0:1], den[:, kv, 0:1], sink_e[:, kv, 0:1], ALU.add))
                step.did(dve.reciprocal(rden[:, 0:1], rden[:, 0:1]))
                dve.wait_ge(spT_made, kv + 1)
                if kv == 1:
                    dve.wait_ge(so_made, 1)
                for half in range(2):
                    dve.tensor_copy(pT_s[:, 4 * half:4 * half + 4, :].rearrange("p b c -> p (b c)"), bank(psum, 6 + half))
                dve.tensor_copy(pT_n[0:NS, :], bank(psum, 0)[0:NS, 0:P]).then_inc(spT_copied, 1)
                dve.wait_ge(so_made, kv + 1)
                for g in range(G):
                    q = slice(32 * g, 32 * g + 32)
                    ins = dve.tensor_scalar(o_sb[0:NS, kv, g, :], bank(psum, 5)[q, 0:HD], rden[q, 0:1], None, ALU.mult)
                ins.then_inc(so_copied, 1)
            oa_low(PT)

        block_ctx.close()
        with nc.Block() as clearing:
            @clearing.gpsimd
            def _(pool):
                for s in used:
                    pool.sem_clear(s)


def sgu_values_phase(nc, io, keep, psum):
    ident, hT, mixT = keep["ident"], (keep["hT_hi"], keep["hT_lo"]), keep["mixT"]
    NP = SW // P
    w_src = io["w_in"][0].rearrange("(k p) c -> p k c", p=P)

    with ExitStack() as ctx:
        def sb(name, shape, dt=F32):
            return ctx.enter_context(nc.sbuf_tensor(name, shape, dt))

        def sem(name):
            return keep["semaphores"].enter_context(nc.semaphore("v_" + name))

        w_raw = sb("vs_w_raw", [P, 2, KD, P])
        w_hi = sb("vs_w_hi", [P, KD, SW], F32R)
        w_lo = sb("vs_w_lo", [P, KD, SW], F32R)
        act_v = sb("act_v", [P, 2, SW])
        vs = sb("vs", [P, 2, SW])
        stats = sb("stats", [P, 6])
        mean_var = sb("mean_var", [P, 2])
        rstd = sb("rstd", [P, 1])
        minus_half = sb("v_minus_half", [P, 1])
        ln_g = sb("ln_g", [P, SW])
        ln_b = sb("ln_b", [P, SW])
        w_mix = sb("w_mix", [P, SG, P])
        w_mixT = sb("w_mixT", [P, SG, P])
        w_mixT_s = sb("w_mixT_s", [NS, SG, NS])
        b_mix = sb("b_mix", [P, SG, P])
        b_mix_s = sb("b_mix_s", [P, SG, NS])

        const_in, zeroed, blocks_in = sem("const_in"), sem("zeroed"), sem("blocks_in")
        w_in = [sem("w_in_even"), sem("w_in_odd")]
        w_hi_made, w_lo_made = sem("w_hi_made"), sem("w_lo_made")
        v_made, v_gelu, v_stats, v_rstd, v_norm, v_gain, vs_made = (
            sem("made"), sem("gelu"), sem("stats"), sem("rstd"), sem("norm"), sem("gain"), sem("vs_made"))
        dve_step, mixed, mix_added = sem("dve_step"), sem("mixed"), sem("mix_added")
        mixT_turned, mixT_copied, mix_ready = sem("mixT_turned"), sem("mixT_copied"), sem("mix_ready")
        vs_stored = sem("vs_stored")
        N_CONST = 4 + DEC_B
        block = ctx.enter_context(nc.Block())

        @block.sync
        def _(sp):
            for c in range(NP):
                if c >= 2:
                    sp.wait_ge(w_hi_made, c - 1)
                    sp.wait_ge(w_lo_made, c - 1)
                c0 = OFF_VS + c * P
                sp.dma_start(w_raw[:, c % 2], w_src[:, :, c0:c0 + P]).then_inc(w_in[c % 2], DMA)
            sp.wait_ge(zeroed, 1)
            for b in range(DEC_B):
                r = slice(b * DEC_T, (b + 1) * DEC_T)
                for h in range(SG):
                    sp.dma_start(w_mixT_s[r, h, r],
                                 io["w_spatial"][0, h, 0:DEC_T, 0:DEC_T].rearrange("i j -> j i")).then_inc(blocks_in, DMA)
            sp.wait_ge(vs_made, NT)
            sp.dma_start(io["new_vs"].rearrange("a b t g c -> (a b t) (g c)"), vs[0:NS, PT % 2, :]).then_inc(vs_stored, DMA)
            sp.wait_ge(vs_stored, DMA)

        @block.gpsimd
        def _(pool):
            pool.memset(w_mixT_s[:, :, :], 0.0).then_inc(zeroed, 1)
            pool.memset(minus_half[:, :], -0.5).then_inc(zeroed, 1)
            pool.wait_ge(mixT_copied, 1)
            pool.affine_select(out=w_mixT[:, :, :], in_=w_mixT[:, :, :], compare_op=ALU.is_ge, fill=0.0, base=0,
                               pattern=[[0, SG], [1, P]], channel_multiplier=-1).then_inc(mix_ready, 1)
            pool.wait_ge(blocks_in, DMA * DEC_B * SG)
            pool.affine_select(out=w_mixT_s[:, :, :], in_=w_mixT_s[:, :, :], compare_op=ALU.is_ge, fill=0.0, base=0,
                               pattern=[[0, SG], [1, NS]], channel_multiplier=-1).then_inc(mix_ready, 1)
            pool.wait_ge(zeroed, 2)
            pool.wait_ge(const_in, DMA * N_CONST)
            for t in range(NT):
                n = rows(t)
                pool.wait_ge(v_stats, t + 1)
                pool.tensor_tensor(rstd[0:n, :], mean_var[0:n, 1:2], minus_half[0:n, :], ALU.pow).then_inc(v_rstd, 1)
                pool.wait_ge(v_norm, t + 1)
                pool.tensor_tensor(vs[0:n, t % 2, :], act_v[0:n, t % 2, :], ln_g[0:n, :], ALU.mult).then_inc(v_gain, 1)
                pool.wait_ge(v_gain, t + 1)
                pool.tensor_tensor(vs[0:n, t % 2, :], vs[0:n, t % 2, :], ln_b[0:n, :], ALU.add).then_inc(vs_made, 1)

        @block.scalar
        def _(act):
            act.dma_start(w_mix[:, :, :], io["w_spatial"][0].rearrange("h i j -> i h j")).then_inc(const_in, DMA)
            act.dma_start(ln_g[:, :], io["ln_v_g"][0].partition_broadcast(P)).then_inc(const_in, DMA)
            act.dma_start(ln_b[:, :], io["ln_v_b"][0].partition_broadcast(P)).then_inc(const_in, DMA)
            act.dma_start(b_mix[:, :, :], io["b_spatial"][0].partition_broadcast(P)).then_inc(const_in, DMA)
            for b in range(DEC_B):
                act.dma_start(b_mix_s[:, :, b * DEC_T:(b + 1) * DEC_T],
                              io["b_spatial"][0, :, 0:DEC_T].partition_broadcast(P)).then_inc(const_in, DMA)
            for c in range(NP):
                act.wait_ge(w_in[c % 2], DMA * (c // 2 + 1))
                act.activation(w_hi[:, :, c * P:(c + 1) * P], w_raw[:, c % 2], ACT.Copy).then_inc(w_hi_made, 1)
            for t in range(NT):
                n = rows(t)
                act.wait_ge(v_made, t + 1)
                if t >= 2:
                    act.wait_ge(v_gain, t - 1)
                act.activation(act_v[0:n, t % 2, :], bank(psum, t % 2)[0:n, :], ACT.Gelu_apprx_tanh).then_inc(v_gelu, 1)

        @block.tensor
        def _(pe):
            pe.wait_ge(const_in, DMA * N_CONST)
            for h in range(SG):
                mm = pe.transpose(bank(psum, 4)[:, h * P:(h + 1) * P], w_mix[:, h, :], ident[:, :])
            mm.then_inc(mixT_turned, 1)
            pe.wait_ge(w_hi_made, NP)
            pe.wait_ge(w_lo_made, NP)

            def mix(t):
                n = rows(t)
                pe.wait_ge(vs_made, t + 1)
                pe.wait_ge(mix_ready, 1 if t < PT else 2)
                if t >= 2:
                    pe.wait_ge(mix_added, t - 1)
                w = w_mixT if t < PT else w_mixT_s
                for h in range(SG):
                    mm = pe.matmul(bank(psum, 2 + t % 2)[:, h * P:h * P + n], vs[0:n, t % 2, h * P:(h + 1) * P],
                                   w[0:n, h, 0:n], start=True, stop=True)
                mm.then_inc(mixed, 1)

            for t in range(NT):
                if t >= 2:
                    pe.wait_ge(v_gelu, t - 1)
                product(pe, bank(psum, t % 2)[0:rows(t), :], lambda k: (hT[0][:, k, toks(t)], hT[1][:, k, toks(t)]),
                        lambda k: (w_hi[:, k, :], w_lo[:, k, :]), KD).then_inc(v_made, 1)
                if t >= 1:
                    mix(t - 1)
            mix(PT)

        @block.vector
        def _(dve):
            step = Step(dve, dve_step)
            for c in range(NP):
                dve.wait_ge(w_hi_made, c + 1)
                dve.tensor_tensor(w_lo[:, :, c * P:(c + 1) * P], w_raw[:, c % 2],
                                  w_hi[:, :, c * P:(c + 1) * P].bitcast(F32), ALU.subtract).then_inc(w_lo_made, 1)
            dve.wait_ge(mixT_turned, 1)
            dve.tensor_copy(w_mixT[:, :, :].rearrange("p h i -> p (h i)"), bank(psum, 4)).then_inc(mixT_copied, 1)
            dve.wait_ge(const_in, DMA * N_CONST)

            def add_bias(t):
                n = rows(t)
                dve.wait_ge(mixed, t + 1)
                dve.tensor_tensor(mixT[:, :, toks(t)], bank(psum, 2 + t % 2).rearrange("p (h i) -> p h i", h=SG)[:, :, 0:n],
                                  (b_mix if t < PT else b_mix_s)[:, :, 0:n], ALU.add).then_inc(mix_added, 1)

            for t in range(NT):
                n = rows(t)
                a = act_v[0:n, t % 2, :]
                dve.wait_ge(v_gelu, t + 1)
                step.did(dve.bn_stats(stats[0:n, :], a))
                if t >= 1:
                    dve.wait_ge(v_norm, t)
                step.did(dve.bn_aggr(mean_var[0:n, :], stats[0:n, :]))
                dve.tensor_scalar(mean_var[0:n, 1:2], mean_var[0:n, 1:2], EPS, None, ALU.add).then_inc(v_stats, 1)
                dve.wait_ge(v_rstd, t + 1)
                if t >= 2:
                    dve.wait_ge(mixed, t - 1)
                dve.tensor_scalar(a, a, mean_var[0:n, 0:1], rstd[0:n, 0:1], ALU.subtract, ALU.mult).then_inc(v_norm, 1)
                if t >= 1:
                    add_bias(t - 1)
            add_bias(PT)


def sgu_gate_phase(nc, io, keep, psum):
    hT, mixT, obT = (keep["hT_hi"], keep["hT_lo"]), keep["mixT"], (keep["obT_hi"], keep["obT_lo"])
    w_src = io["w_in"][0].rearrange("(k p) c -> p k c", p=P)

    with ExitStack() as ctx:
        def sb(name, shape, dt=F32):
            return ctx.enter_context(nc.sbuf_tensor(name, shape, dt))

        def sem(name):
            return keep["semaphores"].enter_context(nc.semaphore("u_" + name))

        w_raw = sb("u_w_raw", [P, 2, KD, P])
        w_hi = sb("u_w_hi", [P, 2, KD, P], F32R)
        w_lo = sb("u_w_lo", [P, 2, KD, P], F32R)
        u_act = sb("u_act", [P, 2, TC])
        ob = sb("ob", [P, 2, TC])
        w_in = [sem("w_in_even"), sem("w_in_odd")]
        w_hi_made, w_lo_made = Flow(sem("w_hi_made")), Flow(sem("w_lo_made"))
        u_made, u_gelu, ob_made = Flow(sem("made"), 6), Flow(sem("gelu")), Flow(sem("ob_made"))
        hi_made, lo_made = Flow(sem("hi_made")), Flow(sem("lo_made"))
        block = ctx.enter_context(nc.Block())

        @block.sync
        def _(sp):
            with sp.Fori(0, KE // 2) as i:
                for j in range(2):
                    w_hi_made.wait(sp, 2 * i + (j - 2))
                    w_lo_made.wait(sp, 2 * i + (j - 2))
                    sp.dma_start(w_raw[:, j], w_src[:, :, bass.ds(i * 2 * P + (QKV + j * P), P)]).then_inc(w_in[j], DMA)

        @block.gpsimd
        def _(pool):
            lo_made.begin(pool)
            with pool.Fori(0, KE // 2) as i:
                for j in range(2):
                    for c in range(3):
                        m = 3 * j + c
                        hi_made.wait(pool, 6 * i + m)
                        part = slice(c * TC, (c + 1) * TC)
                        pool.tensor_tensor(obT[1][:, bass.ds(2 * i + j, 1), part], ob[:, m % 2, :].unsqueeze(1),
                                           obT[0][:, bass.ds(2 * i + j, 1), part].bitcast(F32),
                                           ALU.subtract).then_inc(lo_made.sem, 1)

        @block.scalar
        def _(act):
            w_hi_made.begin(act)
            u_gelu.begin(act)
            hi_made.begin(act)

            with act.Fori(0, KE // 2) as i:
                for j in range(2):
                    act.wait_ge(w_in[j], DMA * i + DMA)
                    u_made.wait(act, 6 * i + (3 * j - 4))
                    act.activation(w_hi[:, j], w_raw[:, j], ACT.Copy).then_inc(w_hi_made.sem, 1)
                for m in range(6):
                    j, c = m // 3, m % 3
                    u_made.wait(act, 6 * i + m)
                    ob_made.wait(act, 6 * i + (m - 2))
                    act.activation(u_act[:, m % 2, :], bank(psum, m % 2)[:, 0:TC], ACT.Gelu_apprx_tanh).then_inc(u_gelu.sem, 1)
                    ob_made.wait(act, 6 * i + m)
                    act.activation(obT[0][:, bass.ds(2 * i + j, 1), c * TC:(c + 1) * TC], ob[:, m % 2, :].unsqueeze(1),
                                   ACT.Copy).then_inc(hi_made.sem, 1)

        @block.tensor
        def _(pe):
            u_made.begin(pe)
            with pe.Fori(0, KE // 2) as i:
                for j in range(2):
                    w_hi_made.wait(pe, 2 * i + j)
                    w_lo_made.wait(pe, 2 * i + j)
                    for c in range(3):
                        m = 3 * j + c
                        u_gelu.wait(pe, 6 * i + (m - 2))
                        part = slice(c * TC, (c + 1) * TC)
                        product(pe, bank(psum, m % 2)[:, 0:TC], lambda k: (w_hi[:, j, k, :], w_lo[:, j, k, :]),
                                lambda k: (hT[0][:, k, part], hT[1][:, k, part]), KD).then_inc(u_made.sem, 1)

        @block.vector
        def _(dve):
            w_lo_made.begin(dve)
            ob_made.begin(dve)
            with dve.Fori(0, KE // 2) as i:
                for j in range(2):
                    w_hi_made.wait(dve, 2 * i + j)
                    u_made.wait(dve, 6 * i + (3 * j - 4))
                    dve.tensor_tensor(w_lo[:, j], w_raw[:, j], w_hi[:, j].bitcast(F32), ALU.subtract).then_inc(w_lo_made.sem, 1)
                for m in range(6):
                    j, c = m // 3, m % 3
                    u_gelu.wait(dve, 6 * i + m)
                    lo_made.wait(dve, 6 * i + (m - 2))
                    dve.tensor_tensor(ob[:, m % 2, :].unsqueeze(1), u_act[:, m % 2, :].unsqueeze(1),
                                      mixT[:, bass.ds(2 * i + j, 1), c * TC:(c + 1) * TC], ALU.mult).then_inc(ob_made.sem, 1)


def gates_phase(nc, io, keep, psum):
    hT = (keep["hT_hi"], keep["hT_lo"])
    branch = ((keep["oaT_hi"], keep["oaT_lo"]), (keep["obT_hi"], keep["obT_lo"]))
    KB = KD + KE
    w_gate = io["w_in"][0].rearrange("(k p) c -> p k c", p=P)
    w_branch = [io[n][0].rearrange("(k p) c -> p k c", p=P) for n in ("w_branch_a", "w_branch_b")]

    with ExitStack() as ctx:
        def sb(name, shape, dt=F32):
            return ctx.enter_context(nc.sbuf_tensor(name, shape, dt))

        def sem(name):
            return keep["semaphores"].enter_context(nc.semaphore("g_" + name))

        w_raw = sb("g_w_raw", [P, 2, KB, P])
        w_hi = sb("g_w_hi", [P, 2, KB, P], F32R)
        w_lo = sb("g_w_lo", [P, 2, KB, P], F32R)
        gate = sb("gate", [P, 2, TC])
        part_a = sb("part_a", [P, 3, TC])
        part_b = sb("part_b", [P, 3, TC])
        h2 = sb("h2", [P, 3, TC])
        w_in = [sem("w_in_a"), sem("w_in_b")]
        h2_stored = [sem(f"h2_stored_{c}") for c in range(3)]
        w_hi_made, w_lo_made = Flow(sem("w_hi_made")), Flow(sem("w_lo_made"))
        made, gated, multiplied, h2_made = (Flow(sem("made"), 6), Flow(sem("gated"), 4), Flow(sem("multiplied"), 4),
                                            Flow(sem("h2_made"), 3))
        block = ctx.enter_context(nc.Block())

        def pair(ab, c):
            return 2 * ((3 * ab + c) % 4)

        def over_pieces(eng, step):
            step(0, 0, 0)
            with eng.Fori(0, KD - 1) as i:
                step(2 * i + 1, i, 1)
                step(2 * i + 2, i + 1, 0)
            step(2 * KD - 1, KD - 1, 1)

        def is_last(q):
            return isinstance(q, int) and q == 2 * KD - 1

        @block.sync
        def _(sp):
            for c in range(3):
                sp.sem_inc(h2_stored[c], DMA)

            def store(d):
                for c in range(3):
                    h2_made.wait(sp, 3 * d + c)
                    sp.dma_start(io["h2T"][:, bass.ds(d, 1), c * TC:(c + 1) * TC],
                                 h2[:, c, :].unsqueeze(1)).then_inc(h2_stored[c], DMA)

            def load(q, d, ab):
                w_hi_made.wait(sp, q - 2)
                w_lo_made.wait(sp, q - 2)
                sp.dma_start(w_raw[:, ab, 0:KD], w_gate[:, :, bass.ds(d * P + (OFF_GA, OFF_GB)[ab], P)]).then_inc(w_in[ab], DMA)
                sp.dma_start(w_raw[:, ab, KD:], w_branch[ab][:, :, bass.ds(d * P, P)]).then_inc(w_in[ab], DMA)
                if ab == 0 and not (isinstance(q, int) and q == 0):
                    store(d - 1)

            over_pieces(sp, load)
            store(KD - 1)
            for c in range(3):
                sp.wait_ge(h2_stored[c], DMA * (KD + 1))

        @block.scalar
        def _(act):
            w_hi_made.begin(act)
            gated.begin(act)

            def weights(q, d, ab):
                act.wait_ge(w_in[ab], 2 * DMA * d + 2 * DMA)
                made.wait(act, 3 * q - 4)
                act.activation(w_hi[:, ab], w_raw[:, ab], ACT.Copy).then_inc(w_hi_made.sem, 1)

            def step(q, d, ab):
                if not is_last(q):
                    weights(q + 1, d + ab, 1 - ab)
                for c in range(3):
                    u = 3 * q + c
                    made.wait(act, u)
                    multiplied.wait(act, u - 2)
                    act.activation(gate[:, (ab + c) % 2, :], bank(psum, pair(ab, c))[:, 0:TC], ACT.Sigmoid).then_inc(gated.sem, 1)

            weights(0, 0, 0)
            over_pieces(act, step)

        @block.tensor
        def _(pe):
            made.begin(pe)

            def step(q, d, ab):
                w_hi_made.wait(pe, q)
                w_lo_made.wait(pe, q)
                src = branch[ab]
                for c in range(3):
                    u = 3 * q + c
                    gated.wait(pe, u - 2)
                    multiplied.wait(pe, u - 2)
                    part = slice(c * TC, (c + 1) * TC)
                    product(pe, bank(psum, pair(ab, c))[:, 0:TC], lambda k: (w_hi[:, ab, k, :], w_lo[:, ab, k, :]),
                            lambda k: (hT[0][:, k, part], hT[1][:, k, part]), KD)
                    product(pe, bank(psum, pair(ab, c) + 1)[:, 0:TC],
                            lambda k: (w_hi[:, ab, KD + k, :], w_lo[:, ab, KD + k, :]),
                            lambda k: (src[0][:, k, part], src[1][:, k, part]), KE).then_inc(made.sem, 1)

            over_pieces(pe, step)

        @block.vector
        def _(dve):
            w_lo_made.begin(dve)
            multiplied.begin(dve)
            h2_made.begin(dve)

            def weights(q, ab):
                w_hi_made.wait(dve, q)
                made.wait(dve, 3 * q - 4)
                dve.tensor_tensor(w_lo[:, ab], w_raw[:, ab], w_hi[:, ab].bitcast(F32), ALU.subtract).then_inc(w_lo_made.sem, 1)

            def step(q, d, ab):
                if not is_last(q):
                    weights(q + 1, 1 - ab)
                for c in range(3):
                    u = 3 * q + c
                    gated.wait(dve, u)
                    h2_made.wait(dve, 3 * d + c - 3)
                    out = part_b[:, c, :] if ab else part_a[:, c, :]
                    dve.tensor_tensor(out, bank(psum, pair(ab, c) + 1)[:, 0:TC], gate[:, (ab + c) % 2, :],
                                      ALU.mult).then_inc(multiplied.sem, 1)
                    if ab:
                        multiplied.wait(dve, u)
                        dve.wait_ge(h2_stored[c], DMA * d + DMA)
                        dve.tensor_tensor(h2[:, c, :], part_a[:, c, :], part_b[:, c, :], ALU.add).then_inc(h2_made.sem, 1)

            weights(0, 0)
            over_pieces(dve, step)


def merge_phase(nc, io, keep, psum):
    hT, ident, y, lg = (keep["hT_hi"], keep["hT_lo"]), keep["ident"], keep["y"], keep["lg"]
    w_src = io["w_out"][0].rearrange("(k p) c -> p k c", p=P)
    x_p = io["x"][0:SEQ, :].rearrange("(t p) d -> p t d", p=P)

    with ExitStack() as ctx:
        def sb(name, shape, dt=F32):
            return ctx.enter_context(nc.sbuf_tensor(name, shape, dt))

        def sem(name):
            return keep["semaphores"].enter_context(nc.semaphore("m_" + name))

        h2 = sb("h2_back", [P, 2, NTOK])
        w_raw = sb("o_w_raw", [P, 2, KD, P])
        w_hi = sb("o_w_hi", [P, 2, KD, P], F32R)
        w_lo = sb("o_w_lo", [P, 2, KD, P], F32R)
        x_in = sb("x_chunk", [P, 2, NT, P])
        wT = sb("woutT", [P, 2, NTOK])
        yT = sb("yT", [P, 2, NTOK])
        g2 = sb("g2_rows", [P, KD])
        w_r = sb("w_router", [P, KD, NR])
        const_in, h2_in, w_in, x_in_done = (sem("const_in"), [sem("h2_in_even"), sem("h2_in_odd")],
                                            [sem("w_in_even"), sem("w_in_odd")], [sem("x_in_even"), sem("x_in_odd")])
        passed = sem("passed")
        h2_hi, h2_lo, w_r_made, zeroed = sem("h2_hi"), sem("h2_lo"), sem("w_r_made"), sem("zeroed")
        w_hi_made, w_lo_made = Flow(sem("w_hi_made")), Flow(sem("w_lo_made"))
        made, evicted = Flow(sem("made"), 6), Flow(sem("evicted"), 6)
        xT_made, yT_made = Flow(sem("xT_made")), Flow(sem("yT_made"))
        back_made, y_copied, y_rest = Flow(sem("back_made")), Flow(sem("y_copied")), Flow(sem("y_rest"))
        block = ctx.enter_context(nc.Block())
        BANKS = ((0, 0, 4), (1, 4, 8), (2, 8, NT))

        def over_chunks(eng, step):
            step(0, 0)
            with eng.Fori(0, KD // 2 - 1) as i:
                step(2 * i + 1, 1)
                step(2 * i + 2, 0)
            step(KD - 1, 1)

        def times(d, j, per=DMA):
            return (d - j) * (per // 2) + per

        @block.sync
        def _(sp):
            for k in range(KD):
                if k >= 2:
                    sp.wait_ge(h2_lo, k - 1)
                sp.dma_start(h2[:, k % 2, :], io["h2T"][:, k, :]).then_inc(h2_in[k % 2], DMA)

        @block.gpsimd
        def _(pool):
            def load(d, j):
                w_hi_made.wait(pool, d - 2)
                w_lo_made.wait_alone(pool, d - 2, passed)
                pool.dma_start(w_raw[:, j], w_src[:, :, bass.ds(d * P, P)]).then_inc(w_in[j], DMA)
                xT_made.wait_alone(pool, d - 2, passed)
                pool.dma_start(x_in[:, j, 0:PT], x_p[:, :, bass.ds(d * P, P)]).then_inc(x_in_done[j], DMA)
                pool.dma_start(x_in[0:NS, j, PT], io["x"][SEQ:NTOK, bass.ds(d * P, P)]).then_inc(x_in_done[j], DMA)

            over_chunks(pool, load)

        @block.scalar
        def _(act):
            act.dma_start(g2[:, :], io["norm2_g"][0].rearrange("(k p) -> p k", p=P)).then_inc(const_in, DMA)
            act.dma_start(w_r[:, :, 0:NG], io["w_router_group"][0].rearrange("(k p) e -> p k e", p=P)).then_inc(const_in, DMA)
            act.dma_start(w_r[:, :, NG:], io["w_router_expert"][0].rearrange("(k p) e -> p k e", p=P)).then_inc(const_in, DMA)
            w_hi_made.begin(act)
            evicted.begin(act)
            y_copied.begin(act)

            def weights(d, j):
                act.wait_ge(w_in[j], times(d, j))
                made.wait(act, 3 * d - 4)
                act.activation(w_hi[:, j], w_raw[:, j], ACT.Copy).then_inc(w_hi_made.sem, 1)

            weights(0, 0)
            for k in range(KD):
                act.wait_ge(h2_in[k % 2], DMA * (k // 2 + 1))
                act.activation(hT[0][:, k, :], h2[:, k % 2, :], ACT.Copy).then_inc(h2_hi, 1)

            def step(d, j):
                if not (isinstance(d, int) and d == KD - 1):
                    weights(d + 1, 1 - j)
                for c in range(3):
                    made.wait(act, 3 * d + c)
                    if c == 0:
                        yT_made.wait(act, d - 2)
                    act.activation(wT[:, j, c * TC:(c + 1) * TC], bank(psum, c % 2)[:, 0:TC], ACT.Copy).then_inc(evicted.sem, 1)
                back_made.wait(act, d)
                for b, t0, t1 in BANKS[0:2]:
                    ins = act.activation(y[:, t0:t1, bass.ds(d * P, P)],
                                         bank(psum, 5 + b).rearrange("p (t c) -> p t c", c=P)[:, 0:t1 - t0], ACT.Copy)
                ins.then_inc(y_copied.sem, 1)

            over_chunks(act, step)

        @block.tensor
        def _(pe):
            made.begin(pe)
            xT_made.begin(pe)
            back_made.begin(pe)

            def step(d, j):
                pe.wait_ge(x_in_done[j], times(d, j, 2 * DMA))
                yT_made.wait(pe, d - 1)
                for b, t0, t1 in BANKS:
                    for t in range(t0, t1):
                        n = rows(t)
                        mm = pe.transpose(bank(psum, 2 + b)[:, (t - t0) * P:(t - t0) * P + n], x_in[0:n, j, t, :],
                                          ident[0:n, 0:n])
                mm.then_inc(xT_made.sem, 1)
                w_hi_made.wait(pe, d)
                w_lo_made.wait(pe, d)
                for c in range(3):
                    evicted.wait(pe, 3 * d + c - (1 if c == 0 else 2))
                    part = slice(c * TC, (c + 1) * TC)
                    if isinstance(d, int) and d == 0 and c == 0:
                        for k in range(KD):
                            pe.wait_ge(h2_lo, k + 1)
                            mm = product(pe, bank(psum, 0)[:, 0:TC], lambda _: (w_hi[:, j, k, :], w_lo[:, j, k, :]),
                                         lambda _: (hT[0][:, k, part], hT[1][:, k, part]), 1, k == 0, k == KD - 1)
                    else:
                        mm = product(pe, bank(psum, c % 2)[:, 0:TC], lambda k: (w_hi[:, j, k, :], w_lo[:, j, k, :]),
                                     lambda k: (hT[0][:, k, part], hT[1][:, k, part]), KD)
                    mm.then_inc(made.sem, 1)
                yT_made.wait(pe, d)
                y_copied.wait(pe, d - 1)
                y_rest.wait(pe, d - 1)
                if isinstance(d, int) and d == 0:
                    pe.wait_ge(w_r_made, 1)
                for b, t0, t1 in BANKS:
                    for t in range(t0, t1):
                        n = rows(t)
                        pe.transpose(bank(psum, 5 + b)[0:n, (t - t0) * P:(t - t0 + 1) * P], yT[:, j, toks(t)], ident[:, :])
                for t in range(NT):
                    mm = pe.matmul(bank(psum, 7)[0:rows(t), P + t * NR:P + (t + 1) * NR], yT[:, j, toks(t)],
                                   w_r[:, bass.ds(d, 1), :].rearrange("p a r -> p (a r)"), start=True, stop=True)
                mm.then_inc(back_made.sem, 1)

            over_chunks(pe, step)

        @block.vector
        def _(dve):
            w_lo_made.begin(dve)
            yT_made.begin(dve)
            y_rest.begin(dve)
            dve.memset(lg[:, :, :], 0.0).then_inc(zeroed, 1)
            dve.memset(y[:, PT, :], 0.0).then_inc(zeroed, 1)
            dve.wait_ge(const_in, DMA * 3)
            dve.tensor_tensor(w_r[:, :, :], w_r[:, :, :], g2[:, :].unsqueeze(2).broadcast_to([P, KD, NR]), ALU.mult).then_inc(w_r_made, 1)

            def weights(d, j):
                w_hi_made.wait(dve, d)
                made.wait(dve, 3 * d - 4)
                dve.tensor_tensor(w_lo[:, j], w_raw[:, j], w_hi[:, j].bitcast(F32), ALU.subtract).then_inc(w_lo_made.sem, 1)

            weights(0, 0)
            for k in range(KD):
                dve.wait_ge(h2_hi, k + 1)
                dve.tensor_tensor(hT[1][:, k, :], h2[:, k % 2, :], hT[0][:, k, :].bitcast(F32), ALU.subtract).then_inc(h2_lo, 1)
            dve.wait_ge(zeroed, 2)

            def step(d, j):
                if not (isinstance(d, int) and d == KD - 1):
                    weights(d + 1, 1 - j)
                xT_made.wait(dve, d)
                evicted.wait(dve, 3 * d + 2)
                back_made.wait(dve, d - 2)
                for b, t0, t1 in BANKS:
                    part = slice(t0 * P, min(t1 * P, NTOK))
                    ins = dve.tensor_tensor(yT[:, j, part], bank(psum, 2 + b)[:, 0:part.stop - part.start], wT[:, j, part], ALU.add)
                ins.then_inc(yT_made.sem, 1)
                back_made.wait(dve, d)
                dve.tensor_copy(y[0:NS, PT:NT, bass.ds(d * P, P)], bank(psum, 7)[0:NS, 0:P].unsqueeze(1))
                y_rest.wait(dve, d - 1)
                sums = bank(psum, 7)[:, P:P + NT * NR].rearrange("p (t r) -> p t r", r=NR)
                dve.tensor_tensor(lg[:, 0:PT, :], lg[:, 0:PT, :], sums[:, 0:PT], ALU.add)
                dve.tensor_tensor(lg[0:NS, PT, :], lg[0:NS, PT, :], sums[0:NS, PT], ALU.add).then_inc(y_rest.sem, 1)

            over_chunks(dve, step)


def routing_phase(nc, io, keep, psum):
    ident, y, lg = keep["ident"], keep["y"], keep["lg"]
    slot_w, gather_at, scatter_at, step_plan = keep["slot_w"], keep["gather_at"], keep["scatter_at"], keep["step_plan"]

    with ExitStack() as ctx:
        def sb(name, shape, dt=F32):
            return ctx.enter_context(nc.sbuf_tensor("r_" + name, shape, dt))

        def sem(name):
            return keep["semaphores"].enter_context(nc.semaphore("r_" + name))

        hn = sb("hn", [P, 3, D])
        g2 = sb("g2", [P, D])
        bias = sb("bias", [P, NR])
        zeros = sb("zeros", [P, D])

        yss = sb("yss", [P, NT])
        r2 = sb("r2", [P, NT])
        minus_half = sb("minus_half", [P, NT])
        logits = sb("logits", [P, NT, NR])
        g_top = sb("g_top", [P, NT])
        g_exp = sb("g_exp", [P, NT, NG])
        g_sum = sb("g_sum", [P, NT])
        g_pick = sb("g_pick", [P, NT, NG])
        eq = sb("eq", [P, NT, EPG])
        pr_top = sb("pr_top", [P, NT])
        prio = sb("prio", [P, EPG])
        sel4 = sb("sel4", [P, NT, NG, EPG])
        e_sel = sb("e_sel", [P, NT, EPG])
        e_top = sb("e_top", [P, 2, NT])
        e_pick = sb("e_pick", [P, 2, NT, EPG])
        wts = sb("wts", [P, 2, NT])
        ratio = sb("ratio", [P, NT])
        chosen = sb("chosen", [P, 2, NT, NE])
        both = sb("both", [P, NT + 1, NE])
        before = sb("before", [P, NT + 1, NE])
        lower = sb("lower", [P, P])
        ones = sb("ones", [P, P])
        place = sb("place", [P, NT, NE])
        limits = sb("limits", [P, NT])
        over = sb("over", [P, NE, NT])
        steps_of = sb("steps_of", [P, NE])
        step_end = sb("step_end", [P, NE])
        picked = sb("picked", [P, NT, NE])
        slot = sb("slot", [P, 2, NT])
        slot_i = sb("slot_i", [P, 2, NT], I32)
        slot_hi_i = sb("slot_hi_i", [P, 2, NT], I32)
        slot_lo_i = sb("slot_lo_i", [P, 2, NT], I32)
        slot_hi = sb("slot_hi", [P, 2, NT])
        slot_lo = sb("slot_lo", [P, 2, NT])
        slots = sb("slots", [P, P])
        steps = sb("steps", [P, PLANNED])
        number = sb("number", [P, NT])
        in_slot = sb("in_slot", [P, 4, P])
        in_step = sb("in_step", [P, 4, 2, PLANNED])
        found = sb("found", [P, 2, PLANNED])
        empty = sb("empty", [P, PLANNED])
        spare = sb("spare", [P, 1])
        where = sb("where", [P, PLANNED])
        ended = sb("ended", [P, PLANNED, NE])
        expert_f = sb("expert_f", [P, PLANNED])
        is_new = sb("is_new", [P, PLANNED])
        load_no = sb("load_no", [P, PLANNED])
        slots_i = sb("slots_i", [P, P], I32)

        const_in, consts, stored = sem("const_in"), sem("consts"), sem("stored")
        hn_stored = [sem(f"hn_stored_{b}") for b in range(3)]
        dve_step, squared, meaned, rooted, hn_made = (sem("dve_step"), sem("squared"), sem("meaned"), sem("rooted"),
                                                      sem("hn_made"))
        g_shifted, g_exped, e_shifted, e_exped = sem("g_shifted"), sem("g_exped"), sem("e_shifted"), sem("e_exped")
        sums_ready, sums_made, pair_made, pair_used, found_made = (sem("sums_ready"), sem("sums_made"), sem("pair_made"),
                                                                   sem("pair_used"), sem("found_made"))
        sq_done = sem("sq_done")
        block = ctx.enter_context(nc.Block())

        @block.sync
        def _(sp):
            for t in range(NT):
                sp.dma_start(io["y"][toks(t), :], y[0:rows(t), t, :]).then_inc(stored, DMA)
            sp.wait_ge(consts, 1)
            sp.dma_start(io["y"][NTOK:NTOK + SLOT, :], zeros[:, :]).then_inc(stored, DMA)
            for t in range(NT):
                sp.wait_ge(hn_made, t + 1)
                sp.dma_start(io["hn"][toks(t), :], hn[0:rows(t), t % 3, :]).then_inc(hn_stored[t % 3], DMA)
            sp.wait_ge(stored, DMA * (NT + 1))
            for b in range(3):
                sp.wait_ge(hn_stored[b], DMA * 3)

        @block.gpsimd
        def _(pool):
            pool.memset(zeros[:, :], 0.0).then_inc(consts, 1)
            pool.memset(minus_half[:, :], -0.5).then_inc(consts, 1)
            pool.memset(ones[:, :], 1.0).then_inc(consts, 1)
            pool.memset(lower[:, :], 1.0).then_inc(consts, 1)
            pool.wait_ge(consts, 4)
            pool.affine_select(out=lower[:, :], in_=lower[:, :], compare_op=ALU.is_ge, fill=0.0, base=-1,
                               pattern=[[1, P]], channel_multiplier=-1).then_inc(consts, 1)
            kw = dict(allow_small_or_imprecise_dtypes=True)
            pool.iota(prio[:, :], [[-1, EPG]], base=EPG, channel_multiplier=0, **kw).then_inc(consts, 1)
            pool.iota(limits[:, :], [[SLOT, NT]], base=0, channel_multiplier=0, **kw).then_inc(consts, 1)
            pool.iota(slots[:, :], [[1, P]], base=0, channel_multiplier=0, **kw).then_inc(consts, 1)
            pool.iota(steps[:, :], [[1, PLANNED]], base=0, channel_multiplier=0, **kw).then_inc(consts, 1)
            pool.iota(number[:, :], [[P, NT]], base=1, channel_multiplier=1, **kw).then_inc(consts, 1)
            pool.iota(spare[:, :], [[1, 1]], base=NTOK + 1, channel_multiplier=1, **kw).then_inc(consts, 1)
            pool.wait_ge(meaned, 1)
            pool.tensor_tensor(r2[:, :], yss[:, :], minus_half[:, :], ALU.pow).then_inc(rooted, 1)

        @block.scalar
        def _(act):
            act.dma_start(g2[:, :], io["norm2_g"][0].partition_broadcast(P)).then_inc(const_in, DMA)
            act.dma_start(bias[:, 0:NG], io["b_router_group"][0].partition_broadcast(P)).then_inc(const_in, DMA)
            act.dma_start(bias[:, NG:], io["b_router_expert"][0].partition_broadcast(P)).then_inc(const_in, DMA)
            for t in range(NT):
                if t >= 3:
                    act.wait_ge(squared, t - 2)
                act.activation(hn[:, t % 3, :], y[:, t, :], ACT.Square, accum_out=yss[:, t:t + 1]).then_inc(squared, 1)
            act.wait_ge(g_shifted, 1)
            act.activation(g_exp[:, :, :], g_exp[:, :, :], ACT.Exp).then_inc(g_exped, 1)
            act.wait_ge(e_shifted, 1)
            act.activation(ratio[:, :], ratio[:, :], ACT.Exp).then_inc(e_exped, 1)

        @block.tensor
        def _(pe):
            pe.wait_ge(sums_ready, 1)
            width = (NT + 1) * NE
            flat = [a[:, :, :].rearrange("p t e -> p (t e)") for a in (both, before)]
            pe.matmul(bank(psum, 0)[:, 0:width], lower[:, :], flat[0], start=True, stop=False)
            pe.matmul(bank(psum, 0)[:, 0:width], ones[:, :], flat[1], start=False, stop=True).then_inc(sums_made, 1)
            for n in range(2 * NT):
                pe.wait_ge(pair_made, n + 1)
                pe.matmul(bank(psum, 1)[:, 0:2 * PLANNED], in_slot[:, n % 4, :],
                          in_step[:, n % 4, :, :].rearrange("p a s -> p (a s)"), start=n == 0,
                          stop=n == 2 * NT - 1).then_inc(pair_used, 1)

        @block.vector
        def _(dve):
            step = Step(dve, dve_step)
            did = step.did

            def tt(out, a, b, op):
                did(dve.tensor_tensor(out, a, b, op))

            def over_last(a, n):
                return a.unsqueeze(2).broadcast_to([P, NT, n])

            def first_top(out, values, top):
                tt(out, values, over_last(top, EPG), ALU.is_equal)
                tt(eq[:, :, :], out, prio[:, :].unsqueeze(1).broadcast_to([P, NT, EPG]), ALU.mult)
                did(dve.tensor_reduce(pr_top[:, :], eq[:, :, :], AX_X, ALU.max))
                tt(out, eq[:, :, :], over_last(pr_top[:, :], EPG), ALU.is_equal)

            dve.wait_ge(squared, NT)
            dve.tensor_scalar(yss[:, :], yss[:, :], 1.0 / D, EPS, ALU.mult, ALU.add).then_inc(meaned, 1)
            dve.wait_ge(const_in, DMA * 3)
            dve.wait_ge(consts, 11)
            dve.wait_ge(rooted, 1)
            tt(logits[:, :, :], lg[:, :, :], over_last(r2[:, :], NR), ALU.mult)
            tt(logits[:, :, :], logits[:, :, :], bias[:, :].unsqueeze(1).broadcast_to([P, NT, NR]), ALU.add)
            gl = logits[:, :, 0:NG]
            el = logits[:, :, NG:].rearrange("p t (g e) -> p t g e", g=NG)
            did(dve.tensor_reduce(g_top[:, :], gl, AX_X, ALU.max))
            dve.tensor_tensor(g_exp[:, :, :], gl, over_last(g_top[:, :], NG), ALU.subtract).then_inc(g_shifted, 1)
            first_top(g_pick[:, :, :], gl, g_top[:, :])
            tt(sel4[:, :, :, :], el, g_pick[:, :, :].unsqueeze(3).broadcast_to([P, NT, NG, EPG]), ALU.mult)
            did(dve.tensor_reduce(e_sel[:, :, :], sel4[:, :, :, :].rearrange("p t g e -> p t e g"), AX_X, ALU.add))
            for n in range(2):
                did(dve.tensor_reduce(e_top[:, n, :], e_sel[:, :, :], AX_X, ALU.max))
                first_top(e_pick[:, n, :, :], e_sel[:, :, :], e_top[:, n, :])
                if n == 0:
                    did(dve.scalar_tensor_tensor(e_sel[:, :, :], e_pick[:, 0, :, :], NEG, e_sel[:, :, :], ALU.mult, ALU.add))
            dve.tensor_tensor(ratio[:, :], e_top[:, 1, :], e_top[:, 0, :], ALU.subtract).then_inc(e_shifted, 1)
            for n in range(2):
                tt(chosen[:, n, :, :].rearrange("p t (g e) -> p t g e", g=NG),
                   g_pick[:, :, :].unsqueeze(3).broadcast_to([P, NT, NG, EPG]),
                   e_pick[:, n, :, :].unsqueeze(2).broadcast_to([P, NT, NG, EPG]), ALU.mult)
            for q in range(NS, P, 32):
                did(dve.memset(chosen[q:q + 32, :, PT, :], 0.0))
                did(dve.memset(number[q:q + 32, PT:NT], 0.0))
            did(dve.memset(both[:, NT, :], 0.0))
            tt(both[:, 0:NT, :], chosen[:, 0, :, :], chosen[:, 1, :, :], ALU.add)
            did(dve.memset(before[:, 0, :], 0.0))
            for t in range(NT - 1):
                tt(before[:, t + 1, :], before[:, t, :], both[:, t, :], ALU.add)
            dve.tensor_tensor(before[:, NT, :], before[:, NT - 1, :], both[:, NT - 1, :], ALU.add).then_inc(sums_ready, 1)
            dve.wait_ge(g_exped, 1)
            did(dve.tensor_reduce(g_sum[:, :], g_exp[:, :, :], AX_X, ALU.add))
            dve.wait_ge(e_exped, 1)
            did(dve.tensor_scalar(wts[:, 0, :], ratio[:, :], 1.0, None, ALU.add))
            tt(wts[:, 0, :], wts[:, 0, :], g_sum[:, :], ALU.mult)
            did(dve.reciprocal(wts[:, 0, :], wts[:, 0, :]))
            tt(wts[:, 1, :], wts[:, 0, :], ratio[:, :], ALU.mult)
            for q in range(NS, P, 32):
                did(dve.memset(wts[q:q + 32, :, PT:NT], 0.0))
            dve.wait_ge(sums_made, 1)
            sums = bank(psum, 0)[:, 0:(NT + 1) * NE].rearrange("p (t e) -> p t e", e=NE)
            did(dve.tensor_copy(place[:, :, :], sums[:, 0:NT, :]))
            did(dve.tensor_copy(step_end[:, :], sums[:, NT, :]))
            tt(over[:, :, :], step_end[:, :].unsqueeze(2).broadcast_to([P, NE, NT]),
               limits[:, :].unsqueeze(1).broadcast_to([P, NE, NT]), ALU.is_gt)
            did(dve.tensor_reduce(steps_of[:, :], over[:, :, :], AX_X, ALU.add))
            did(dve.tensor_tensor_scan(step_end[:, :], ones[:, 0:NE], steps_of[:, :], 0.0, ALU.mult, ALU.add))
            tt(steps_of[:, :], step_end[:, :], steps_of[:, :], ALU.subtract)
            did(dve.tensor_scalar(steps_of[:, :], steps_of[:, :], float(SLOT), None, ALU.mult))
            tt(place[:, :, :], place[:, :, :], steps_of[:, :].unsqueeze(1).broadcast_to([P, NT, NE]), ALU.add)
            for n in range(2):
                tt(picked[:, :, :], place[:, :, :], chosen[:, n, :, :], ALU.mult)
                did(dve.tensor_reduce(slot[:, n, :], picked[:, :, :], AX_X, ALU.add))
            did(dve.tensor_copy(slot_i[:, :, :], slot[:, :, :]))
            did(dve.tensor_scalar(slot_hi_i[:, :, :], slot_i[:, :, :], SLOT.bit_length() - 1, None, ALU.logical_shift_right))
            did(dve.tensor_scalar(slot_lo_i[:, :, :], slot_i[:, :, :], SLOT - 1, None, ALU.bitwise_and))
            did(dve.tensor_copy(slot_hi[:, :, :], slot_hi_i[:, :, :]))
            did(dve.tensor_copy(slot_lo[:, :, :], slot_lo_i[:, :, :]))
            for n in range(2 * NT):
                t, c = n // 2, n % 2
                if n >= 4:
                    dve.wait_ge(pair_used, n - 3)
                dve.tensor_scalar(in_slot[:, n % 4, :], slots[:, :], slot_lo[:, c, t:t + 1], None, ALU.is_equal)
                for v, value in enumerate((number[:, t:t + 1], wts[:, c, t:t + 1])):
                    ins = dve.tensor_scalar(in_step[:, n % 4, v, :], steps[:, :], slot_hi[:, c, t:t + 1], value,
                                            ALU.is_equal, ALU.mult)
                ins.then_inc(pair_made, 1)
            tt(ended[:, :, :], step_end[:, :].unsqueeze(1).broadcast_to([P, PLANNED, NE]),
               steps[:, :].unsqueeze(2).broadcast_to([P, PLANNED, NE]), ALU.is_le)
            did(dve.tensor_reduce(expert_f[:, :], ended[:, :, :], AX_X, ALU.add))
            did(dve.tensor_scalar(expert_f[:, :], expert_f[:, :], float(NE - 1), None, ALU.min))
            did(dve.tensor_copy(step_plan[:, 2, 0:PLANNED], expert_f[:, :]))
            did(dve.memset(is_new[:, 0:1], 0.0))
            tt(is_new[:, 1:PLANNED], expert_f[:, 1:PLANNED], expert_f[:, 0:PLANNED - 1], ALU.is_gt)
            did(dve.tensor_copy(step_plan[:, 1, 0:PLANNED], is_new[:, :]))
            did(dve.tensor_tensor_scan(load_no[:, :], ones[:, 0:PLANNED], is_new[:, :], 0.0, ALU.mult, ALU.add))
            did(dve.tensor_copy(step_plan[:, 0, 0:PLANNED], load_no[:, :]))
            did(dve.tensor_copy(step_plan[:, 0, PLANNED:PLANNED + 1], step_end[:, NE - 1:NE]))
            dve.wait_ge(pair_used, 2 * NT)
            did(dve.tensor_copy(found[:, :, :].rearrange("p a s -> p (a s)"), bank(psum, 1)[:, 0:2 * PLANNED]))
            did(dve.tensor_copy(slot_w[:, :], found[:, 1, :]))
            did(dve.tensor_scalar(where[:, :], found[:, 0, :], -1.0, 0.0, ALU.add, ALU.max))
            did(dve.tensor_copy(gather_at[:, :], where[:, :]))
            did(dve.tensor_scalar(empty[:, :], found[:, 0, :], 0.0, spare[:, 0:1], ALU.is_equal, ALU.mult))
            tt(empty[:, :], empty[:, :], found[:, 0, :], ALU.add)
            did(dve.tensor_scalar(empty[:, :], empty[:, :], -1.0, None, ALU.add))
            did(dve.tensor_copy(scatter_at[:, :], empty[:, :]))
            for t in range(NT):
                n = rows(t)
                if t >= 3:
                    dve.wait_ge(hn_stored[t % 3], DMA * (t // 3))
                dve.scalar_tensor_tensor(hn[0:n, t % 3, :], y[0:n, t, :], r2[0:n, t:t + 1], g2[0:n, :], ALU.mult,
                                         ALU.mult).then_inc(hn_made, 1)


def experts_phase(nc, io, keep, psum):
    ident = keep["ident"]
    slot_w, gather_at, scatter_at, step_plan = keep["slot_w"], keep["gather_at"], keep["scatter_at"], keep["step_plan"]
    w_gate = io["w_exp_gate"][0].rearrange("e (k p) f -> p e k f", p=P)
    w_up = io["w_exp_up"][0].rearrange("e (k p) f -> p e k f", p=P)
    w_down = io["w_exp_down"][0].rearrange("e (k p) d -> p e k d", p=P)
    KF = DE // P
    KH = KD // 2
    HD2 = D // 2

    with ExitStack() as ctx:
        def sb(name, shape, dt=F32):
            return ctx.enter_context(nc.sbuf_tensor("x_" + name, shape, dt))

        def sem(name):
            return keep["semaphores"].enter_context(nc.semaphore("x_" + name))

        gu_raw = sb("gu_raw", [P, 2, KD, 2, DE])
        gu_hi = sb("gu_hi", [P, 2, KD, 2, DE], F32R)
        gu_lo = sb("gu_lo", [P, 2, KD, 2, DE], F32R)
        dn_raw = sb("dn_raw", [P, 2, KF, D])
        dn_hi = sb("dn_hi", [P, 2, KF, D], F32R)
        dn_lo = sb("dn_lo", [P, 2, KF, D], F32R)
        at = sb("at", [P, 2, 2], I32)
        xg = sb("xg", [P, 2, D])
        xT_hi = sb("xT_hi", [P, 2, KD, P], F32R)
        xT_lo = sb("xT_lo", [P, 2, KD, P], F32R)
        silu = sb("silu", [P, DE])
        hid = sb("hid", [P, DE])
        hidT_hi = sb("hidT_hi", [P, KF, P], F32R)
        hidT_lo = sb("hidT_lo", [P, KF, P], F32R)
        out = sb("out", [P, 2, D])

        gu_in, dn_in = sem("gu_in"), sem("dn_in")
        gathered, added = [sem("gathered_0"), sem("gathered_1")], sem("added")
        passed, loads_passed = sem("passed"), sem("loads_passed")
        gu_hi_made, gu_lo_made = Flow(sem("gu_hi_made"), 4), Flow(sem("gu_lo_made"), 4)
        dn_hi_made, dn_lo_made = Flow(sem("dn_hi_made")), Flow(sem("dn_lo_made"))
        xT_made, xT_hi_made, xT_lo_made = Flow(sem("xT_made"), 4), Flow(sem("xT_hi_made"), 4), Flow(sem("xT_lo_made"), 4)
        at_made, up_made, silu_made, hid_made = Flow(sem("at_made")), Flow(sem("up_made")), Flow(sem("silu_made")), Flow(sem("hid_made"))
        hidT_made, hidT_hi_made, hidT_lo_made = Flow(sem("hidT_made")), Flow(sem("hidT_hi_made")), Flow(sem("hidT_lo_made"))
        down_made, out_made, at_copied = Flow(sem("down_made")), Flow(sem("out_made")), Flow(sem("at_copied"))
        add_turn = Flow(sem("add_turn"))
        block = ctx.enter_context(nc.Block())

        def over_steps(eng, step):
            used = steps_used(eng)
            step(0, 0)
            with eng.Fori(0, MOST_STEPS // 2) as i:
                for ahead in range(2):
                    with eng.If(i * 2 + (ahead + 1) <= used):
                        step(2 * i + (ahead + 1), 1 - ahead)

        def steps_used(eng):
            return eng.value_load(step_plan[0:1, 0, PLANNED:PLANNED + 1], min_val=1, max_val=MOST_STEPS)

        def load_of(eng, s):
            return eng.value_load(step_plan[0:1, 0, bass.ds(s, 1)], min_val=0, max_val=NE - 1)

        def if_new(eng, s):
            return eng.If(eng.value_load(step_plan[0:1, 1, bass.ds(s, 1)], min_val=0, max_val=1) > 0)

        def first(s):
            return isinstance(s, int) and s == 0

        def times(s, j, per=DMA):
            return (s - j) * (per // 2) + per

        @block.sync
        def _(sp):
            def load(s):
                n = load_of(sp, s)
                e = sp.value_load(step_plan[0:1, 2, bass.ds(s, 1)], min_val=0, max_val=NE - 1)
                buf = bass.ds(n % 2, 1)
                gu_hi_made.wait_alone(sp, n * 2 - 3, loads_passed)
                gu_lo_made.wait_alone(sp, n * 2 - 3, loads_passed)
                if not first(s):
                    sp.wait_ge(gu_in, n * (2 * DMA))
                    sp.sem_inc(loads_passed, 1)
                sp.dma_start(gu_raw[:, buf, :, 0, :], w_gate[:, bass.ds(e, 1)]).then_inc(gu_in, DMA)
                sp.dma_start(gu_raw[:, buf, :, 1, :], w_up[:, bass.ds(e, 1)]).then_inc(gu_in, DMA)
                dn_hi_made.wait_alone(sp, n - 2, loads_passed)
                dn_lo_made.wait_alone(sp, n - 2, loads_passed)
                if not first(s):
                    sp.wait_ge(dn_in, n * DMA)
                    sp.sem_inc(loads_passed, 1)
                sp.dma_start(dn_raw[:, buf], w_down[:, bass.ds(e, 1)]).then_inc(dn_in, DMA)

            load(0)
            with sp.Fori(0, MOST_STEPS) as i:
                with if_new(sp, i + 1):
                    load(i + 1)

        @block.gpsimd
        def _(pool):
            for f in (at_made, dn_lo_made, at_copied, add_turn):
                f.begin(pool)

            def gather(s, j):
                xT_made.wait(pool, 2 * s - 3)
                pool.tensor_copy(at[:, j, 0:1], gather_at[:, bass.ds(s, 1)]).then_inc(at_made.sem, 1)
                at_made.wait_alone(pool, s, passed)
                pool.indirect_dma_start(xg[:, j, :], None, io["hn"], bass.IndirectOffsetOnAxis(at[:, j, 0:1], 0)).then_inc(gathered[j], DMA)

            def scatter(s, j):
                out_made.wait(pool, s)
                pool.tensor_copy(at[:, j, 1:2], scatter_at[:, bass.ds(s, 1)]).then_inc(at_copied.sem, 1)
                at_copied.wait(pool, s)
                if not first(s):
                    pool.wait_ge(added, s * DMA)
                pool.sem_inc(add_turn.sem, 1)
                pool.indirect_dma_start(io["y"], bass.IndirectOffsetOnAxis(at[:, j, 1:2], 0), out[:, j, :], None,
                                        compute_op=ALU.add).then_inc(added, DMA)

            def down_low(s):
                n = load_of(pool, s)
                buf = bass.ds(n % 2, 1)
                dn_hi_made.wait(pool, n)
                down_made.wait(pool, s - 2)
                pool.tensor_tensor(dn_lo[:, buf], dn_raw[:, buf], dn_hi[:, buf].bitcast(F32), ALU.subtract).then_inc(dn_lo_made.sem, 1)

            def step(s, j):
                gather(s + 2, j)
                if first(s):
                    down_low(s)
                else:
                    with if_new(pool, s):
                        down_low(s)
                    scatter(s - 1, 1 - j)

            gather(0, 0)
            gather(1, 1)
            over_steps(pool, step)
            used = steps_used(pool)
            pool.wait_ge(added, used * DMA)
            pool.wait_ge(gathered[0], (used + 4) // 2 * DMA)
            pool.wait_ge(gathered[1], (used + 3) // 2 * DMA)

        @block.scalar
        def _(act):
            for f in (gu_hi_made, dn_hi_made, xT_hi_made, silu_made, hidT_hi_made):
                f.begin(act)

            def up_high(s, half):
                n = load_of(act, s)
                buf = bass.ds(n % 2, 1)
                ks = slice(half * KH, (half + 1) * KH)
                act.wait_ge(gu_in, n * (2 * DMA) + 2 * DMA)
                up_made.wait(act, s - 2)
                act.activation(gu_hi[:, buf, ks], gu_raw[:, buf, ks], ACT.Copy).then_inc(gu_hi_made.sem, 1)

            def down_high(s):
                n = load_of(act, s)
                buf = bass.ds(n % 2, 1)
                act.wait_ge(dn_in, n * DMA + DMA)
                down_made.wait(act, s - 2)
                act.activation(dn_hi[:, buf], dn_raw[:, buf], ACT.Copy).then_inc(dn_hi_made.sem, 1)

            def tokens_high(s, j):
                up_made.wait(act, s - 2)
                for half in range(2):
                    xT_made.wait(act, 2 * s + half)
                    act.activation(xT_hi[:, j, half * KH:(half + 1) * KH, :].rearrange("p k c -> p (k c)"),
                                   bank(psum, half), ACT.Copy).then_inc(xT_hi_made.sem, 1)

            def hidden_high(s):
                hidT_made.wait(act, s)
                down_made.wait(act, s - 1)
                act.activation(hidT_hi[:, :, :].rearrange("p k c -> p (k c)"), bank(psum, 4)[:, 0:DE], ACT.Copy).then_inc(hidT_hi_made.sem, 1)

            def step(s, j):
                if first(s):
                    down_high(s)
                else:
                    hidden_high(s - 1)
                    with if_new(act, s):
                        down_high(s)
                with if_new(act, s + 1):
                    up_high(s + 1, 0)
                up_made.wait(act, s)
                hid_made.wait(act, s - 1)
                act.activation(silu[:, :], bank(psum, 2 + j)[:, 0:DE], ACT.Silu).then_inc(silu_made.sem, 1)
                tokens_high(s + 1, 1 - j)
                with if_new(act, s + 1):
                    up_high(s + 1, 1)

            tokens_high(0, 0)
            for half in range(2):
                up_high(0, half)
            over_steps(act, step)

        @block.tensor
        def _(pe):
            for f in (xT_made, up_made, hidT_made, down_made):
                f.begin(pe)

            def token_turn(s, j):
                pe.wait_ge(gathered[j], times(s, j))
                for half in range(2):
                    xT_lo_made.wait(pe, 2 * s - 2 + half)
                    for k in range(KH):
                        ks = slice((half * KH + k) * P, (half * KH + k + 1) * P)
                        mm = pe.transpose(bank(psum, half)[:, k * P:(k + 1) * P], xg[:, j, ks], ident[:, :])
                    mm.then_inc(xT_made.sem, 1)

            def up(s, j):
                n = load_of(pe, s)
                buf = bass.ds(n % 2, 1)
                hid_made.wait(pe, s - 2)
                for half in range(2):
                    xT_hi_made.wait(pe, 2 * s + half)
                    xT_lo_made.wait(pe, 2 * s + half)
                    gu_hi_made.wait(pe, n * 2 + half)
                    gu_lo_made.wait(pe, n * 2 + half)
                    h = half * KH
                    mm = product(pe, bank(psum, 2 + j), lambda k: (xT_hi[:, j, h + k, :], xT_lo[:, j, h + k, :]),
                                 lambda k: (gu_hi[:, buf, h + k], gu_lo[:, buf, h + k]), KH, first=half == 0, last=half == 1)
                mm.then_inc(up_made.sem, 1)

            def hidden_turn(s):
                hid_made.wait(pe, s)
                hidT_lo_made.wait(pe, s - 1)
                for f in range(KF):
                    mm = pe.transpose(bank(psum, 4)[:, f * P:(f + 1) * P], hid[:, f * P:(f + 1) * P], ident[:, :])
                mm.then_inc(hidT_made.sem, 1)

            def down(s):
                n = load_of(pe, s)
                buf = bass.ds(n % 2, 1)
                hidT_hi_made.wait(pe, s)
                hidT_lo_made.wait(pe, s)
                dn_hi_made.wait(pe, n)
                dn_lo_made.wait(pe, n)
                out_made.wait(pe, s - 1)
                for half in range(2):
                    part = slice(half * HD2, (half + 1) * HD2)
                    mm = product(pe, bank(psum, 5 + half), lambda k: (hidT_hi[:, k, :], hidT_lo[:, k, :]),
                                 lambda k: (dn_hi[:, buf, k, part], dn_lo[:, buf, k, part]), KF)
                mm.then_inc(down_made.sem, 1)

            def step(s, j):
                up(s, j)
                token_turn(s + 1, 1 - j)
                if not first(s):
                    down(s - 1)
                hidden_turn(s)

            token_turn(0, 0)
            over_steps(pe, step)

        @block.vector
        def _(dve):
            for f in (gu_lo_made, xT_lo_made, hid_made, hidT_lo_made, out_made):
                f.begin(dve)

            def up_low(s, half):
                n = load_of(dve, s)
                buf = bass.ds(n % 2, 1)
                ks = slice(half * KH, (half + 1) * KH)
                gu_hi_made.wait(dve, n * 2 + half)
                up_made.wait(dve, s - 2)
                dve.tensor_tensor(gu_lo[:, buf, ks], gu_raw[:, buf, ks], gu_hi[:, buf, ks].bitcast(F32),
                                  ALU.subtract).then_inc(gu_lo_made.sem, 1)

            def tokens_low(s, j):
                for half in range(2):
                    xT_hi_made.wait(dve, 2 * s + half)
                    ks = slice(half * KH, (half + 1) * KH)
                    dve.tensor_tensor(xT_lo[:, j, ks, :].rearrange("p k c -> p (k c)"), bank(psum, half),
                                      xT_hi[:, j, ks, :].rearrange("p k c -> p (k c)").bitcast(F32),
                                      ALU.subtract).then_inc(xT_lo_made.sem, 1)

            def hidden_low(s):
                hidT_hi_made.wait(dve, s)
                dve.tensor_tensor(hidT_lo[:, :, :].rearrange("p k c -> p (k c)"), bank(psum, 4)[:, 0:DE],
                                  hidT_hi[:, :, :].rearrange("p k c -> p (k c)").bitcast(F32), ALU.subtract).then_inc(hidT_lo_made.sem, 1)

            def evict(s, j):
                down_made.wait(dve, s)
                add_turn.wait(dve, s - 1)
                dve.tensor_copy(out[:, j, :], psum[:, 5:7, :].rearrange("p a c -> p (a c)")).then_inc(out_made.sem, 1)

            def step(s, j):
                if not first(s):
                    hidden_low(s - 1)
                with if_new(dve, s + 1):
                    up_low(s + 1, 0)
                silu_made.wait(dve, s)
                hidT_made.wait(dve, s - 1)
                dve.scalar_tensor_tensor(hid[:, :], silu[:, :], slot_w[:, bass.ds(s, 1)], bank(psum, 2 + j)[:, DE:], ALU.mult,
                                         ALU.mult).then_inc(hid_made.sem, 1)
                tokens_low(s + 1, 1 - j)
                with if_new(dve, s + 1):
                    up_low(s + 1, 1)
                if not first(s):
                    evict(s - 1, 1 - j)

            tokens_low(0, 0)
            for half in range(2):
                up_low(0, half)
            over_steps(dve, step)


def hybrid_layer(nc, io):
    with ExitStack() as ctx:
        def sb(stack, name, shape, dt=F32):
            return stack.enter_context(nc.sbuf_tensor(name, shape, dt))

        ctx.enter_context(nc.allow_non_contiguous_dma(reason="small per-row constants"))
        psum = ctx.enter_context(nc.psum_tensor("psum", [P, 8, 512], F32))
        keep = {"ident": sb(ctx, "ident", [P, P]), "semaphores": ctx}
        for name in ("gather_at", "scatter_at"):
            keep[name] = sb(ctx, name, [P, PLANNED], I32)
        keep["step_plan"] = sb(ctx, "step_plan", [P, 3, PLANNED + 1], I32)
        keep["slot_w"] = sb(ctx, "slot_w", [P, PLANNED])
        keep["lg"] = sb(ctx, "lg", [P, NT, NR])
        with ExitStack() as dense:
            for name in ("hT_hi", "hT_lo"):
                keep[name] = sb(dense, name, [P, KD, NTOK], F32R)
            with ExitStack() as branches:
                for name in ("oaT_hi", "oaT_lo"):
                    keep[name] = sb(branches, name, [P, KE, NTOK], F32R)
                attention_phase(nc, io, keep, psum)
                keep["mixT"] = sb(branches, "mixT", [P, SG, NTOK])
                sgu_values_phase(nc, io, keep, psum)
                for name in ("obT_hi", "obT_lo"):
                    keep[name] = sb(branches, name, [P, KE, NTOK], F32R)
                sgu_gate_phase(nc, io, keep, psum)
                gates_phase(nc, io, keep, psum)
            keep["y"] = sb(dense, "y", [P, NT, D])
            merge_phase(nc, io, keep, psum)
            routing_phase(nc, io, keep, psum)
        experts_phase(nc, io, keep, psum)


_INS = ["cache_k_win", "cache_v_win", "norm1_g", "w_in", "q_norm_g", "k_norm_g", "attn_sinks", "ln_v_g", "ln_v_b",
        "w_spatial", "b_spatial", "w_branch_a", "w_branch_b", "w_out", "norm2_g", "w_router_group", "b_router_group",
        "w_router_expert", "b_router_expert", "w_exp_gate", "w_exp_up", "w_exp_down"]
_OUTS = {"y": (NTOK + SLOT, D), "new_k_p": (1, 1, WIN, KV, HD), "new_v_p": (1, 1, WIN, KV, HD),
         "new_k_s": (1, DEC_B, WIN, KV, HD), "new_v_s": (1, DEC_B, WIN, KV, HD),
         "new_vs": (1, DEC_B, DEC_T, SG, SW // SG)}


def kernel(**inputs):
    import numpy as np
    import concourse.bacc as bacc
    from concourse.bass_utils import run_bass_kernel_spmd

    nc = bacc.Bacc("TRN2", target_bir_lowering=False, num_devices=1)
    arrays = {"in_x": np.concatenate([np.asarray(inputs["x_prompt"]).reshape(SEQ, D),
                                      np.asarray(inputs["x_sample"]).reshape(NS, D)])}
    for name in _INS:
        arrays["in_" + name] = np.ascontiguousarray(inputs[name])
    short = {"cache_k_win": "cache_k", "cache_v_win": "cache_v"}
    io = {}
    for name, a in arrays.items():
        t = nc.dram_tensor(name, a.shape, mybir.dt.from_np(a.dtype), kind="ExternalInput").ap()
        io[short.get(name[3:], name[3:])] = t
    for name, shape in _OUTS.items():
        io[name] = nc.dram_tensor("out_" + name, shape, F32, kind="ExternalOutput").ap()
    io["h2T"] = nc.dram_tensor("h2T_rows", (P, KD, NTOK), F32, kind="Internal").ap()
    io["hn"] = nc.dram_tensor("hn_rows", (NTOK, D), F32, kind="Internal").ap()
    hybrid_layer(nc, io)
    got = run_bass_kernel_spmd(nc, [arrays], core_ids=[0]).results[0]
    y = got["out_y"]
    return (y[0:SEQ].reshape(1, SEQ, D), y[SEQ:NTOK].reshape(DEC_B, DEC_T, D), got["out_new_k_p"], got["out_new_v_p"],
            got["out_new_k_s"], got["out_new_v_s"], got["out_new_vs"])
```

```python
from contextlib import ExitStack

import concourse.bass as bass
from concourse import mybir

F32 = mybir.dt.float32
F32R = mybir.dt.float32r
I32 = mybir.dt.int32
ALU = mybir.AluOpType
ACT = mybir.ActivationFunctionType
AX_X = mybir.AxisListType.X

P = 128
D = 1024
KD = D // P
SEQ = 1024
DEC_B, DEC_T = 8, 4
NS = DEC_B * DEC_T
NTOK = SEQ + NS
PT = SEQ // P
NT = PT + 1
HEADS, KV, G, HD = 8, 2, 4, 64
AW = HEADS * HD
KVW = KV * HD
QKV = AW + 2 * KVW
WIN = 128
SG = 4
SW = 512
KE = AW // P
OFF_VS = QKV + SW
OFF_GA = QKV + 2 * SW
OFF_GB = OFF_GA + D
TC = NTOK // 3
NG, EPG = 4, 4
NE = NG * EPG
NR = NG + NE
DE = 256
EPS = 1e-6
NEG = -1e30
SLOT = 128
MOST_STEPS = (2 * NTOK + NE * (SLOT - 1)) // SLOT
MOST_STEPS += MOST_STEPS % 2
PLANNED = MOST_STEPS + 3
FAR = 1 << 20
DMA = 16


def rows(t):
    return P if t < PT else NS


def toks(t):
    return slice(t * P, t * P + rows(t))


def product(eng, out, lhs, rhs, nk, first=True, last=True):
    for k in range(nk):
        lh, ll = lhs(k)
        rh, rl = rhs(k)
        eng.matmul(out, lh, rh, start=first and k == 0, stop=False)
        eng.matmul(out, lh, rl, start=False, stop=False)
        mm = eng.matmul(out, ll, rh, start=False, stop=last and k == nk - 1)
    return mm


def bank(psum, n):
    return psum[:, n, :]


class Step:

    def __init__(self, eng, sem):
        self.eng, self.sem, self.n = eng, sem, 0

    def did(self, ins):
        self.n += 1
        ins.then_inc(self.sem, 1)
        self.eng.wait_ge(self.sem, self.n)


class Flow:

    def __init__(self, sem, start=2):
        self.sem, self.start = sem, start

    def begin(self, eng):
        eng.sem_inc(self.sem, self.start)

    def after(self, n):
        return n + (self.start + 1)

    def wait(self, eng, n):
        eng.wait_ge(self.sem, self.after(n))

    def wait_alone(self, eng, n, passed):
        eng.wait_ge(self.sem, self.after(n))
        eng.sem_inc(passed, 1)


def attention_phase(nc, io, keep, psum):
    ident, hT, oaT = keep["ident"], (keep["hT_hi"], keep["hT_lo"]), (keep["oaT_hi"], keep["oaT_lo"])
    NP = QKV // P
    SK = DEC_B * WIN + NS
    w_src = io["w_in"][0].rearrange("(k p) c -> p k c", p=P)

    used = []
    with ExitStack() as ctx:
        def sb(name, shape, dt=F32):
            return ctx.enter_context(nc.sbuf_tensor(name, shape, dt))

        def sem(name):
            used.append(ctx.enter_context(nc.semaphore(name)))
            return used[-1]

        w_raw = sb("qkv_w_raw", [P, 2, KD, P])
        w_hi, w_lo = keep["w_hi"], keep["w_lo"]

        x_in = sb("x_in", [P, 2, D])
        x_norm = sb("x_norm", [P, D])
        h_raw = sb("h_raw", [P, 2, 4, P])
        z = sb("z_qkv", [P, AW + KVW])
        z_sq = w_raw[:, 1].rearrange("p k c -> p (k c)")[:, 0:AW + KVW]
        v_ring = sb("v_ring", [P, 4, KVW])
        q_norm = sb("q_norm", [P, G, KV, HD])
        k_norm = sb("k_norm", [P, KV, HD])
        qT = sb("qT", [P, G, P])
        kT = sb("kT", [P, NT, P])
        vs_raw = [w_raw[:, 1], kT[:, 0:PT, :]]
        sp_sb = sb("sp_sb", [P, 1 + KV, G, 2 * WIN])
        s_sb, p_sb = sp_sb[:, 0], sp_sb[:, 1:]
        pT = sb("pT", [P, 2, G, P])
        raw = ([w_raw[:, b] for b in range(2)] +
               [sp_sb[:, b, :, :].rearrange("p g (a c) -> p (g a) c", c=P) for b in range(1 + KV)] +
               [pT[:, :, :, :].rearrange("p a g c -> p (a g) c")])
        o_sb = sb("o_sb", [P, KV, G, HD])
        mask = sb("mask", [P, 2 * WIN])
        g1 = sb("g1", [P, KD])
        qk_gain = sb("qk_gain", [P, 2])
        k_gain = sb("k_gain", [P, HD])
        sinks = sb("sinks", [P, HEADS])
        minus_half = sb("minus_half", [P, 1])
        xss = sb("xss", [P, NT])
        xrs = sb("xrs", [P, NT])
        qks = sb("qks", [P, HEADS + KV])
        qkr = sb("qkr", [P, HEADS + KV])
        top = sb("top", [P, G])
        ntop = sb("ntop", [P, 2, G])
        sink_d = sb("sink_d", [P, 2, G])
        den = sb("den", [P, 2, G])
        sink_e = sb("sink_e", [P, 2, G])
        rden = sb("rden", [P, G])
        k_out = sb("k_out", [P, KV, HD])
        s_mask_old = w_raw[:, 0].rearrange("p k c -> p (k c)")
        s_mask_new = sb("s_mask_new", [P, NS])
        s_sinks = sb("s_sinks", [P, KV])
        s_scores = [sp_sb[:, :, :, :].rearrange("p a g s -> p (a g s)")[:, kv * SK:(kv + 1) * SK] for kv in range(KV)]
        s_top = sb("s_top", [P, KV, 4])
        v_cache = h_raw[:, :, :, :].rearrange("p a k c -> p (a k) c")
        k_cache = x_in[:, 0, :].rearrange("p (b c) -> p b c", b=DEC_B)
        kT_cache = x_norm
        pT_s = [x_in[:, 1 - kv, :].rearrange("p (b c) -> p b c", b=DEC_B) for kv in range(KV)]
        pT_n = [pT[:, 0, kv, :] for kv in range(KV)]

        const_in = sem("const_in")
        w_in = [sem(f"w_in_{c}") for c in range(NP)]
        g1_in = sem("g1_in")
        x_came = [sem("x_came_even"), sem("x_came_odd")]
        act_step, dve_step, pool_step = sem("act_step"), sem("dve_step"), sem("pool_step")
        masks_made = sem("masks_made")
        ident_made = sem("ident_made")
        gains_made = sem("gains_made")
        w_hi_made, w_lo_made = sem("w_hi_made"), sem("w_lo_made")
        x_squared, x_meaned, x_rstd, x_normed = sem("x_squared"), sem("x_meaned"), sem("x_rstd"), sem("x_normed")
        xT_made = sem("xT_made")
        h_scaled, h_hi_made, h_lo_made = sem("h_scaled"), sem("h_hi_made"), sem("h_lo_made")
        q_made, kv_made = sem("q_made"), sem("kv_made")
        z_copied, z_squared, z_summed, z_rstd, qk_normed = (sem("z_copied"), sem("z_squared"), sem("z_summed"),
                                                             sem("z_rstd"), sem("qk_normed"))
        qkT_made, qkT_copied = sem("qkT_made"), sem("qkT_copied")
        s_made, s_ready, p_made = sem("s_made"), sem("s_ready"), sem("p_made")
        pT_made, pT_copied = sem("pT_made"), sem("pT_copied")
        o_made, o_copied = sem("o_made"), sem("o_copied")
        oT_made, oa_hi_made, oa_lo_made = sem("oT_made"), sem("oa_hi_made"), sem("oa_lo_made")
        k_out_made = sem("k_out_made")
        kv_stored = sem("kv_stored")
        k_out_stored = sem("k_out_stored")
        k_cache_in, v_cache_in = sem("k_cache_in"), sem("v_cache_in")
        cT_made, cT_copied = sem("cT_made"), sem("cT_copied")
        vs_in, vs_hi_made, vs_lo_made = [sem("vs_in_0"), sem("vs_in_1")], sem("vs_hi_made"), sem("vs_lo_made")
        ss_made, ss_ready, sp_made = sem("ss_made"), sem("ss_ready"), sem("sp_made")
        spT_made, spT_copied, so_made, so_copied = sem("spT_made"), sem("spT_copied"), sem("so_made"), sem("so_copied")
        N_CONST = 6 + G * KV
        KT_AT = QKV - AW

        def scores_bank():
            return psum[:, 2:4, :].rearrange("p a (b c) -> p (a b) c", c=2 * WIN)

        def block_keys(t):
            return WIN if t == 0 else 0

        block_ctx = ctx.enter_context(ExitStack())
        block = block_ctx.enter_context(nc.Block())

        @block.sync
        def _(sp):
            def load_x(t):
                if t >= 2:
                    sp.wait_ge(x_normed, t - 1)
                sp.dma_start(x_in[0:rows(t), t % 2, :], io["x"][toks(t), :]).then_inc(x_came[t % 2], DMA)

            load_x(0)
            for c in range(NP):
                sp.dma_start(raw[c], w_src[:, :, c * P:(c + 1) * P]).then_inc(w_in[c], DMA)
            load_x(1)
            for half in range(2):
                part = slice(HD * half, HD * half + HD)
                sp.dma_start(qk_gain[part, 0:1], io["q_norm_g"].rearrange("a d -> d a")).then_inc(const_in, DMA)
                sp.dma_start(qk_gain[part, 1:2], io["k_norm_g"].rearrange("a d -> d a")).then_inc(const_in, DMA)
            sp.dma_start(k_gain[:, :], io["k_norm_g"][0].partition_broadcast(P)).then_inc(const_in, DMA)
            sp.dma_start(sinks[:, :], io["attn_sinks"][0].partition_broadcast(P)).then_inc(const_in, DMA)
            for g in range(G):
                for kv in range(KV):
                    h = kv * G + g
                    sp.dma_start(s_sinks[32 * g:32 * g + 32, kv:kv + 1],
                                  io["attn_sinks"][0, h:h + 1].partition_broadcast(32)).then_inc(const_in, DMA)
            for t in range(2, NT):
                load_x(t)
            for cached, new in (("cache_k", "new_k_s"), ("cache_v", "new_v_s")):
                sp.dma_start(io[new][0, :, 0:WIN - DEC_T], io[cached][0, :, DEC_T:WIN]).then_inc(kv_stored, DMA)
            sp.wait_ge(x_normed, NT)
            sp.dma_start(k_cache, io["cache_k"][0].rearrange("b s k d -> s b (k d)")).then_inc(k_cache_in, DMA)
            sp.wait_ge(h_lo_made, 2 * NT)
            sp.dma_start(v_cache, io["cache_v"][0].rearrange("b s k d -> s b (k d)")).then_inc(v_cache_in, DMA)
            sp.wait_ge(k_out_made, 1)
            sp.dma_start(io["new_k_p"][0, 0].rearrange("s k d -> s (k d)"),
                         k_out[:, :, :].rearrange("p k d -> p (k d)")).then_inc(k_out_stored, DMA)
            sp.wait_ge(z_copied, 2 * PT)
            sp.dma_start(io["new_v_p"][0, 0].rearrange("s k d -> s (k d)"), v_ring[:, (PT - 1) % 4, :]).then_inc(kv_stored, DMA)
            sp.wait_ge(kv_made, NT)
            sp.wait_ge(z_summed, NT)
            sp.wait_ge(s_made, 2 * PT)
            for c in range(4):
                if c >= 2:
                    sp.wait_ge(vs_hi_made, c - 1)
                    sp.wait_ge(vs_lo_made, c - 1)
                sp.dma_start(vs_raw[c % 2], w_src[:, :, OFF_VS + c * P:OFF_VS + (c + 1) * P]).then_inc(vs_in[c % 2], DMA)
            sp.wait_ge(z_copied, 2 * NT)
            for b in range(DEC_B):
                sp.dma_start(io["new_v_s"][0, b, WIN - DEC_T:WIN].rearrange("s k d -> s (k d)"),
                             v_ring[b * DEC_T:(b + 1) * DEC_T, PT % 4, :]).then_inc(kv_stored, DMA)
            sp.wait_ge(k_out_made, 2)
            for b in range(DEC_B):
                sp.dma_start(io["new_k_s"][0, b, WIN - DEC_T:WIN].rearrange("s k d -> s (k d)"),
                             k_out[b * DEC_T:(b + 1) * DEC_T, :, :].rearrange("p k d -> p (k d)")).then_inc(kv_stored, DMA)
            sp.wait_ge(kv_stored, DMA * (3 + 2 * DEC_B))

        @block.gpsimd
        def _(pool):
            step = Step(pool, pool_step)
            step.did(pool.memset(ident[:, :], 0.0))
            pool.affine_select(out=ident[:, :], in_=ident[:, :], compare_op=ALU.not_equal, fill=1.0, base=0,
                               pattern=[[-1, P]], channel_multiplier=1).then_inc(ident_made, 1)
            step.did(pool.memset(minus_half[:, :], -0.5))
            step.did(pool.memset(mask[:, :], 0.0))
            step.did(pool.affine_select(out=mask[:, :], in_=mask[:, :], compare_op=ALU.is_ge, fill=NEG, base=-1,
                                        pattern=[[1, 2 * WIN]], channel_multiplier=-1))
            pool.affine_select(out=mask[:, :], in_=mask[:, :], compare_op=ALU.is_ge, fill=NEG, base=WIN,
                               pattern=[[-1, 2 * WIN]], channel_multiplier=1).then_inc(masks_made, 1)

            def rstd(t):
                pool.wait_ge(x_meaned, t + 1)
                pool.tensor_tensor(xrs[0:rows(t), t:t + 1], xss[0:rows(t), t:t + 1], minus_half[0:rows(t), :],
                                   ALU.pow).then_inc(x_rstd, 1)

            def h_low(t):
                for half in range(2):
                    pool.wait_ge(h_hi_made, 2 * t + half + 1)
                    ks = slice(4 * half, 4 * half + 4)
                    pool.tensor_tensor(hT[1][:, ks, toks(t)], h_raw[:, half, :, 0:rows(t)],
                                       hT[0][:, ks, toks(t)].bitcast(F32), ALU.subtract).then_inc(h_lo_made, 1)

            def z_root(t):
                pool.wait_ge(z_summed, t + 1)
                pool.tensor_tensor(qkr[0:rows(t), :], qks[0:rows(t), :],
                                   minus_half[0:rows(t), 0:1].broadcast_to([rows(t), HEADS + KV]),
                                   ALU.pow).then_inc(z_rstd, 1)

            def sample_mask(g):
                q = slice(32 * g, 32 * g + 32)
                step.did(pool.memset(s_mask_old[q, :], 0.0))
                step.did(pool.memset(s_mask_new[q, :], 0.0))
                old = s_mask_old[q, :].rearrange("p (b s) -> p b s", b=DEC_B)
                new = s_mask_new[q, :].rearrange("p (b j) -> p b j", b=DEC_B)
                for part, n in ((old, WIN), (new, DEC_T)):
                    step.did(pool.affine_select(out=part, in_=part, compare_op=ALU.is_ge, fill=NEG, base=0,
                                                pattern=[[-DEC_T, DEC_B], [0, n]], channel_multiplier=1))
                    step.did(pool.affine_select(out=part, in_=part, compare_op=ALU.is_ge, fill=NEG, base=DEC_T - 1,
                                                pattern=[[DEC_T, DEC_B], [0, n]], channel_multiplier=-1))
                step.did(pool.affine_select(out=old, in_=old, compare_op=ALU.is_ge, fill=NEG, base=-1,
                                            pattern=[[DEC_T, DEC_B], [1, WIN]], channel_multiplier=-1))
                pool.affine_select(out=new, in_=new, compare_op=ALU.is_ge, fill=NEG, base=0,
                                   pattern=[[-DEC_T, DEC_B], [-1, DEC_T]], channel_multiplier=1).then_inc(masks_made, 1)
                pool.wait_ge(masks_made, 2 + g)

            rstd(0)
            h_low(0)
            rstd(1)
            h_low(1)
            z_root(0)
            rstd(2)
            for s in range(1, NT):
                if s + 1 < NT:
                    h_low(s + 1)
                z_root(s)
                if s + 2 < NT:
                    rstd(s + 2)
                if s == 1:
                    pool.wait_ge(w_lo_made, NP)
                if s <= G:
                    pool.wait_ge(z_rstd, s + 1)
                    pool.wait_ge(x_rstd, s + 3)
                    sample_mask(s - 1)

        @block.scalar
        def _(act):
            act.dma_start(g1[:, :], io["norm1_g"][0].rearrange("(k p) -> p k", p=P)).then_inc(g1_in, DMA)

            def square(t):
                n = rows(t)
                act.wait_ge(x_came[t % 2], DMA * (t // 2 + 1))
                if t >= 1:
                    act.wait_ge(xT_made, t)
                act.activation(x_norm[0:n, :], x_in[0:n, t % 2, :], ACT.Square,
                               accum_out=xss[0:n, t:t + 1]).then_inc(x_squared, 1)

            def normalise(t):
                n = rows(t)
                act.wait_ge(x_rstd, t + 1)
                act.activation(x_norm[0:n, :], x_in[0:n, t % 2, :], ACT.Copy,
                               scale=xrs[0:n, t:t + 1]).then_inc(x_normed, 1)

            def h_high(t):
                for half in range(2):
                    act.wait_ge(h_scaled, 2 * t + half + 1)
                    act.activation(hT[0][:, 4 * half:4 * half + 4, toks(t)], h_raw[:, half, :, 0:rows(t)],
                                   ACT.Copy).then_inc(h_hi_made, 1)

            def copy_q(t):
                n = rows(t)
                act.wait_ge(q_made, t + 1)
                if t >= 1:
                    act.wait_ge(qk_normed, 2 * t)
                act.activation(z[0:n, 0:AW], bank(psum, 0)[0:n, 0:AW], ACT.Copy).then_inc(z_copied, 1)

            def copy_kv(t):
                n = rows(t)
                act.wait_ge(kv_made, t + 1)
                act.activation(z[0:n, AW:], bank(psum, 1)[0:n, 0:KVW], ACT.Copy).then_inc(act_step, 1)
                if t >= 4:
                    act.wait_ge(o_made, 2 * (t - 2))
                act.activation(v_ring[0:n, t % 4, :], bank(psum, 1)[0:n, KVW:2 * KVW], ACT.Copy).then_inc(z_copied, 1)
                act.wait_ge(act_step, t + 1)
                act.wait_ge(z_copied, 2 * t + 1)
                act.activation(z_sq[0:n, :], z[0:n, :], ACT.Square).then_inc(z_squared, 1)

            def probs(t, kv):
                u = 2 * t + kv
                k0 = block_keys(t)
                act.wait_ge(s_ready, u + 1)
                if t >= 1:
                    act.wait_ge(pT_made, u - 1)
                    act.wait_ge(o_copied, u - 1)
                for g in range(G):
                    act.activation(p_sb[:, kv, g, k0:], s_sb[:, g, k0:], ACT.Exp, bias=ntop[:, kv, g:g + 1],
                                   accum_out=den[:, kv, g:g + 1])
                act.activation(sink_e[:, kv, :], sink_d[:, kv, :], ACT.Exp).then_inc(p_made, 1)

            def oa_high(t):
                act.wait_ge(oT_made, t + 1)
                act.activation(oaT[0][:, :, toks(t)], bank(psum, 4).rearrange("p (k c) -> p k c", k=KE)[:, :, 0:rows(t)],
                               ACT.Copy).then_inc(oa_hi_made, 1)

            square(0)
            normalise(0)
            for c in range(NP):
                act.wait_ge(w_in[c], DMA)
                act.activation(w_hi[:, :, c * P:(c + 1) * P], raw[c], ACT.Copy).then_inc(w_hi_made, 1)
                if c == 1:
                    h_high(0)
            square(1)
            normalise(1)
            copy_q(0)
            h_high(1)
            copy_kv(0)
            square(2)
            for s in range(1, NT + 1):
                t, done = s - 1, s - 2
                if done >= 0:
                    probs(done, 1)
                if s + 1 < NT:
                    normalise(s + 1)
                if s < NT:
                    copy_q(s)
                if 0 <= done < PT - 1:
                    oa_high(done)
                if t < PT:
                    probs(t, 0)
                if s + 1 < NT:
                    h_high(s + 1)
                if s < NT:
                    copy_kv(s)
                if s + 2 < NT:
                    square(s + 2)
            def vs_high(c):
                act.wait_ge(vs_in[c % 2], DMA * (c // 2 + 1))
                act.activation(w_hi[:, :, c * P:(c + 1) * P], vs_raw[c % 2], ACT.Copy).then_inc(vs_hi_made, 1)

            vs_high(0)
            vs_high(1)
            for kv in range(KV):
                act.wait_ge(ss_ready, kv + 1)
                act.activation(s_scores[kv], s_scores[kv], ACT.Exp, bias=ntop[:, kv, 0:1], accum_out=den[:, kv, 0:1])
                act.activation(sink_e[:, kv, 0:1], s_sinks[:, kv:kv + 1], ACT.Exp, bias=ntop[:, kv, 0:1]).then_inc(sp_made, 1)
            oa_high(PT - 1)
            vs_high(2)
            vs_high(3)
            oa_high(PT)

        @block.tensor
        def _(pe):
            pe.wait_ge(ident_made, 1)

            def x_turn(t):
                n = rows(t)
                pe.wait_ge(x_normed, t + 1)
                if t >= 1:
                    pe.wait_ge(h_scaled, 2 * t)
                if t >= 3:
                    pe.wait_ge(pT_copied, 2 * (t - 2))
                for half in range(2):
                    for k in range(4):
                        mm = pe.transpose(bank(psum, 6 + half)[:, k * P:k * P + n],
                                          x_norm[0:n, (4 * half + k) * P:(4 * half + k + 1) * P], ident[0:n, 0:n])
                mm.then_inc(xT_made, 1)

            def project_q(t, half):
                n = rows(t)
                pe.wait_ge(h_hi_made, 2 * t + half + 1)
                pe.wait_ge(h_lo_made, 2 * t + half + 1)
                pe.wait_ge(w_hi_made, AW // P)
                pe.wait_ge(w_lo_made, AW // P)
                if t >= 1:
                    pe.wait_ge(z_copied, 2 * t - 1)
                h = half * (KD // 2)
                mm = product(pe, bank(psum, 0)[0:n, 0:AW], lambda k: (hT[0][:, h + k, toks(t)], hT[1][:, h + k, toks(t)]),
                             lambda k: (w_hi[:, h + k, 0:AW], w_lo[:, h + k, 0:AW]), KD // 2, first=half == 0, last=half == 1)
                if half == 1:
                    mm.then_inc(q_made, 1)

            def project_kv(t):
                n = rows(t)
                pe.wait_ge(w_hi_made, NP)
                pe.wait_ge(w_lo_made, NP)
                if t >= 1:
                    pe.wait_ge(z_copied, 2 * t)
                    pe.wait_ge(qkT_copied, 2 * t)
                product(pe, bank(psum, 1)[0:n, 0:QKV - AW], lambda k: (hT[0][:, k, toks(t)], hT[1][:, k, toks(t)]),
                        lambda k: (w_hi[:, k, AW:], w_lo[:, k, AW:]), KD).then_inc(kv_made, 1)

            def qk_turn(t):
                n = rows(t)
                pe.wait_ge(qk_normed, 2 * t + 2)
                if t >= 2:
                    pe.wait_ge(oa_lo_made, t - 1)
                for g in range(G):
                    pe.transpose(bank(psum, 4)[:, g * P:g * P + n], q_norm[0:n, g, :, :].rearrange("p k d -> p (k d)"),
                                 ident[0:n, 0:n])
                pe.transpose(bank(psum, 1)[:, KT_AT:KT_AT + n], k_norm[0:n, :, :].rearrange("p k d -> p (k d)"),
                             ident[0:n, 0:n]).then_inc(qkT_made, 1)

            def scores(t, kv):
                u = 2 * t + kv
                k0 = block_keys(t)
                head = slice(HD * kv, HD * kv + HD)
                pe.wait_ge(qkT_copied, 2 * t + 2)
                if u >= 1:
                    pe.wait_ge(s_ready, u)
                keys = kT[:, :, :].rearrange("p a b -> p (a b)")[head, (t - 1) * P + k0:(t + 1) * P]
                for g in range(G):
                    mm = pe.matmul(scores_bank()[:, g, k0:], qT[head, g, :], keys, start=True, stop=True)
                mm.then_inc(s_made, 1)

            def probs_turn(t, kv):
                u = 2 * t + kv
                pe.wait_ge(p_made, u + 1)
                if u >= 1:
                    pe.wait_ge(pT_copied, u)
                if kv == 0:
                    pe.wait_ge(h_scaled, 2 * min(t + 3, NT))
                    if t == PT - 1:
                        pe.wait_ge(cT_copied, 2)
                for half in range(block_keys(t) // WIN, 2):
                    for g in range(G):
                        mm = pe.transpose(bank(psum, 6 + half)[:, g * P:(g + 1) * P],
                                          p_sb[:, kv, g, half * WIN:(half + 1) * WIN], ident[:, :])
                mm.then_inc(pT_made, 1)

            def values(t, kv):
                u = 2 * t + kv
                pe.wait_ge(pT_copied, u + 1)
                pe.wait_ge(z_copied, 2 * t + 2)
                if u >= 1:
                    pe.wait_ge(o_copied, u)
                first = block_keys(t) // WIN
                for g in range(G):
                    for half in range(first, 2):
                        mm = pe.matmul(bank(psum, 5)[:, g * HD:(g + 1) * HD], pT[:, half, g, :],
                                       v_ring[:, (t - 1 + half) % 4, kv * HD:(kv + 1) * HD],
                                       start=half == first, stop=half == 1)
                mm.then_inc(o_made, 1)

            def o_turn(t):
                n = rows(t)
                pe.wait_ge(o_copied, 2 * t + 2)
                pe.wait_ge(qkT_copied, 2 * t + 4)
                flat = o_sb[:, :, :, :].rearrange("p k g d -> p (k g d)")
                for c in range(KE):
                    mm = pe.transpose(bank(psum, 4)[:, c * P:c * P + n], flat[0:n, c * P:(c + 1) * P], ident[0:n, 0:n])
                mm.then_inc(oT_made, 1)

            def cache_turn():
                pe.wait_ge(k_cache_in, DMA)
                pe.wait_ge(pT_copied, 2 * (PT - 1))
                for b in range(DEC_B):
                    mm = pe.transpose(bank(psum, 6 + b // 4)[:, (b % 4) * P:(b % 4 + 1) * P], k_cache[:, b, :], ident[:, :])
                mm.then_inc(cT_made, 1)

            def sample_scores():
                pe.wait_ge(qkT_copied, 2 * NT)
                pe.wait_ge(s_ready, 2 * PT)
                pe.wait_ge(pT_copied, 2 * PT)
                for kv in range(KV):
                    head = slice(HD * kv, HD * kv + HD)
                    q_all = qT[head, 0, :]
                    for c in range(2):
                        pe.matmul(bank(psum, 2 + 4 * kv + c), q_all, kT_cache[head, c * 512:(c + 1) * 512], start=True,
                                  stop=True)
                    pe.matmul(bank(psum, 1 - kv)[:, 0:NS], q_all, kT[head, PT, 0:NS], start=True, stop=True).then_inc(ss_made, 1)

            x_turn(0)
            for half in range(2):
                project_q(0, half)
            x_turn(1)
            project_kv(0)
            for s in range(1, NT + 1):
                t, done = s - 1, s - 2
                if done >= 0:
                    probs_turn(done, 0)
                if s < NT:
                    project_q(s, 0)
                if done >= 0:
                    values(done, 0)
                    probs_turn(done, 1)
                if s < NT:
                    project_q(s, 1)
                qk_turn(t)
                if done >= 0:
                    values(done, 1)
                if t < PT:
                    scores(t, 0)
                else:
                    sample_scores()
                if done >= 0:
                    o_turn(done)
                if s + 1 < NT:
                    x_turn(s + 1)
                elif s < NT:
                    cache_turn()
                if s < NT:
                    project_kv(s)
                if t < PT:
                    scores(t, 1)
            for kv in range(KV):
                pe.wait_ge(sp_made, kv + 1)
                for b in range(DEC_B):
                    pe.transpose(bank(psum, 2 + 4 * kv + b // 4)[:, (b % 4) * P:(b % 4 + 1) * P],
                                 s_scores[kv][:, b * WIN:(b + 1) * WIN], ident[:, :])
                pe.transpose(bank(psum, 1 - kv)[0:NS, 0:P], s_scores[kv][:, DEC_B * WIN:], ident[:, :]).then_inc(spT_made, 1)
            pe.wait_ge(v_cache_in, DMA)
            for kv in range(KV):
                pe.wait_ge(spT_copied, kv + 1)
                if kv == 1:
                    pe.wait_ge(oa_lo_made, PT)
                for b in range(DEC_B):
                    pe.matmul(bank(psum, 5 - kv)[:, 0:HD], pT_s[kv][:, b, :], v_cache[:, b, kv * HD:(kv + 1) * HD],
                              start=b == 0, stop=False)
                pe.matmul(bank(psum, 5 - kv)[:, 0:HD], pT_n[kv][0:NS, :], v_ring[0:NS, PT % 4, kv * HD:(kv + 1) * HD],
                          start=False, stop=True).then_inc(so_made, 1)
            pe.wait_ge(so_copied, 2)
            flat = o_sb[:, :, :, :].rearrange("p k g d -> p (k g d)")
            for c in range(KE):
                mm = pe.transpose(bank(psum, 4)[:, c * P:c * P + NS], flat[0:NS, c * P:(c + 1) * P], ident[0:NS, 0:NS])
            mm.then_inc(oT_made, 1)

        @block.vector
        def _(dve):
            step = Step(dve, dve_step)

            def mean_square(t):
                n = rows(t)
                dve.wait_ge(x_squared, t + 1)
                dve.tensor_scalar(xss[0:n, t:t + 1], xss[0:n, t:t + 1], 1.0 / D, EPS, ALU.mult,
                                  ALU.add).then_inc(x_meaned, 1)

            def h_scale(t):
                n = rows(t)
                dve.wait_ge(xT_made, t + 1)
                if t >= 1:
                    dve.wait_ge(h_lo_made, 2 * t)
                for half in range(2):
                    ks = slice(4 * half, 4 * half + 4)
                    dve.tensor_tensor(h_raw[:, half, :, 0:n],
                                      bank(psum, 6 + half).rearrange("p (k c) -> p k c", k=4)[:, :, 0:n],
                                      g1[:, ks].unsqueeze(2).broadcast_to([P, 4, n]), ALU.mult).then_inc(h_scaled, 1)

            def qk_squares(t):
                n = rows(t)
                dve.wait_ge(z_squared, t + 1)
                step.did(dve.tensor_reduce(qks[0:n, :], z_sq[0:n, :].rearrange("p (h d) -> p h d", d=HD), AX_X, ALU.add))
                dve.tensor_scalar(qks[0:n, :], qks[0:n, :], 1.0 / HD, EPS, ALU.mult, ALU.add).then_inc(z_summed, 1)

            def qk_scale(t):
                n = rows(t)
                zz = z[0:n, :].rearrange("p (h d) -> p h d", d=HD)
                dve.wait_ge(z_rstd, t + 1)
                if t >= 1:
                    dve.wait_ge(qkT_made, t)
                dve.tensor_tensor(q_norm[0:n, :, :, :].rearrange("p g k d -> p k g d"),
                                  zz[:, 0:HEADS, :].rearrange("p (k g) d -> p k g d", k=KV),
                                  qkr[0:n, 0:HEADS].rearrange("p (k g) -> p k g", k=KV).unsqueeze(3)
                                  .broadcast_to([n, KV, G, HD]), ALU.mult).then_inc(qk_normed, 1)
                dve.tensor_tensor(k_norm[0:n, :, :], zz[:, HEADS:, :],
                                  qkr[0:n, HEADS:].unsqueeze(2).broadcast_to([n, KV, HD]), ALU.mult).then_inc(qk_normed, 1)
                if t == PT:
                    dve.wait_ge(k_out_stored, DMA)
                if t >= PT - 1:
                    dve.wait_ge(qk_normed, 2 * t + 2)
                    dve.tensor_tensor(k_out[0:n, :, :], k_norm[0:n, :, :],
                                      k_gain[0:n, :].unsqueeze(1).broadcast_to([n, KV, HD]), ALU.mult).then_inc(k_out_made, 1)

            def qk_copy(t):
                n = rows(t)
                dve.wait_ge(qkT_made, t + 1)
                if t >= 1:
                    dve.wait_ge(s_made, 2 * t)
                if t < PT:
                    out = qT[:, :, 0:n]
                else:
                    out = qT[:, 0, :].rearrange("p (g n) -> p g n", g=G)
                dve.tensor_scalar(out, bank(psum, 4).rearrange("p (g n) -> p g n", g=G)[:, :, 0:n], qk_gain[:, 0:1],
                                  HD ** -0.5, ALU.mult, ALU.mult).then_inc(qkT_copied, 1)
                dve.tensor_scalar(kT[:, t, 0:n], bank(psum, 1)[:, KT_AT:KT_AT + n], qk_gain[:, 1:2], None,
                                  ALU.mult).then_inc(qkT_copied, 1)

            def mask_scores(t, kv):
                u = 2 * t + kv
                k0 = block_keys(t)
                dve.wait_ge(s_made, u + 1)
                if u >= 1:
                    dve.wait_ge(p_made, u)
                for g in range(G):
                    ins = dve.tensor_tensor_reduce(s_sb[:, g, k0:], scores_bank()[:, g, k0:], mask[:, k0:], 1.0, NEG,
                                                   ALU.add, ALU.max, top[:, g:g + 1])
                step.did(ins)
                sink = sinks[:, kv * G:(kv + 1) * G]
                step.did(dve.tensor_tensor(top[:, :], top[:, :], sink, ALU.max))
                step.did(dve.tensor_scalar(ntop[:, kv, :], top[:, :], -1.0, None, ALU.mult))
                dve.tensor_tensor(sink_d[:, kv, :], sink, ntop[:, kv, :], ALU.add).then_inc(s_ready, 1)

            def pT_copy(t, kv):
                u = 2 * t + kv
                dve.wait_ge(pT_made, u + 1)
                if u >= 1:
                    dve.wait_ge(o_made, u)
                first = block_keys(t) // WIN
                for half in range(first, 2):
                    ins = dve.tensor_copy(pT[:, half, :, :].rearrange("p g c -> p (g c)"), bank(psum, 6 + half))
                ins.then_inc(pT_copied, 1)

            def o_scale(t, kv):
                u = 2 * t + kv
                if u >= 1:
                    dve.wait_ge(o_copied, u)
                step.did(dve.tensor_tensor(rden[:, :], den[:, kv, :], sink_e[:, kv, :], ALU.add))
                step.did(dve.reciprocal(rden[:, :], rden[:, :]))
                dve.wait_ge(o_made, u + 1)
                if t >= 1:
                    dve.wait_ge(oT_made, t)
                dve.tensor_tensor(o_sb[:, kv, :, :], bank(psum, 5)[:, 0:G * HD].rearrange("p (g d) -> p g d", g=G),
                                  rden[:, :].unsqueeze(2).broadcast_to([P, G, HD]), ALU.mult).then_inc(o_copied, 1)

            def oa_low(t):
                dve.wait_ge(oa_hi_made, t + 1)
                dve.tensor_tensor(oaT[1][:, :, toks(t)],
                                  bank(psum, 4).rearrange("p (k c) -> p k c", k=KE)[:, :, 0:rows(t)],
                                  oaT[0][:, :, toks(t)].bitcast(F32), ALU.subtract).then_inc(oa_lo_made, 1)

            mean_square(0)
            dve.wait_ge(g1_in, DMA)
            h_scale(0)
            for c in range(NP):
                dve.wait_ge(w_hi_made, c + 1)
                dve.tensor_tensor(w_lo[:, :, c * P:(c + 1) * P], raw[c],
                                  w_hi[:, :, c * P:(c + 1) * P].bitcast(F32), ALU.subtract).then_inc(w_lo_made, 1)
            mean_square(1)
            dve.wait_ge(masks_made, 1)
            dve.wait_ge(const_in, DMA * N_CONST)
            dve.wait_ge(w_lo_made, NP)
            h_scale(1)
            qk_squares(0)
            mean_square(2)
            for s in range(1, NT + 1):
                t, done = s - 1, s - 2
                if done >= 0:
                    pT_copy(done, 0)
                    o_scale(done, 0)
                    pT_copy(done, 1)
                qk_scale(t)
                qk_copy(t)
                if done >= 0:
                    o_scale(done, 1)
                if t < PT:
                    mask_scores(t, 0)
                if 0 <= done < PT - 1:
                    oa_low(done)
                if s + 1 < NT:
                    h_scale(s + 1)
                elif s < NT:
                    dve.wait_ge(cT_made, 1)
                    for half in range(2):
                        dve.tensor_copy(kT_cache[:, half * 512:(half + 1) * 512], bank(psum, 6 + half)).then_inc(cT_copied, 1)
                if t < PT:
                    mask_scores(t, 1)
                if s < NT:
                    qk_squares(s)
                if s + 2 < NT:
                    mean_square(s + 2)
            def vs_low(c):
                dve.wait_ge(vs_hi_made, c + 1)
                dve.tensor_tensor(w_lo[:, :, c * P:(c + 1) * P], vs_raw[c % 2],
                                  w_hi[:, :, c * P:(c + 1) * P].bitcast(F32), ALU.subtract).then_inc(vs_lo_made, 1)

            dve.wait_ge(masks_made, 1 + G)
            for kv in range(KV):
                dve.tensor_copy(s_top[:, kv, 3:4], s_sinks[:, kv:kv + 1])
                dve.wait_ge(ss_made, kv + 1)
                for c in range(2):
                    part = slice(c * 512, (c + 1) * 512)
                    dve.tensor_tensor_reduce(s_scores[kv][:, part], bank(psum, 2 + 4 * kv + c), s_mask_old[:, part], 1.0, NEG,
                                             ALU.add, ALU.max, s_top[:, kv, c:c + 1])
                step.did(dve.tensor_tensor_reduce(s_scores[kv][:, DEC_B * WIN:], bank(psum, 1 - kv)[:, 0:NS], s_mask_new[:, :],
                                                  1.0, NEG, ALU.add, ALU.max, s_top[:, kv, 2:3]))
                step.did(dve.tensor_reduce(top[:, kv:kv + 1], s_top[:, kv, :], AX_X, ALU.max))
                dve.tensor_scalar(ntop[:, kv, 0:1], top[:, kv:kv + 1], -1.0, None, ALU.mult).then_inc(ss_ready, 1)
            vs_low(0)
            dve.wait_ge(o_copied, 2 * PT)
            for kv in range(KV):
                dve.wait_ge(spT_made, kv + 1)
                for half in range(2):
                    dve.tensor_copy(pT_s[kv][:, 4 * half:4 * half + 4, :].rearrange("p b c -> p (b c)"),
                                    bank(psum, 2 + 4 * kv + half))
                dve.tensor_copy(pT_n[kv][0:NS, :], bank(psum, 1 - kv)[0:NS, 0:P]).then_inc(spT_copied, 1)
                step.did(dve.tensor_tensor(rden[:, kv:kv + 1], den[:, kv, 0:1], sink_e[:, kv, 0:1], ALU.add))
                step.did(dve.reciprocal(rden[:, kv:kv + 1], rden[:, kv:kv + 1]))
            oa_low(PT - 1)
            vs_low(1)
            for kv in range(KV):
                dve.wait_ge(so_made, kv + 1)
                for g in range(G):
                    q = slice(32 * g, 32 * g + 32)
                    ins = dve.tensor_scalar(o_sb[0:NS, kv, g, :], bank(psum, 5 - kv)[q, 0:HD], rden[q, kv:kv + 1], None,
                                            ALU.mult)
                ins.then_inc(so_copied, 1)
            vs_low(2)
            vs_low(3)
            oa_low(PT)

        block_ctx.close()
        with nc.Block() as clearing:
            def clear(eng, first):
                for s in used[first::4]:
                    eng.sem_clear(s)

            @clearing.gpsimd
            def _(pool):
                clear(pool, 0)

            @clearing.scalar
            def _(act):
                clear(act, 1)

            @clearing.vector
            def _(dve):
                clear(dve, 2)

            @clearing.sync
            def _(sp):
                clear(sp, 3)


def sgu_values_phase(nc, io, keep, psum):
    ident, hT, mixT = keep["ident"], (keep["hT_hi"], keep["hT_lo"]), keep["mixT"]
    w_hi, w_lo, first_u = keep["w_hi"], keep["w_lo"], keep["first_u"]
    w_src = io["w_in"][0].rearrange("(k p) c -> p k c", p=P)

    with ExitStack() as ctx:
        def sb(name, shape, dt=F32):
            return ctx.enter_context(nc.sbuf_tensor(name, shape, dt))

        def sem(name):
            return keep["semaphores"].enter_context(nc.semaphore("v_" + name))

        act_v = sb("act_v", [P, 2, SW])
        vs = sb("vs", [P, 2, SW])
        stats = sb("stats", [P, 6])
        mean_var = sb("mean_var", [P, 2])
        rstd = sb("rstd", [P, 1])
        minus_half = sb("v_minus_half", [P, 1])
        ln_g, ln_b, w_mix = (keep["first_g"][0][:, n * SG:(n + 1) * SG, :] for n in range(3))
        w_mixT = sb("w_mixT", [P, SG, P])
        b_mix = sb("b_mix", [P, SG, P])


        w_mixT_s = keep["lg"][0:NS, :, :].rearrange("p t n -> p (t n)")[:, 0:SG * NS].rearrange("p (h n) -> p h n", h=SG)

        b_mix_s = sb("b_mix_s", [P, SG, DEC_T])

        const_in, zeroed, blocks_in = sem("const_in"), sem("zeroed"), sem("blocks_in")
        first_in, first_hi_made, first_lo_made = sem("first_in"), sem("first_hi_made"), sem("first_lo_made")
        v_made, v_gelu, v_stats, v_rstd, v_norm, v_gain, vs_made = (
            sem("made"), sem("gelu"), sem("stats"), sem("rstd"), sem("norm"), sem("gain"), sem("vs_made"))
        dve_step, mixed, mix_added = sem("dve_step"), sem("mixed"), sem("mix_added")
        mixT_turned, mixT_copied, mix_ready = sem("mixT_turned"), sem("mixT_copied"), sem("mix_ready")
        vs_stored = sem("vs_stored")
        N_CONST = 5
        block = ctx.enter_context(nc.Block())

        @block.sync
        def _(sp):
            sp.dma_start(first_u[0][:, :, :], w_src[:, :, QKV:QKV + P]).then_inc(first_in, DMA)
            sp.wait_ge(zeroed, 1)
            for b in range(DEC_B):
                r = slice(b * DEC_T, (b + 1) * DEC_T)
                for h in range(SG):
                    sp.dma_start(w_mixT_s[r, h, r],
                                 io["w_spatial"][0, h, 0:DEC_T, 0:DEC_T].rearrange("i j -> j i")).then_inc(blocks_in, DMA)
            sp.wait_ge(vs_made, NT)
            sp.dma_start(io["new_vs"].rearrange("a b t g c -> (a b t) (g c)"), vs[0:NS, PT % 2, :]).then_inc(vs_stored, DMA)
            sp.wait_ge(vs_stored, DMA)

        @block.gpsimd
        def _(pool):
            pool.memset(w_mixT_s[:, :, :], 0.0).then_inc(zeroed, 1)
            pool.memset(minus_half[:, :], -0.5).then_inc(zeroed, 1)
            pool.wait_ge(mixT_copied, 1)
            pool.affine_select(out=w_mixT[:, :, :], in_=w_mixT[:, :, :], compare_op=ALU.is_ge, fill=0.0, base=0,
                               pattern=[[0, SG], [1, P]], channel_multiplier=-1).then_inc(mix_ready, 1)
            pool.wait_ge(mix_ready, 1)
            pool.wait_ge(zeroed, 2)
            pool.wait_ge(const_in, DMA * N_CONST)
            for t in range(NT):
                n = rows(t)
                if t == PT - 1:
                    pool.wait_ge(vs_made, t)
                    pool.wait_ge(blocks_in, DMA * DEC_B * SG)
                    pool.affine_select(out=w_mixT_s[:, :, :], in_=w_mixT_s[:, :, :], compare_op=ALU.is_ge, fill=0.0, base=0,
                                       pattern=[[0, SG], [1, NS]], channel_multiplier=-1).then_inc(mix_ready, 1)
                    pool.wait_ge(mix_ready, 2)
                pool.wait_ge(v_stats, t + 1)
                pool.tensor_tensor(rstd[0:n, :], mean_var[0:n, 1:2], minus_half[0:n, :], ALU.pow).then_inc(v_rstd, 1)
                pool.wait_ge(v_norm, t + 1)
                out, a = (b[0:n, t % 2, :].rearrange("p (h c) -> p h c", h=SG) for b in (vs, act_v))
                pool.tensor_tensor(out, a, ln_g[0:n], ALU.mult).then_inc(v_gain, 1)
                pool.wait_ge(v_gain, t + 1)
                pool.tensor_tensor(out, out, ln_b[0:n], ALU.add).then_inc(vs_made, 1)

        @block.scalar
        def _(act):
            act.dma_start(w_mix, io["w_spatial"][0].rearrange("h i j -> i h j")).then_inc(const_in, DMA)
            for out, name in ((ln_g, "ln_v_g"), (ln_b, "ln_v_b")):
                act.dma_start(out, io[name][0].rearrange("(h c) -> h c", h=SG).partition_broadcast(P)).then_inc(const_in, DMA)
            act.dma_start(b_mix[:, :, :], io["b_spatial"][0].partition_broadcast(P)).then_inc(const_in, DMA)
            act.dma_start(b_mix_s[:, :, :], io["b_spatial"][0, :, 0:DEC_T].partition_broadcast(P)).then_inc(const_in, DMA)
            act.wait_ge(first_in, DMA)
            act.activation(first_u[1][:, :, :], first_u[0][:, :, :], ACT.Copy).then_inc(first_hi_made, 1)
            for t in range(NT):
                n = rows(t)
                act.wait_ge(v_made, t + 1)
                if t >= 2:
                    act.wait_ge(v_gain, t - 1)
                act.activation(act_v[0:n, t % 2, :], bank(psum, t % 2)[0:n, :], ACT.Gelu_apprx_tanh).then_inc(v_gelu, 1)

        @block.tensor
        def _(pe):
            def mix(t):
                n = rows(t)
                pe.wait_ge(vs_made, t + 1)
                pe.wait_ge(mix_ready, 1 if t < PT else 2)
                if t >= 2:
                    pe.wait_ge(mix_added, t - 1)
                w = w_mixT if t < PT else w_mixT_s
                for h in range(SG):
                    mm = pe.matmul(bank(psum, 2 + t % 2)[:, h * P:h * P + n], vs[0:n, t % 2, h * P:(h + 1) * P],
                                   w[0:n, h, 0:n], start=True, stop=True)
                mm.then_inc(mixed, 1)

            for t in range(NT):
                if t >= 2:
                    pe.wait_ge(v_gelu, t - 1)
                product(pe, bank(psum, t % 2)[0:rows(t), :], lambda k: (hT[0][:, k, toks(t)], hT[1][:, k, toks(t)]),
                        lambda k: (w_hi[:, k, 0:SW], w_lo[:, k, 0:SW]), KD).then_inc(v_made, 1)
                if t == 0:
                    pe.wait_ge(const_in, DMA * N_CONST)
                    for h in range(SG):
                        mm = pe.transpose(bank(psum, 4)[:, h * P:(h + 1) * P], w_mix[:, h, :], ident[:, :])
                    mm.then_inc(mixT_turned, 1)
                else:
                    mix(t - 1)
            mix(PT)

        @block.vector
        def _(dve):
            step = Step(dve, dve_step)
            dve.wait_ge(first_hi_made, 1)
            dve.tensor_tensor(first_u[2][:, :, :], first_u[0][:, :, :], first_u[1][:, :, :].bitcast(F32),
                              ALU.subtract).then_inc(first_lo_made, 1)
            dve.wait_ge(mixT_turned, 1)
            dve.tensor_copy(w_mixT[:, :, :], bank(psum, 4).rearrange("p (h i) -> p h i", h=SG)).then_inc(mixT_copied, 1)
            dve.wait_ge(const_in, DMA * N_CONST)

            def add_bias(t):
                n = rows(t)
                dve.wait_ge(mixed, t + 1)
                out, sums = mixT[:, :, toks(t)], bank(psum, 2 + t % 2).rearrange("p (h i) -> p h i", h=SG)[:, :, 0:n]
                add = b_mix[:, :, :]
                if t == PT:
                    out, sums = (a.rearrange("p h (b t) -> p h b t", b=DEC_B) for a in (out, sums))
                    add = b_mix_s[:, :, :].unsqueeze(2).broadcast_to([P, SG, DEC_B, DEC_T])
                dve.tensor_tensor(out, sums, add, ALU.add).then_inc(mix_added, 1)

            for t in range(NT):
                n = rows(t)
                a = act_v[0:n, t % 2, :]
                dve.wait_ge(v_gelu, t + 1)
                step.did(dve.bn_stats(stats[0:n, :], a))
                if t >= 1:
                    dve.wait_ge(v_norm, t)
                step.did(dve.bn_aggr(mean_var[0:n, :], stats[0:n, :]))
                dve.tensor_scalar(mean_var[0:n, 1:2], mean_var[0:n, 1:2], EPS, None, ALU.add).then_inc(v_stats, 1)
                dve.wait_ge(v_rstd, t + 1)
                if t >= 2:
                    dve.wait_ge(mixed, t - 1)
                dve.tensor_scalar(a, a, mean_var[0:n, 0:1], rstd[0:n, 0:1], ALU.subtract, ALU.mult).then_inc(v_norm, 1)
                if t >= 1:
                    add_bias(t - 1)
            add_bias(PT)


def sgu_gate_phase(nc, io, keep, psum):
    first_g = keep["first_g"]
    hT, mixT, obT = (keep["hT_hi"], keep["hT_lo"]), keep["mixT"], (keep["obT_hi"], keep["obT_lo"])
    w_src = io["w_in"][0].rearrange("(k p) c -> p k c", p=P)

    with ExitStack() as ctx:
        def sb(name, shape, dt=F32):
            return ctx.enter_context(nc.sbuf_tensor(name, shape, dt))

        def sem(name):
            return keep["semaphores"].enter_context(nc.semaphore("u_" + name))

        behind = [keep["behind_" + name][:, 0:KD * P].rearrange("p (k c) -> p k c", k=KD) for name in ("obT_hi", "obT_lo")]
        weights = [keep["first_u"], [sb("u_w_raw", [P, KD, P])] + behind]
        u_act = sb("u_act", [P, 2, TC])
        ob = sb("ob", [P, 2, TC])
        w_in = [sem("w_in_even"), sem("w_in_odd")]
        w_hi_made, w_lo_made = Flow(sem("w_hi_made")), Flow(sem("w_lo_made"))
        u_made, u_gelu, ob_made = Flow(sem("made"), 6), Flow(sem("gelu")), Flow(sem("ob_made"))
        hi_made, lo_made = Flow(sem("hi_made")), Flow(sem("lo_made"))
        first_in, first_hi_made, first_lo_made = sem("first_in"), sem("first_hi_made"), sem("first_lo_made")
        block = ctx.enter_context(nc.Block())

        def over_chunks(eng, step):
            step(0, 0)
            with eng.Fori(0, KE // 2 - 1) as i:
                step(2 * i + 1, 1)
                step(2 * i + 2, 0)
            step(KE - 1, 1)

        def is_last(q):
            return isinstance(q, int) and q == KE - 1

        def next_chunk(q, j, step):
            if not is_last(q):
                step(q + 1, 1 - j)

        @block.sync
        def _(sp):
            def load(q, j):
                w_hi_made.wait(sp, q - 2)
                w_lo_made.wait(sp, q - 2)
                sp.dma_start(weights[j][0][:, :, :], w_src[:, :, bass.ds(q * P + QKV, P)]).then_inc(w_in[j], DMA)

            sp.dma_start(first_g[0][:, 0:KD], w_src[:, :, OFF_GA:OFF_GA + P]).then_inc(first_in, DMA)
            sp.dma_start(first_g[0][:, KD:], io["w_branch_a"][0].rearrange("(k p) c -> p k c", p=P)[:, :, 0:P]).then_inc(first_in, DMA)
            over_chunks(sp, lambda q, j: next_chunk(q, j, load))

        @block.gpsimd
        def _(pool):
            lo_made.begin(pool)

            def step(q, j):
                for c in range(3):
                    u = 3 * q + c
                    hi_made.wait(pool, u)
                    part = slice(c * TC, (c + 1) * TC)
                    pool.tensor_tensor(obT[1][:, bass.ds(q, 1), part], ob[:, (j + c) % 2, :].unsqueeze(1),
                                       obT[0][:, bass.ds(q, 1), part].bitcast(F32), ALU.subtract).then_inc(lo_made.sem, 1)

            over_chunks(pool, step)

        @block.scalar
        def _(act):
            w_hi_made.begin(act)
            u_gelu.begin(act)
            hi_made.begin(act)
            act.sem_inc(w_hi_made.sem, 1)

            def high(q, j):
                act.wait_ge(w_in[j], (q + j) * (DMA // 2))
                u_made.wait(act, 3 * q - 4)
                act.activation(weights[j][1][:, :, :], weights[j][0][:, :, :], ACT.Copy).then_inc(w_hi_made.sem, 1)

            def step(q, j):
                next_chunk(q, j, high)
                if is_last(q):
                    act.wait_ge(first_in, 2 * DMA)
                    act.activation(first_g[1][:, :, :], first_g[0][:, :, :], ACT.Copy).then_inc(first_hi_made, 1)
                for c in range(3):
                    u, b = 3 * q + c, (j + c) % 2
                    u_made.wait(act, u)
                    ob_made.wait(act, u - 2)
                    act.activation(u_act[:, b, :], bank(psum, b)[:, 0:TC], ACT.Gelu_apprx_tanh).then_inc(u_gelu.sem, 1)
                    ob_made.wait(act, u)
                    act.activation(obT[0][:, bass.ds(q, 1), c * TC:(c + 1) * TC], ob[:, b, :].unsqueeze(1),
                                   ACT.Copy).then_inc(hi_made.sem, 1)

            over_chunks(act, step)

        @block.tensor
        def _(pe):
            u_made.begin(pe)

            def step(q, j):
                _, hi, lo = weights[j]
                w_hi_made.wait(pe, q)
                w_lo_made.wait(pe, q)
                for c in range(3):
                    u = 3 * q + c
                    u_gelu.wait(pe, u - 2)
                    part = slice(c * TC, (c + 1) * TC)
                    product(pe, bank(psum, (j + c) % 2)[:, 0:TC], lambda k: (hi[:, k, :], lo[:, k, :]),
                            lambda k: (hT[0][:, k, part], hT[1][:, k, part]), KD).then_inc(u_made.sem, 1)

            over_chunks(pe, step)

        @block.vector
        def _(dve):
            w_lo_made.begin(dve)
            ob_made.begin(dve)
            dve.sem_inc(w_lo_made.sem, 1)

            def low(q, j):
                raw, hi, lo = weights[j]
                w_hi_made.wait(dve, q)
                u_made.wait(dve, 3 * q - 4)
                dve.tensor_tensor(lo[:, :, :], raw[:, :, :], hi[:, :, :].bitcast(F32), ALU.subtract).then_inc(w_lo_made.sem, 1)

            def step(q, j):
                next_chunk(q, j, low)
                if is_last(q):
                    dve.wait_ge(first_hi_made, 1)
                    dve.tensor_tensor(first_g[2][:, :, :], first_g[0][:, :, :], first_g[1][:, :, :].bitcast(F32),
                                      ALU.subtract).then_inc(first_lo_made, 1)
                for c in range(3):
                    u, b = 3 * q + c, (j + c) % 2
                    u_gelu.wait(dve, u)
                    lo_made.wait(dve, u - 2)
                    dve.tensor_tensor(ob[:, b, :].unsqueeze(1), u_act[:, b, :].unsqueeze(1),
                                      mixT[:, bass.ds(q, 1), c * TC:(c + 1) * TC], ALU.mult).then_inc(ob_made.sem, 1)

            over_chunks(dve, step)


def gates_phase(nc, io, keep, psum):
    hT = (keep["hT_hi"], keep["hT_lo"])
    branch = ((keep["oaT_hi"], keep["oaT_lo"]), (keep["obT_hi"], keep["obT_lo"]))
    KB = KD + KE
    w_gate = io["w_in"][0].rearrange("(k p) c -> p k c", p=P)
    w_branch = [io[n][0].rearrange("(k p) c -> p k c", p=P) for n in ("w_branch_a", "w_branch_b")]

    with ExitStack() as ctx:
        def sb(name, shape, dt=F32):
            return ctx.enter_context(nc.sbuf_tensor(name, shape, dt))

        def sem(name):
            return keep["semaphores"].enter_context(nc.semaphore("g_" + name))

        behind = [keep["behind_" + name][:, 0:KB * P].rearrange("p (k c) -> p k c", k=KB) for name in ("obT_hi", "obT_lo")]
        first, other = keep["first_g"], [sb("g_w_raw", [P, KB, P])] + behind
        w_raw, w_hi, w_lo = zip(first, other)
        room = keep["mixT"][:, :, :].rearrange("p h n -> p (h n)")
        gate = room[:, 0:2 * TC].rearrange("p (a n) -> p a n", a=2)
        part_a, part_b, h2 = (room[:, n * TC:(n + 3) * TC].rearrange("p (a n) -> p a n", a=3) for n in (2, 5, 8))
        w_in = [sem("w_in_a"), sem("w_in_b")]
        h2_stored = [sem(f"h2_stored_{c}") for c in range(3)]
        w_hi_made, w_lo_made = Flow(sem("w_hi_made")), Flow(sem("w_lo_made"))
        made, gated, multiplied, h2_made = (Flow(sem("made"), 6), Flow(sem("gated"), 4), Flow(sem("multiplied"), 4),
                                            Flow(sem("h2_made"), 3))
        block = ctx.enter_context(nc.Block())

        def pair(ab, c):
            return 2 * ((3 * ab + c) % 4)

        def over_pieces(eng, step):
            step(0, 0, 0)
            with eng.Fori(0, KD - 1) as i:
                step(2 * i + 1, i, 1)
                step(2 * i + 2, i + 1, 0)
            step(2 * KD - 1, KD - 1, 1)

        def is_last(q):
            return isinstance(q, int) and q == 2 * KD - 1

        @block.sync
        def _(sp):
            for c in range(3):
                sp.sem_inc(h2_stored[c], DMA)

            def store(d):
                for c in range(3):
                    h2_made.wait(sp, 3 * d + c)
                    sp.dma_start(io["h2T"][:, bass.ds(d, 1), c * TC:(c + 1) * TC],
                                 h2[:, c, :].unsqueeze(1)).then_inc(h2_stored[c], DMA)

            def load(q, d, ab):
                if not (isinstance(q, int) and q == 0):
                    load_weights(q, d, ab)
                    if ab == 0:
                        store(d - 1)

            def load_weights(q, d, ab):
                w_hi_made.wait(sp, q - 2)
                w_lo_made.wait(sp, q - 2)
                sp.dma_start(w_raw[ab][:, 0:KD], w_gate[:, :, bass.ds(d * P + (OFF_GA, OFF_GB)[ab], P)]).then_inc(w_in[ab], DMA)
                sp.dma_start(w_raw[ab][:, KD:], w_branch[ab][:, :, bass.ds(d * P, P)]).then_inc(w_in[ab], DMA)

            over_pieces(sp, load)
            store(KD - 1)
            for c in range(3):
                sp.wait_ge(h2_stored[c], DMA * (KD + 1))

        @block.scalar
        def _(act):
            w_hi_made.begin(act)
            gated.begin(act)

            def weights(q, d, ab):
                act.wait_ge(w_in[ab], 2 * DMA * d + 2 * DMA * ab)
                made.wait(act, 3 * q - 4)
                act.activation(w_hi[ab][:, :, :], w_raw[ab][:, :, :], ACT.Copy).then_inc(w_hi_made.sem, 1)

            def step(q, d, ab):
                if not is_last(q):
                    weights(q + 1, d + ab, 1 - ab)
                for c in range(3):
                    u = 3 * q + c
                    made.wait(act, u)
                    multiplied.wait(act, u - 2)
                    act.activation(gate[:, (ab + c) % 2, :], bank(psum, pair(ab, c))[:, 0:TC], ACT.Sigmoid).then_inc(gated.sem, 1)

            act.sem_inc(w_hi_made.sem, 1)
            over_pieces(act, step)

        @block.tensor
        def _(pe):
            made.begin(pe)

            def step(q, d, ab):
                w_hi_made.wait(pe, q)
                w_lo_made.wait(pe, q)
                src = branch[ab]
                for c in range(3):
                    u = 3 * q + c
                    gated.wait(pe, u - 2)
                    multiplied.wait(pe, u - 2)
                    part = slice(c * TC, (c + 1) * TC)
                    product(pe, bank(psum, pair(ab, c))[:, 0:TC], lambda k: (w_hi[ab][:, k, :], w_lo[ab][:, k, :]),
                            lambda k: (hT[0][:, k, part], hT[1][:, k, part]), KD)
                    product(pe, bank(psum, pair(ab, c) + 1)[:, 0:TC],
                            lambda k: (w_hi[ab][:, KD + k, :], w_lo[ab][:, KD + k, :]),
                            lambda k: (src[0][:, k, part], src[1][:, k, part]), KE).then_inc(made.sem, 1)

            over_pieces(pe, step)

        @block.vector
        def _(dve):
            w_lo_made.begin(dve)
            multiplied.begin(dve)
            h2_made.begin(dve)

            def weights(q, ab):
                w_hi_made.wait(dve, q)
                made.wait(dve, 3 * q - 4)
                dve.tensor_tensor(w_lo[ab][:, :, :], w_raw[ab][:, :, :], w_hi[ab][:, :, :].bitcast(F32), ALU.subtract).then_inc(w_lo_made.sem, 1)

            def step(q, d, ab):
                if not is_last(q):
                    weights(q + 1, 1 - ab)
                for c in range(3):
                    u = 3 * q + c
                    gated.wait(dve, u)
                    h2_made.wait(dve, 3 * d + c - 3)
                    out = part_b[:, c, :] if ab else part_a[:, c, :]
                    dve.tensor_tensor(out, bank(psum, pair(ab, c) + 1)[:, 0:TC], gate[:, (ab + c) % 2, :],
                                      ALU.mult).then_inc(multiplied.sem, 1)
                    if ab:
                        multiplied.wait(dve, u)
                        dve.wait_ge(h2_stored[c], DMA * d + DMA)
                        dve.tensor_tensor(h2[:, c, :], part_a[:, c, :], part_b[:, c, :], ALU.add).then_inc(h2_made.sem, 1)

            dve.sem_inc(w_lo_made.sem, 1)
            over_pieces(dve, step)


def merge_phase(nc, io, keep, psum):
    hT, ident, y, lg = (keep["hT_hi"], keep["hT_lo"]), keep["ident"], keep["y"], keep["lg"]
    w_src = io["w_out"][0].rearrange("(k p) c -> p k c", p=P)
    x_p = io["x"][0:SEQ, :].rearrange("(t p) d -> p t d", p=P)

    with ExitStack() as ctx:
        def sb(name, shape, dt=F32):
            return ctx.enter_context(nc.sbuf_tensor(name, shape, dt))

        def sem(name):
            return keep["semaphores"].enter_context(nc.semaphore("m_" + name))

        h2 = sb("h2_back", [P, KD, NTOK])
        w_raw = sb("o_w_raw", [P, 2, KD, P])
        w_hi = sb("o_w_hi", [P, 2, KD, P], F32R)
        w_lo = sb("o_w_lo", [P, 2, KD, P], F32R)
        x_in = sb("x_chunk", [P, 2, NT, P])
        wT = sb("woutT", [P, 2, NTOK])
        yT = sb("yT", [P, 2, NTOK])
        g2 = sb("g2_rows", [P, KD])
        w_r = sb("w_router", [P, KD, NR])
        squares = sb("squares", [P, NT, P])
        square_sums = keep["square_sums"]
        const_in, h2_in, w_in, x_in_done = (sem("const_in"), [sem(f"h2_in_{k}") for k in range(KD)],
                                            [sem("w_in_even"), sem("w_in_odd")], [sem("x_in_even"), sem("x_in_odd")])
        first_w_in = sem("first_w_in")
        passed, squares_passed, squared, summed = sem("passed"), sem("squares_passed"), Flow(sem("squared")), Flow(sem("summed"))
        h2_hi, h2_lo, w_r_made, zeroed = sem("h2_hi"), sem("h2_lo"), sem("w_r_made"), sem("zeroed")
        w_hi_made, w_lo_made = Flow(sem("w_hi_made")), Flow(sem("w_lo_made"))
        made, evicted = Flow(sem("made"), 6), Flow(sem("evicted"), 6)
        xT_made, yT_made = Flow(sem("xT_made")), Flow(sem("yT_made"))
        back_made, y_copied, y_rest = Flow(sem("back_made")), Flow(sem("y_copied")), Flow(sem("y_rest"))
        block = ctx.enter_context(nc.Block())
        BANKS = ((0, 0, 4), (1, 4, 8), (2, 8, NT))

        def unit_bank(d, j, c):
            return 5 if first(d) and c == 2 else (j + c) % 2

        def first(d):
            return isinstance(d, int) and d == 0

        def last(d):
            return isinstance(d, int) and d == KD - 1

        def over_chunks(eng, step):
            step(0, 0)
            with eng.Fori(0, KD // 2 - 1) as i:
                step(2 * i + 1, 1)
                step(2 * i + 2, 0)
            step(KD - 1, 1)

        def times(d, j, per=DMA):
            return (d - j) * (per // 2) + per

        @block.sync
        def _(sp):
            sp.dma_start(w_raw[:, 0], w_src[:, :, 0:P]).then_inc(first_w_in, DMA)
            for k in range(KD):
                sp.dma_start(h2[:, k, :], io["h2T"][:, k, :]).then_inc(h2_in[k], DMA)

        @block.gpsimd
        def _(pool):
            def load(d, j):
                if not first(d):
                    w_hi_made.wait(pool, d - 2)
                    w_lo_made.wait_alone(pool, d - 2, passed)
                    pool.dma_start(w_raw[:, j], w_src[:, :, bass.ds(d * P, P)]).then_inc(w_in[j], DMA)
                xT_made.wait_alone(pool, d - 2, passed)
                pool.dma_start(x_in[:, j, 0:PT], x_p[:, :, bass.ds(d * P, P)]).then_inc(x_in_done[j], DMA)
                pool.dma_start(x_in[0:NS, j, PT], io["x"][SEQ:NTOK, bass.ds(d * P, P)]).then_inc(x_in_done[j], DMA)

            over_chunks(pool, load)

        @block.scalar
        def _(act):
            act.dma_start(g2[:, :], io["norm2_g"][0].rearrange("(k p) -> p k", p=P)).then_inc(const_in, DMA)
            act.dma_start(w_r[:, :, 0:NG], io["w_router_group"][0].rearrange("(k p) e -> p k e", p=P)).then_inc(const_in, DMA)
            act.dma_start(w_r[:, :, NG:], io["w_router_expert"][0].rearrange("(k p) e -> p k e", p=P)).then_inc(const_in, DMA)
            w_hi_made.begin(act)
            evicted.begin(act)
            y_copied.begin(act)
            squared.begin(act)

            def weights(d, j):
                if first(d):
                    act.wait_ge(first_w_in, DMA)
                else:
                    act.wait_ge(w_in[j], (d + j) * (DMA // 2))
                made.wait(act, 3 * d - 4)
                act.activation(w_hi[:, j], w_raw[:, j], ACT.Copy).then_inc(w_hi_made.sem, 1)

            weights(0, 0)
            for k in range(KD):
                act.wait_ge(h2_in[k], DMA)
                act.activation(hT[0][:, k, :], h2[:, k, :], ACT.Copy).then_inc(h2_hi, 1)

            def keep_y(d):
                back_made.wait(act, d)
                for b, t0, t1 in BANKS[0:2]:
                    ins = act.activation(y[:, t0:t1, bass.ds(d * P, P)],
                                         bank(psum, 5 + b).rearrange("p (t c) -> p t c", c=P)[:, 0:t1 - t0], ACT.Copy)
                ins.then_inc(y_copied.sem, 1)
                y_copied.wait(act, d)
                y_rest.wait(act, d)
                summed.wait_alone(act, d - 1, squares_passed)
                act.activation(squares[:, :, :], y[:, :, bass.ds(d * P, P)], ACT.Square).then_inc(squared.sem, 1)

            def step(d, j):
                if not last(d):
                    weights(d + 1, 1 - j)
                for c in range(3):
                    made.wait(act, 3 * d + c)
                    if c == 0:
                        yT_made.wait(act, d - 2)
                    act.activation(wT[:, j, c * TC:(c + 1) * TC], bank(psum, unit_bank(d, j, c))[:, 0:TC],
                                   ACT.Copy).then_inc(evicted.sem, 1)
                    if c == 0 and not first(d):
                        keep_y(d - 1)

            over_chunks(act, step)
            keep_y(KD - 1)

        @block.tensor
        def _(pe):
            made.begin(pe)
            xT_made.begin(pe)
            back_made.begin(pe)

            def x_turn(d, j):
                pe.wait_ge(x_in_done[j], times(d, j, 2 * DMA))
                yT_made.wait(pe, d - 1)
                for b, t0, t1 in BANKS:
                    for t in range(t0, t1):
                        n = rows(t)
                        mm = pe.transpose(bank(psum, 2 + b)[:, (t - t0) * P:(t - t0) * P + n], x_in[0:n, j, t, :],
                                          ident[0:n, 0:n])
                mm.then_inc(xT_made.sem, 1)
            def all_units(d, j):
                w_hi_made.wait(pe, d)
                w_lo_made.wait(pe, d)
                for k in range(KD):
                    pe.wait_ge(h2_lo, k + 1)
                    for c in range(3):
                        part = slice(c * TC, (c + 1) * TC)
                        mm = product(pe, bank(psum, unit_bank(d, j, c))[:, 0:TC],
                                     lambda _: (w_hi[:, j, k, :], w_lo[:, j, k, :]),
                                     lambda _: (hT[0][:, k, part], hT[1][:, k, part]), 1, k == 0, k == KD - 1)
                        if k == KD - 1:
                            mm.then_inc(made.sem, 1)

            def unit(d, j, c):
                w_hi_made.wait(pe, d)
                w_lo_made.wait(pe, d)
                evicted.wait(pe, 3 * d + (c - 2))
                part = slice(c * TC, (c + 1) * TC)
                product(pe, bank(psum, unit_bank(d, j, c))[:, 0:TC], lambda k: (w_hi[:, j, k, :], w_lo[:, j, k, :]),
                        lambda k: (hT[0][:, k, part], hT[1][:, k, part]), KD).then_inc(made.sem, 1)

            def step(d, j):
                if first(d):
                    all_units(d, j)
                    x_turn(d, j)
                else:
                    unit(d, j, 0)
                    back(d - 1, 1 - j)
                    x_turn(d, j)
                    unit(d, j, 1)
                    unit(d, j, 2)

            def back(d, j):
                yT_made.wait(pe, d)
                y_copied.wait(pe, d - 1)
                y_rest.wait(pe, d - 1)
                pe.wait_ge(w_r_made, 1)
                for b, t0, t1 in BANKS:
                    for t in range(t0, t1):
                        n = rows(t)
                        pe.transpose(bank(psum, 5 + b)[0:n, (t - t0) * P:(t - t0 + 1) * P], yT[:, j, toks(t)], ident[:, :])
                for t in range(NT):
                    mm = pe.matmul(bank(psum, 7)[0:rows(t), P + t * NR:P + (t + 1) * NR], yT[:, j, toks(t)],
                                   w_r[:, bass.ds(d, 1), :].rearrange("p a r -> p (a r)"), start=True, stop=True)
                mm.then_inc(back_made.sem, 1)

            over_chunks(pe, step)
            back(KD - 1, 1)

        @block.vector
        def _(dve):
            w_lo_made.begin(dve)
            yT_made.begin(dve)
            y_rest.begin(dve)
            summed.begin(dve)
            dve.memset(lg[:, :, :], 0.0).then_inc(zeroed, 1)
            dve.memset(y[:, PT, :], 0.0).then_inc(zeroed, 1)
            dve.wait_ge(const_in, DMA * 3)
            dve.tensor_tensor(w_r[:, :, :], w_r[:, :, :], g2[:, :].unsqueeze(2).broadcast_to([P, KD, NR]), ALU.mult).then_inc(w_r_made, 1)

            def weights(d, j):
                w_hi_made.wait(dve, d)
                made.wait(dve, 3 * d - 4)
                dve.tensor_tensor(w_lo[:, j], w_raw[:, j], w_hi[:, j].bitcast(F32), ALU.subtract).then_inc(w_lo_made.sem, 1)

            weights(0, 0)
            for k in range(KD):
                dve.wait_ge(h2_hi, k + 1)
                dve.tensor_tensor(hT[1][:, k, :], h2[:, k, :], hT[0][:, k, :].bitcast(F32), ALU.subtract).then_inc(h2_lo, 1)
            dve.wait_ge(zeroed, 2)

            def step(d, j):
                if not last(d):
                    weights(d + 1, 1 - j)
                if not first(d):
                    rest(d - 1)
                xT_made.wait(dve, d)
                evicted.wait(dve, 3 * d + 2)
                back_made.wait(dve, d - 2)
                for b, t0, t1 in BANKS:
                    part = slice(t0 * P, min(t1 * P, NTOK))
                    ins = dve.tensor_tensor(yT[:, j, part], bank(psum, 2 + b)[:, 0:part.stop - part.start], wT[:, j, part], ALU.add)
                ins.then_inc(yT_made.sem, 1)
                if not first(d):
                    sum_squares(d - 1)

            def rest(d):
                back_made.wait(dve, d)
                dve.tensor_copy(y[0:NS, PT:NT, bass.ds(d * P, P)], bank(psum, 7)[0:NS, 0:P].unsqueeze(1))
                y_rest.wait(dve, d - 1)
                sums = bank(psum, 7)[:, P:P + NT * NR].rearrange("p (t r) -> p t r", r=NR)
                dve.tensor_tensor(lg[:, 0:PT, :], lg[:, 0:PT, :], sums[:, 0:PT], ALU.add)
                dve.tensor_tensor(lg[0:NS, PT, :], lg[0:NS, PT, :], sums[0:NS, PT], ALU.add).then_inc(y_rest.sem, 1)

            def sum_squares(d):
                squared.wait(dve, d)
                dve.tensor_reduce(square_sums[:, :, bass.ds(d, 1)], squares[:, :, :], AX_X, ALU.add).then_inc(summed.sem, 1)

            over_chunks(dve, step)
            rest(KD - 1)
            sum_squares(KD - 1)


def expert_weights(io):
    return [io[name][0].rearrange("e (k p) f -> p e k f", p=P) for name in ("w_exp_gate", "w_exp_up", "w_exp_down")]


def routing_phase(nc, io, keep, psum):
    ident, y, lg = keep["ident"], keep["y"], keep["lg"]
    slot_w, gather_at, scatter_at, step_plan = keep["slot_w"], keep["gather_at"], keep["scatter_at"], keep["step_plan"]

    with ExitStack() as ctx:
        def sb(name, shape, dt=F32):
            return ctx.enter_context(nc.sbuf_tensor("r_" + name, shape, dt))

        def sem(name):
            return keep["semaphores"].enter_context(nc.semaphore("r_" + name))

        g2 = sb("g2", [P, D])
        bias = sb("bias", [P, NR])
        zeros = sb("zeros", [P, D])

        yss = sb("yss", [P, NT])
        r2 = sb("r2", [P, NT])
        minus_half = sb("minus_half", [P, NT])
        logits = sb("logits", [P, NT, NR])
        g_top = sb("g_top", [P, NT])
        g_exp = sb("g_exp", [P, NT, NG])
        g_sum = sb("g_sum", [P, NT])
        g_pick = sb("g_pick", [P, NT, NG])
        eq = sb("eq", [P, NT, EPG])
        pr_top = sb("pr_top", [P, NT])
        prio = sb("prio", [P, EPG])
        sel4 = sb("sel4", [P, NT, NG, EPG])
        e_sel = sb("e_sel", [P, NT, EPG])
        e_top = sb("e_top", [P, 2, NT])
        e_pick = sb("e_pick", [P, 2, NT, EPG])
        wts = sb("wts", [P, 2, NT])
        ratio = sb("ratio", [P, NT])
        chosen = sb("chosen", [P, 2, NT, NE])
        both = sb("both", [P, NT + 1, NE])
        before = sb("before", [P, NT + 1, NE])
        lower = sb("lower", [P, P])
        ones = sb("ones", [P, P])
        hot = sb("hot", [P, 2, NT, PLANNED])
        place = sb("place", [P, NT, NE])
        limits = sb("limits", [P, NT])
        over = sb("over", [P, NE, NT])
        steps_of = sb("steps_of", [P, NE])
        step_end = sb("step_end", [P, NE])
        picked = sb("picked", [P, NT, NE])
        slot = sb("slot", [P, 2, NT])
        slot_i = sb("slot_i", [P, 2, NT], I32)
        slot_hi_i = sb("slot_hi_i", [P, 2, NT], I32)
        slot_lo_i = sb("slot_lo_i", [P, 2, NT], I32)
        slot_hi = sb("slot_hi", [P, 2, NT])
        slot_lo = sb("slot_lo", [P, 2, NT])
        slots = sb("slots", [P, P])
        steps = sb("steps", [P, PLANNED])
        number = sb("number", [P, NT])
        in_slot = sb("in_slot", [P, 2, NT, P])
        in_step = sb("in_step", [P, 2, NT, 2, PLANNED])
        found = sb("found", [P, 2, PLANNED])
        empty = sb("empty", [P, PLANNED])
        spare = sb("spare", [P, 1])
        where = sb("where", [P, PLANNED])
        ended = sb("ended", [P, PLANNED, NE])
        expert_f = sb("expert_f", [P, PLANNED])
        is_new = sb("is_new", [P, PLANNED])
        load_no = sb("load_no", [P, PLANNED])
        slots_i = sb("slots_i", [P, P], I32)

        const_in, consts, stored = sem("const_in"), sem("consts"), sem("stored")
        y_stored = [sem(f"y_stored_{b}") for b in range(3)]
        dve_step, meaned, rooted, hn_scaled, hn_made = (sem("dve_step"), sem("meaned"), sem("rooted"), sem("hn_scaled"),
                                                        sem("hn_made"))
        plan_made, last_hn_made = sem("plan_made"), sem("last_hn_made")
        POOL_TILES = NT - 2
        g_shifted, g_exped, e_shifted, e_exped = sem("g_shifted"), sem("g_exped"), sem("e_shifted"), sem("e_exped")
        sums_ready, sums_made, pairs_made, found_made = sem("sums_ready"), sem("sums_made"), sem("pairs_made"), sem("found_made")
        block = ctx.enter_context(nc.Block())

        @block.sync
        def _(sp):
            sp.wait_ge(const_in, DMA * 3)
            for t in range(NT):
                sp.dma_start(io["y"][toks(t), :], y[0:rows(t), t, :]).then_inc(y_stored[t // 3], DMA)
            sp.wait_ge(consts, 1)
            sp.dma_start(io["y"][NTOK:NTOK + SLOT, :], zeros[:, :]).then_inc(stored, DMA)
            for t in range(POOL_TILES):
                sp.wait_ge(hn_made, t + 1)
                sp.dma_start(io["hn"][toks(t), :], y[0:rows(t), t, :]).then_inc(stored, DMA)
            sp.wait_ge(plan_made, 1)
            e = sp.value_load(step_plan[0:1, 2, 0:1], min_val=0, max_val=NE - 1)
            for ab, w in enumerate(expert_weights(io)[0:2]):
                sp.dma_start(keep["gu_raw"][:, 0:1, :, ab, :], w[:, bass.ds(e, 1)]).then_inc(keep["gu_in"], DMA)
            for t in range(POOL_TILES, NT):
                sp.wait_ge(last_hn_made, t - POOL_TILES + 1)
                sp.dma_start(io["hn"][toks(t), :], y[0:rows(t), t, :]).then_inc(stored, DMA)
            sp.dma_start(keep["dn_raw"][:, 0:1], expert_weights(io)[2][:, bass.ds(e, 1)]).then_inc(keep["dn_in"], DMA)
            sp.wait_ge(stored, DMA * (NT + 1))
            for b in range(3):
                sp.wait_ge(y_stored[b], DMA * 3)

        @block.gpsimd
        def _(pool):
            pool.memset(zeros[:, :], 0.0).then_inc(consts, 1)
            pool.memset(minus_half[:, :], -0.5).then_inc(consts, 1)
            pool.memset(ones[:, :], 1.0).then_inc(consts, 1)
            pool.memset(lower[:, :], 1.0).then_inc(consts, 1)
            pool.wait_ge(consts, 4)
            pool.affine_select(out=lower[:, :], in_=lower[:, :], compare_op=ALU.is_ge, fill=0.0, base=-1,
                               pattern=[[1, P]], channel_multiplier=-1).then_inc(consts, 1)
            kw = dict(allow_small_or_imprecise_dtypes=True)
            pool.iota(prio[:, :], [[-1, EPG]], base=EPG, channel_multiplier=0, **kw).then_inc(consts, 1)
            pool.iota(limits[:, :], [[SLOT, NT]], base=0, channel_multiplier=0, **kw).then_inc(consts, 1)
            pool.iota(slots[:, :], [[1, P]], base=0, channel_multiplier=0, **kw).then_inc(consts, 1)
            pool.iota(steps[:, :], [[1, PLANNED]], base=0, channel_multiplier=0, **kw).then_inc(consts, 1)
            pool.iota(number[:, :], [[P, NT]], base=1, channel_multiplier=1, **kw).then_inc(consts, 1)
            pool.iota(spare[:, :], [[1, 1]], base=NTOK + 1, channel_multiplier=1, **kw).then_inc(consts, 1)
            pool.wait_ge(meaned, 1)
            pool.tensor_tensor(r2[:, :], yss[:, :], minus_half[:, :], ALU.pow).then_inc(rooted, 1)
            pool.wait_ge(const_in, DMA * 3)
            for t in range(POOL_TILES):
                pool.wait_ge(hn_scaled, t + 1)
                pool.tensor_tensor(y[:, t, :], y[:, t, :], g2[:, :], ALU.mult).then_inc(hn_made, 1)

        @block.scalar
        def _(act):
            act.dma_start(g2[:, :], io["norm2_g"][0].partition_broadcast(P)).then_inc(const_in, DMA)
            act.dma_start(bias[:, 0:NG], io["b_router_group"][0].partition_broadcast(P)).then_inc(const_in, DMA)
            act.dma_start(bias[:, NG:], io["b_router_expert"][0].partition_broadcast(P)).then_inc(const_in, DMA)
            act.wait_ge(rooted, 1)
            for t in range(NT):
                n = rows(t)
                if t == 3:
                    act.wait_ge(g_shifted, 1)
                    act.activation(g_exp[:, :, :], g_exp[:, :, :], ACT.Exp).then_inc(g_exped, 1)
                if t == 6:
                    act.wait_ge(e_shifted, 1)
                    act.activation(ratio[:, :], ratio[:, :], ACT.Exp).then_inc(e_exped, 1)
                if t % 3 == 0:
                    act.wait_ge(y_stored[t // 3], DMA * 3)
                act.activation(y[0:n, t, :], y[0:n, t, :], ACT.Copy, scale=r2[0:n, t:t + 1]).then_inc(hn_scaled, 1)

        @block.tensor
        def _(pe):
            pe.wait_ge(sums_ready, 1)
            width = (NT + 1) * NE
            flat = [a[:, :, :].rearrange("p t e -> p (t e)") for a in (both, before)]
            pe.matmul(bank(psum, 0)[:, 0:width], lower[:, :], flat[0], start=True, stop=False)
            pe.matmul(bank(psum, 0)[:, 0:width], ones[:, :], flat[1], start=False, stop=True).then_inc(sums_made, 1)
            for n in range(2):
                pe.wait_ge(pairs_made, n + 1)
                for t in range(NT):
                    mm = pe.matmul(bank(psum, 1)[:, 0:2 * PLANNED], in_slot[:, n, t, :],
                                   in_step[:, n, t, :, :].rearrange("p a s -> p (a s)"), start=n + t == 0,
                                   stop=n == 1 and t == NT - 1)
            mm.then_inc(found_made, 1)

        @block.vector
        def _(dve):
            step = Step(dve, dve_step)
            did = step.did

            def tt(out, a, b, op):
                did(dve.tensor_tensor(out, a, b, op))

            def over_last(a, n):
                return a.unsqueeze(2).broadcast_to([P, NT, n])

            def first_top(out, values, top):
                tt(out, values, over_last(top, EPG), ALU.is_equal)
                tt(eq[:, :, :], out, prio[:, :].unsqueeze(1).broadcast_to([P, NT, EPG]), ALU.mult)
                did(dve.tensor_reduce(pr_top[:, :], eq[:, :, :], AX_X, ALU.max))
                tt(out, eq[:, :, :], over_last(pr_top[:, :], EPG), ALU.is_equal)

            did(dve.tensor_reduce(yss[:, :], keep["square_sums"][:, :, :], AX_X, ALU.add))
            dve.tensor_scalar(yss[:, :], yss[:, :], 1.0 / D, EPS, ALU.mult, ALU.add).then_inc(meaned, 1)
            dve.wait_ge(const_in, DMA * 3)
            dve.wait_ge(consts, 11)
            dve.wait_ge(rooted, 1)
            tt(logits[:, :, :], lg[:, :, :], over_last(r2[:, :], NR), ALU.mult)
            tt(logits[:, :, :], logits[:, :, :], bias[:, :].unsqueeze(1).broadcast_to([P, NT, NR]), ALU.add)
            gl = logits[:, :, 0:NG]
            el = logits[:, :, NG:].rearrange("p t (g e) -> p t g e", g=NG)
            did(dve.tensor_reduce(g_top[:, :], gl, AX_X, ALU.max))
            dve.tensor_tensor(g_exp[:, :, :], gl, over_last(g_top[:, :], NG), ALU.subtract).then_inc(g_shifted, 1)
            first_top(g_pick[:, :, :], gl, g_top[:, :])
            tt(sel4[:, :, :, :], el, g_pick[:, :, :].unsqueeze(3).broadcast_to([P, NT, NG, EPG]), ALU.mult)
            did(dve.tensor_reduce(e_sel[:, :, :], sel4[:, :, :, :].rearrange("p t g e -> p t e g"), AX_X, ALU.add))
            for n in range(2):
                did(dve.tensor_reduce(e_top[:, n, :], e_sel[:, :, :], AX_X, ALU.max))
                first_top(e_pick[:, n, :, :], e_sel[:, :, :], e_top[:, n, :])
                if n == 0:
                    did(dve.scalar_tensor_tensor(e_sel[:, :, :], e_pick[:, 0, :, :], NEG, e_sel[:, :, :], ALU.mult, ALU.add))
            dve.tensor_tensor(ratio[:, :], e_top[:, 1, :], e_top[:, 0, :], ALU.subtract).then_inc(e_shifted, 1)
            for n in range(2):
                tt(chosen[:, n, :, :].rearrange("p t (g e) -> p t g e", g=NG),
                   g_pick[:, :, :].unsqueeze(3).broadcast_to([P, NT, NG, EPG]),
                   e_pick[:, n, :, :].unsqueeze(2).broadcast_to([P, NT, NG, EPG]), ALU.mult)
            for q in range(NS, P, 32):
                did(dve.memset(chosen[q:q + 32, :, PT, :], 0.0))
                did(dve.memset(number[q:q + 32, PT:NT], 0.0))
            did(dve.memset(both[:, NT, :], 0.0))
            tt(both[:, 0:NT, :], chosen[:, 0, :, :], chosen[:, 1, :, :], ALU.add)
            did(dve.memset(before[:, 0, :], 0.0))
            for t in range(NT - 1):
                tt(before[:, t + 1, :], before[:, t, :], both[:, t, :], ALU.add)
            dve.tensor_tensor(before[:, NT, :], before[:, NT - 1, :], both[:, NT - 1, :], ALU.add).then_inc(sums_ready, 1)
            dve.wait_ge(g_exped, 1)
            did(dve.tensor_reduce(g_sum[:, :], g_exp[:, :, :], AX_X, ALU.add))
            dve.wait_ge(e_exped, 1)
            did(dve.tensor_scalar(wts[:, 0, :], ratio[:, :], 1.0, None, ALU.add))
            tt(wts[:, 0, :], wts[:, 0, :], g_sum[:, :], ALU.mult)
            did(dve.reciprocal(wts[:, 0, :], wts[:, 0, :]))
            tt(wts[:, 1, :], wts[:, 0, :], ratio[:, :], ALU.mult)
            for q in range(NS, P, 32):
                did(dve.memset(wts[q:q + 32, :, PT:NT], 0.0))
            dve.wait_ge(sums_made, 1)
            sums = bank(psum, 0)[:, 0:(NT + 1) * NE].rearrange("p (t e) -> p t e", e=NE)
            did(dve.tensor_copy(place[:, :, :], sums[:, 0:NT, :]))
            did(dve.tensor_copy(step_end[:, :], sums[:, NT, :]))
            tt(over[:, :, :], step_end[:, :].unsqueeze(2).broadcast_to([P, NE, NT]),
               limits[:, :].unsqueeze(1).broadcast_to([P, NE, NT]), ALU.is_gt)
            did(dve.tensor_reduce(steps_of[:, :], over[:, :, :], AX_X, ALU.add))
            did(dve.tensor_tensor_scan(step_end[:, :], ones[:, 0:NE], steps_of[:, :], 0.0, ALU.mult, ALU.add))
            tt(ended[:, :, :], step_end[:, :].unsqueeze(1).broadcast_to([P, PLANNED, NE]),
               steps[:, :].unsqueeze(2).broadcast_to([P, PLANNED, NE]), ALU.is_le)
            did(dve.tensor_reduce(expert_f[:, :], ended[:, :, :], AX_X, ALU.add))
            did(dve.tensor_scalar(expert_f[:, :], expert_f[:, :], float(NE - 1), None, ALU.min))
            did(dve.tensor_copy(step_plan[:, 2, 0:PLANNED], expert_f[:, :]))
            did(dve.memset(is_new[:, 0:1], 0.0))
            tt(is_new[:, 1:PLANNED], expert_f[:, 1:PLANNED], expert_f[:, 0:PLANNED - 1], ALU.is_gt)
            did(dve.tensor_copy(step_plan[:, 1, 0:PLANNED], is_new[:, :]))
            did(dve.tensor_tensor_scan(load_no[:, :], ones[:, 0:PLANNED], is_new[:, :], 0.0, ALU.mult, ALU.add))
            did(dve.tensor_copy(step_plan[:, 0, 0:PLANNED], load_no[:, :]))
            dve.tensor_copy(step_plan[:, 0, PLANNED:PLANNED + 1], step_end[:, NE - 1:NE]).then_inc(plan_made, 1)
            tt(steps_of[:, :], step_end[:, :], steps_of[:, :], ALU.subtract)
            did(dve.tensor_scalar(steps_of[:, :], steps_of[:, :], float(SLOT), None, ALU.mult))
            tt(place[:, :, :], place[:, :, :], steps_of[:, :].unsqueeze(1).broadcast_to([P, NT, NE]), ALU.add)
            for n in range(2):
                tt(picked[:, :, :], place[:, :, :], chosen[:, n, :, :], ALU.mult)
                did(dve.tensor_reduce(slot[:, n, :], picked[:, :, :], AX_X, ALU.add))
            did(dve.tensor_copy(slot_i[:, :, :], slot[:, :, :]))
            did(dve.tensor_scalar(slot_hi_i[:, :, :], slot_i[:, :, :], SLOT.bit_length() - 1, None, ALU.logical_shift_right))
            did(dve.tensor_scalar(slot_lo_i[:, :, :], slot_i[:, :, :], SLOT - 1, None, ALU.bitwise_and))
            did(dve.tensor_copy(slot_hi[:, :, :], slot_hi_i[:, :, :]))
            did(dve.tensor_copy(slot_lo[:, :, :], slot_lo_i[:, :, :]))
            for n in range(2):
                tt(hot[:, n, :, :], steps[:, :].unsqueeze(1).broadcast_to([P, NT, PLANNED]),
                   over_last(slot_hi[:, n, :], PLANNED), ALU.is_equal)
                for v, value in enumerate((number[:, :], wts[:, n, :])):
                    dve.tensor_tensor(in_step[:, n, :, v, :], hot[:, n, :, :], over_last(value, PLANNED), ALU.mult)
                dve.tensor_tensor(in_slot[:, n, :, :], slots[:, :].unsqueeze(1).broadcast_to([P, NT, P]),
                                  over_last(slot_lo[:, n, :], P), ALU.is_equal).then_inc(pairs_made, 1)
            for t in range(POOL_TILES, NT):
                n = rows(t)
                dve.wait_ge(hn_scaled, t + 1)
                dve.tensor_tensor(y[0:n, t, :], y[0:n, t, :], g2[0:n, :], ALU.mult).then_inc(last_hn_made, 1)
            dve.wait_ge(found_made, 1)
            did(dve.tensor_copy(found[:, :, :].rearrange("p a s -> p (a s)"), bank(psum, 1)[:, 0:2 * PLANNED]))
            did(dve.tensor_copy(slot_w[:, :], found[:, 1, :]))
            did(dve.tensor_scalar(where[:, :], found[:, 0, :], -1.0, 0.0, ALU.add, ALU.max))
            did(dve.tensor_copy(gather_at[:, :], where[:, :]))
            did(dve.tensor_scalar(empty[:, :], found[:, 0, :], 0.0, spare[:, 0:1], ALU.is_equal, ALU.mult))
            tt(empty[:, :], empty[:, :], found[:, 0, :], ALU.add)
            did(dve.tensor_scalar(empty[:, :], empty[:, :], -1.0, None, ALU.add))
            did(dve.tensor_copy(scatter_at[:, :], empty[:, :]))



def experts_phase(nc, io, keep, psum):
    ident = keep["ident"]
    slot_w, gather_at, scatter_at, step_plan = keep["slot_w"], keep["gather_at"], keep["scatter_at"], keep["step_plan"]
    w_gate, w_up, w_down = expert_weights(io)
    KF = DE // P
    KH = KD // 2
    HD2 = D // 2

    with ExitStack() as ctx:
        def sb(name, shape, dt=F32):
            return ctx.enter_context(nc.sbuf_tensor("x_" + name, shape, dt))

        def sem(name):
            return keep["semaphores"].enter_context(nc.semaphore("x_" + name))

        gu_raw, dn_raw = keep["gu_raw"], keep["dn_raw"]
        gu_hi, gu_lo = (keep[name][:, :, :].rearrange("p k n -> p (k n)")[:, 0:2 * KD * 2 * DE]
                        .rearrange("p (b k a f) -> p b k a f", b=2, k=KD, a=2) for name in ("hT_hi", "hT_lo"))
        dn_hi = sb("dn_hi", [P, 2, KF, D], F32R)
        dn_lo = sb("dn_lo", [P, 2, KF, D], F32R)
        at = sb("at", [P, 2, 2], I32)
        xg, out = keep["y"][:, 0:2, :], keep["y"][:, 2:4, :]
        silu, hid = keep["y"][:, 4, 0:DE], keep["y"][:, 5, 0:DE]
        xT_hi = sb("xT_hi", [P, 2, KD, P], F32R)
        xT_lo = sb("xT_lo", [P, 2, KD, P], F32R)
        hidT_hi = sb("hidT_hi", [P, KF, P], F32R)
        hidT_lo = sb("hidT_lo", [P, KF, P], F32R)

        gu_in, dn_in = keep["gu_in"], keep["dn_in"]
        gathered, added = [sem("gathered_0"), sem("gathered_1")], sem("added")
        passed, loads_passed = sem("passed"), sem("loads_passed")
        gu_hi_made, gu_lo_made = Flow(sem("gu_hi_made"), 4), Flow(sem("gu_lo_made"), 4)
        dn_hi_made, dn_lo_made = Flow(sem("dn_hi_made")), Flow(sem("dn_lo_made"))
        xT_made, xT_hi_made, xT_lo_made = Flow(sem("xT_made"), 4), Flow(sem("xT_hi_made"), 4), Flow(sem("xT_lo_made"), 4)
        at_made, up_made, silu_made, hid_made = Flow(sem("at_made")), Flow(sem("up_made")), Flow(sem("silu_made")), Flow(sem("hid_made"))
        hidT_made, hidT_hi_made, hidT_lo_made = Flow(sem("hidT_made")), Flow(sem("hidT_hi_made")), Flow(sem("hidT_lo_made"))
        down_made, out_made, at_copied = Flow(sem("down_made")), Flow(sem("out_made")), Flow(sem("at_copied"))
        add_turn = Flow(sem("add_turn"))
        block = ctx.enter_context(nc.Block())

        def over_steps(eng, step):
            used = steps_used(eng)
            step(0, 0)
            with eng.Fori(0, MOST_STEPS // 2) as i:
                for ahead in range(2):
                    with eng.If(i * 2 + (ahead + 1) <= used):
                        step(2 * i + (ahead + 1), 1 - ahead)

        def steps_used(eng):
            return eng.value_load(step_plan[0:1, 0, PLANNED:PLANNED + 1], min_val=1, max_val=MOST_STEPS)

        def load_of(eng, s):
            return eng.value_load(step_plan[0:1, 0, bass.ds(s, 1)], min_val=0, max_val=NE - 1)

        def if_new(eng, s):
            return eng.If(eng.value_load(step_plan[0:1, 1, bass.ds(s, 1)], min_val=0, max_val=1) > 0)

        def first(s):
            return isinstance(s, int) and s == 0

        def times(s, j, per=DMA):
            return (s - j) * (per // 2) + per

        @block.sync
        def _(sp):
            def load(s):
                n = load_of(sp, s)
                e = sp.value_load(step_plan[0:1, 2, bass.ds(s, 1)], min_val=0, max_val=NE - 1)
                buf = bass.ds(n % 2, 1)
                gu_hi_made.wait_alone(sp, n * 2 - 3, loads_passed)
                gu_lo_made.wait_alone(sp, n * 2 - 3, loads_passed)
                sp.wait_ge(gu_in, n * (2 * DMA))
                sp.sem_inc(loads_passed, 1)
                sp.dma_start(gu_raw[:, buf, :, 0, :], w_gate[:, bass.ds(e, 1)]).then_inc(gu_in, DMA)
                sp.dma_start(gu_raw[:, buf, :, 1, :], w_up[:, bass.ds(e, 1)]).then_inc(gu_in, DMA)
                dn_hi_made.wait_alone(sp, n - 2, loads_passed)
                dn_lo_made.wait_alone(sp, n - 2, loads_passed)
                sp.wait_ge(dn_in, n * DMA)
                sp.sem_inc(loads_passed, 1)
                sp.dma_start(dn_raw[:, buf], w_down[:, bass.ds(e, 1)]).then_inc(dn_in, DMA)

            with sp.Fori(0, MOST_STEPS) as i:
                with if_new(sp, i + 1):
                    load(i + 1)

        @block.gpsimd
        def _(pool):
            for f in (at_made, dn_lo_made, at_copied, add_turn):
                f.begin(pool)

            def gather(s, j):
                xT_made.wait(pool, 2 * s - 3)
                pool.tensor_copy(at[:, j, 0:1], gather_at[:, bass.ds(s, 1)]).then_inc(at_made.sem, 1)
                at_made.wait_alone(pool, s, passed)
                pool.indirect_dma_start(xg[:, j, :], None, io["hn"], bass.IndirectOffsetOnAxis(at[:, j, 0:1], 0)).then_inc(gathered[j], DMA)

            def scatter(s, j):
                out_made.wait(pool, s)
                pool.tensor_copy(at[:, j, 1:2], scatter_at[:, bass.ds(s, 1)]).then_inc(at_copied.sem, 1)
                at_copied.wait(pool, s)
                if not first(s):
                    pool.wait_ge(added, s * DMA)
                pool.sem_inc(add_turn.sem, 1)
                pool.indirect_dma_start(io["y"], bass.IndirectOffsetOnAxis(at[:, j, 1:2], 0), out[:, j, :], None,
                                        compute_op=ALU.add).then_inc(added, DMA)

            def down_low(s):
                n = load_of(pool, s)
                buf = bass.ds(n % 2, 1)
                dn_hi_made.wait(pool, n)
                down_made.wait(pool, s - 2)
                pool.tensor_tensor(dn_lo[:, buf], dn_raw[:, buf], dn_hi[:, buf].bitcast(F32), ALU.subtract).then_inc(dn_lo_made.sem, 1)

            def step(s, j):
                gather(s + 2, j)
                if first(s):
                    down_low(s)
                else:
                    with if_new(pool, s):
                        down_low(s)
                    scatter(s - 1, 1 - j)

            gather(0, 0)
            gather(1, 1)
            over_steps(pool, step)
            used = steps_used(pool)
            pool.wait_ge(added, used * DMA)
            pool.wait_ge(gathered[0], (used + 4) // 2 * DMA)
            pool.wait_ge(gathered[1], (used + 3) // 2 * DMA)

        @block.scalar
        def _(act):
            for f in (gu_hi_made, dn_hi_made, xT_hi_made, silu_made, hidT_hi_made):
                f.begin(act)

            def up_high(s, half):
                n = load_of(act, s)
                buf = bass.ds(n % 2, 1)
                ks = slice(half * KH, (half + 1) * KH)
                act.wait_ge(gu_in, n * (2 * DMA) + 2 * DMA)
                up_made.wait(act, s - 2)
                act.activation(gu_hi[:, buf, ks], gu_raw[:, buf, ks], ACT.Copy).then_inc(gu_hi_made.sem, 1)

            def down_high(s):
                n = load_of(act, s)
                buf = bass.ds(n % 2, 1)
                act.wait_ge(dn_in, n * DMA + DMA)
                down_made.wait(act, s - 2)
                act.activation(dn_hi[:, buf], dn_raw[:, buf], ACT.Copy).then_inc(dn_hi_made.sem, 1)

            def tokens_high(s, j):
                up_made.wait(act, s - 2)
                for half in range(2):
                    xT_made.wait(act, 2 * s + half)
                    act.activation(xT_hi[:, j, half * KH:(half + 1) * KH, :].rearrange("p k c -> p (k c)"),
                                   bank(psum, half), ACT.Copy).then_inc(xT_hi_made.sem, 1)

            def hidden_high(s):
                hidT_made.wait(act, s)
                down_made.wait(act, s - 1)
                act.activation(hidT_hi[:, :, :].rearrange("p k c -> p (k c)"), bank(psum, 4)[:, 0:DE], ACT.Copy).then_inc(hidT_hi_made.sem, 1)

            def step(s, j):
                if first(s):
                    down_high(s)
                else:
                    hidden_high(s - 1)
                    with if_new(act, s):
                        down_high(s)
                with if_new(act, s + 1):
                    up_high(s + 1, 0)
                up_made.wait(act, s)
                hid_made.wait(act, s - 1)
                act.activation(silu[:, :], bank(psum, 2 + j)[:, 0:DE], ACT.Silu).then_inc(silu_made.sem, 1)
                tokens_high(s + 1, 1 - j)
                with if_new(act, s + 1):
                    up_high(s + 1, 1)

            for half in range(2):
                up_high(0, half)
            tokens_high(0, 0)
            over_steps(act, step)

        @block.tensor
        def _(pe):
            for f in (xT_made, up_made, hidT_made, down_made):
                f.begin(pe)

            def token_turn(s, j):
                pe.wait_ge(gathered[j], times(s, j))
                for half in range(2):
                    xT_lo_made.wait(pe, 2 * s - 2 + half)
                    for k in range(KH):
                        ks = slice((half * KH + k) * P, (half * KH + k + 1) * P)
                        mm = pe.transpose(bank(psum, half)[:, k * P:(k + 1) * P], xg[:, j, ks], ident[:, :])
                    mm.then_inc(xT_made.sem, 1)

            def up(s, j):
                n = load_of(pe, s)
                buf = bass.ds(n % 2, 1)
                hid_made.wait(pe, s - 2)
                for half in range(2):
                    xT_hi_made.wait(pe, 2 * s + half)
                    xT_lo_made.wait(pe, 2 * s + half)
                    gu_hi_made.wait(pe, n * 2 + half)
                    gu_lo_made.wait(pe, n * 2 + half)
                    h = half * KH
                    mm = product(pe, bank(psum, 2 + j), lambda k: (xT_hi[:, j, h + k, :], xT_lo[:, j, h + k, :]),
                                 lambda k: (gu_hi[:, buf, h + k], gu_lo[:, buf, h + k]), KH, first=half == 0, last=half == 1)
                mm.then_inc(up_made.sem, 1)

            def hidden_turn(s):
                hid_made.wait(pe, s)
                hidT_lo_made.wait(pe, s - 1)
                for f in range(KF):
                    mm = pe.transpose(bank(psum, 4)[:, f * P:(f + 1) * P], hid[:, f * P:(f + 1) * P], ident[:, :])
                mm.then_inc(hidT_made.sem, 1)

            def down(s):
                n = load_of(pe, s)
                buf = bass.ds(n % 2, 1)
                hidT_hi_made.wait(pe, s)
                hidT_lo_made.wait(pe, s)
                dn_hi_made.wait(pe, n)
                dn_lo_made.wait(pe, n)
                out_made.wait(pe, s - 1)
                for half in range(2):
                    part = slice(half * HD2, (half + 1) * HD2)
                    mm = product(pe, bank(psum, 5 + half), lambda k: (hidT_hi[:, k, :], hidT_lo[:, k, :]),
                                 lambda k: (dn_hi[:, buf, k, part], dn_lo[:, buf, k, part]), KF)
                mm.then_inc(down_made.sem, 1)

            def step(s, j):
                up(s, j)
                token_turn(s + 1, 1 - j)
                if not first(s):
                    down(s - 1)
                hidden_turn(s)

            token_turn(0, 0)
            over_steps(pe, step)

        @block.vector
        def _(dve):
            for f in (gu_lo_made, xT_lo_made, hid_made, hidT_lo_made, out_made):
                f.begin(dve)

            def up_low(s, half):
                n = load_of(dve, s)
                buf = bass.ds(n % 2, 1)
                ks = slice(half * KH, (half + 1) * KH)
                gu_hi_made.wait(dve, n * 2 + half)
                up_made.wait(dve, s - 2)
                dve.tensor_tensor(gu_lo[:, buf, ks], gu_raw[:, buf, ks], gu_hi[:, buf, ks].bitcast(F32),
                                  ALU.subtract).then_inc(gu_lo_made.sem, 1)

            def tokens_low(s, j):
                for half in range(2):
                    xT_hi_made.wait(dve, 2 * s + half)
                    ks = slice(half * KH, (half + 1) * KH)
                    dve.tensor_tensor(xT_lo[:, j, ks, :].rearrange("p k c -> p (k c)"), bank(psum, half),
                                      xT_hi[:, j, ks, :].rearrange("p k c -> p (k c)").bitcast(F32),
                                      ALU.subtract).then_inc(xT_lo_made.sem, 1)

            def hidden_low(s):
                hidT_hi_made.wait(dve, s)
                dve.tensor_tensor(hidT_lo[:, :, :].rearrange("p k c -> p (k c)"), bank(psum, 4)[:, 0:DE],
                                  hidT_hi[:, :, :].rearrange("p k c -> p (k c)").bitcast(F32), ALU.subtract).then_inc(hidT_lo_made.sem, 1)

            def evict(s, j):
                down_made.wait(dve, s)
                add_turn.wait(dve, s - 1)
                dve.tensor_copy(out[:, j, :], psum[:, 5:7, :].rearrange("p a c -> p (a c)")).then_inc(out_made.sem, 1)

            def step(s, j):
                if not first(s):
                    hidden_low(s - 1)
                with if_new(dve, s + 1):
                    up_low(s + 1, 0)
                silu_made.wait(dve, s)
                hidT_made.wait(dve, s - 1)
                dve.scalar_tensor_tensor(hid[:, :], silu[:, :], slot_w[:, bass.ds(s, 1)], bank(psum, 2 + j)[:, DE:], ALU.mult,
                                         ALU.mult).then_inc(hid_made.sem, 1)
                tokens_low(s + 1, 1 - j)
                with if_new(dve, s + 1):
                    up_low(s + 1, 1)
                if not first(s):
                    evict(s - 1, 1 - j)

            for half in range(2):
                up_low(0, half)
            tokens_low(0, 0)
            over_steps(dve, step)


def hybrid_layer(nc, io):
    with ExitStack() as ctx:
        def sb(stack, name, shape, dt=F32):
            return stack.enter_context(nc.sbuf_tensor(name, shape, dt))

        ctx.enter_context(nc.allow_non_contiguous_dma(reason="small per-row constants"))
        psum = ctx.enter_context(nc.psum_tensor("psum", [P, 8, 512], F32))
        keep = {"ident": sb(ctx, "ident", [P, P]), "semaphores": ctx}
        for name in ("gather_at", "scatter_at"):
            keep[name] = sb(ctx, name, [P, PLANNED], I32)
        keep["step_plan"] = sb(ctx, "step_plan", [P, 3, PLANNED + 1], I32)
        keep["slot_w"] = sb(ctx, "slot_w", [P, PLANNED])
        keep["lg"] = sb(ctx, "lg", [P, NT, NR])

        with ExitStack() as dense:
            for name in ("hT_hi", "hT_lo"):
                keep[name] = sb(dense, name, [P, KD, NTOK], F32R)
            with ExitStack() as branches:
                for name in ("oaT_hi", "oaT_lo"):
                    keep[name] = sb(branches, name, [P, KE, NTOK], F32R)
                for name in ("w_hi", "w_lo"):
                    keep[name] = sb(branches, name, [P, KD, QKV], F32R)
                attention_phase(nc, io, keep, psum)
                keep["mixT"] = sb(branches, "mixT", [P, SG, NTOK])
                for name, nk in (("first_u", KD), ("first_g", KD + KE)):
                    keep[name] = [sb(branches, name + part, [P, nk, P], dt)
                                  for part, dt in (("_raw", F32), ("_hi", F32R), ("_lo", F32R))]
                sgu_values_phase(nc, io, keep, psum)
                for name, w in (("obT_hi", keep["w_hi"]), ("obT_lo", keep["w_lo"])):
                    flat = w[:, :, :].rearrange("p k c -> p (k c)")
                    keep[name] = flat[:, 0:KE * NTOK].rearrange("p (k n) -> p k n", k=KE)
                    keep["behind_" + name] = flat[:, KE * NTOK:]
                sgu_gate_phase(nc, io, keep, psum)
                gates_phase(nc, io, keep, psum)
            keep["y"] = sb(dense, "y", [P, NT, D])
            keep["square_sums"] = sb(dense, "square_sums", [P, NT, KD])
            merge_phase(nc, io, keep, psum)
            keep["gu_raw"] = sb(dense, "gu_raw", [P, 2, KD, 2, DE])
            keep["dn_raw"] = sb(dense, "dn_raw", [P, 2, DE // P, D])
            for name in ("gu_in", "dn_in"):
                keep[name] = ctx.enter_context(nc.semaphore(name))
            routing_phase(nc, io, keep, psum)
            experts_phase(nc, io, keep, psum)


_INS = ["cache_k_win", "cache_v_win", "norm1_g", "w_in", "q_norm_g", "k_norm_g", "attn_sinks", "ln_v_g", "ln_v_b",
        "w_spatial", "b_spatial", "w_branch_a", "w_branch_b", "w_out", "norm2_g", "w_router_group", "b_router_group",
        "w_router_expert", "b_router_expert", "w_exp_gate", "w_exp_up", "w_exp_down"]
_OUTS = {"y": (NTOK + SLOT, D), "new_k_p": (1, 1, WIN, KV, HD), "new_v_p": (1, 1, WIN, KV, HD),
         "new_k_s": (1, DEC_B, WIN, KV, HD), "new_v_s": (1, DEC_B, WIN, KV, HD),
         "new_vs": (1, DEC_B, DEC_T, SG, SW // SG)}


def kernel(**inputs):
    import numpy as np
    import concourse.bacc as bacc
    from concourse.bass_utils import run_bass_kernel_spmd

    nc = bacc.Bacc("TRN2", target_bir_lowering=False, num_devices=1)
    arrays = {"in_x": np.concatenate([np.asarray(inputs["x_prompt"]).reshape(SEQ, D),
                                      np.asarray(inputs["x_sample"]).reshape(NS, D)])}
    for name in _INS:
        arrays["in_" + name] = np.ascontiguousarray(inputs[name])
    short = {"cache_k_win": "cache_k", "cache_v_win": "cache_v"}
    io = {}
    for name, a in arrays.items():
        t = nc.dram_tensor(name, a.shape, mybir.dt.from_np(a.dtype), kind="ExternalInput").ap()
        io[short.get(name[3:], name[3:])] = t
    for name, shape in _OUTS.items():
        io[name] = nc.dram_tensor("out_" + name, shape, F32, kind="ExternalOutput").ap()
    io["h2T"] = nc.dram_tensor("h2T_rows", (P, KD, NTOK), F32, kind="Internal").ap()
    io["hn"] = nc.dram_tensor("hn_rows", (NTOK, D), F32, kind="Internal").ap()
    hybrid_layer(nc, io)
    got = run_bass_kernel_spmd(nc, [arrays], core_ids=[0]).results[0]
    y = got["out_y"]
    return (y[0:SEQ].reshape(1, SEQ, D), y[SEQ:NTOK].reshape(DEC_B, DEC_T, D), got["out_new_k_p"], got["out_new_v_p"],
            got["out_new_k_s"], got["out_new_v_s"], got["out_new_vs"])
```
